# Optimizing a Trainium2 kernel written in Bass

```python
import math
import jax, jax.numpy as jnp
from jax import lax
import numpy as np

D_MODEL = 1024
BATCH = 1
SEQ = 512
DEPTH = 1

ATT_PATTERNS = ((128, 1), (512, 4), (2048, 16))
ATT_GROUPS = len(ATT_PATTERNS)
ATT_HEADS = 8
ATT_HEAD_DIM = 64
ATT_WIDTH = ATT_HEADS * ATT_HEAD_DIM
ATT_BLOCK = 128
RWKV_WIDTH = D_MODEL
RWKV_HEAD_DIM = 64
RWKV_HEADS = RWKV_WIDTH // RWKV_HEAD_DIM
DECAY_LORA = 64
AAA_LORA = 64
GATE_LORA = 160
D_FF = 2816
CONV_WIDTH = 3
N_BRANCHES = 2
ATT_IN = ATT_GROUPS * 3 * ATT_WIDTH
RWKV_IN = 3 * RWKV_WIDTH + DECAY_LORA + AAA_LORA + GATE_LORA
GATE_IN = N_BRANCHES * D_MODEL
N_IN = ATT_IN + RWKV_IN + GATE_IN
RMS_EPS = 1e-6
GN_EPS = 64e-5


def rms_norm(x, w):
    xf = x.astype(jnp.float32)
    y = xf * lax.rsqrt(jnp.mean(xf * xf, axis=-1, keepdims=True) + RMS_EPS)
    return (y * w).astype(x.dtype)

def dilated_window_attention(q, k, v, window, dilation):
    b, s, h, e = q.shape
    back = window // dilation
    sub_len = -(-s // dilation)
    n_blk = -(-sub_len // ATT_BLOCK)
    s_pad = n_blk * ATT_BLOCK * dilation

    def to_blocks(t):
        t = jnp.pad(t, ((0, 0), (0, s_pad - s), (0, 0), (0, 0)))
        return t.reshape(b, n_blk, ATT_BLOCK, dilation, h, e)

    def with_prev(t):
        prev = jnp.concatenate([jnp.zeros_like(t[:, :1]), t[:, :-1]], axis=1)
        return jnp.concatenate([prev, t], axis=2)

    qb = to_blocks(q)
    kc = with_prev(to_blocks(k))
    vc = with_prev(to_blocks(v))
    scores = jnp.einsum('bnqrhe,bnkrhe->bnrhqk', qb, kc).astype(jnp.float32) * (e ** -0.5)
    qi = jnp.arange(ATT_BLOCK)[:, None]
    kj = jnp.arange(2 * ATT_BLOCK)[None, :]
    dist = qi + ATT_BLOCK - kj
    kpos = jnp.arange(n_blk)[:, None] * ATT_BLOCK + kj - ATT_BLOCK
    valid = ((dist >= 0) & (dist <= back))[None] & (kpos >= 0)[:, None, :]
    scores = jnp.where(valid[None, :, None, None], scores, -jnp.inf)
    m = jnp.max(scores, axis=-1, keepdims=True)
    p = jnp.exp(scores - m)
    den = jnp.sum(p, axis=-1)
    num = jnp.einsum('bnrhqk,bnkrhe->bnqrhe', p, vc.astype(jnp.float32))
    den_q = jnp.transpose(den, (0, 1, 4, 2, 3))
    out = (num / den_q[..., None]).reshape(b, s_pad, h, e)[:, :s]
    lse = (jnp.transpose(m[..., 0], (0, 1, 4, 2, 3)) + jnp.log(den_q)).reshape(b, s_pad, h)[:, :s]
    return out, lse

def attention_mixer(z):
    b, s, _ = z.shape
    qkv = z.reshape(b, s, ATT_GROUPS, 3, ATT_HEADS, ATT_HEAD_DIM)
    outs, lses = [], []
    for g, (window, dilation) in enumerate(ATT_PATTERNS):
        o, l = dilated_window_attention(qkv[:, :, g, 0], qkv[:, :, g, 1], qkv[:, :, g, 2], window, dilation)
        outs.append(o)
        lses.append(l)
    wts = jax.nn.softmax(jnp.stack(lses), axis=0)
    out = jnp.sum(wts[..., None] * jnp.stack(outs), axis=0)
    return out.reshape(b, s, ATT_WIDTH).astype(z.dtype)

def rwkv7_mixer(z, mu, w0, w2, a0, a2, g2, k_k, k_a, r_k, lnx_w, lnx_b):
    f32 = jnp.float32
    b, s, _ = z.shape
    z_prev = jnp.pad(z, ((0, 0), (1, 0), (0, 0)))[:, :s]
    z = z + (z_prev - z) * mu
    c = RWKV_WIDTH
    r, k, v, w_low, a_low, g_low = jnp.split(
        z, [c, 2 * c, 3 * c, 3 * c + DECAY_LORA, 3 * c + DECAY_LORA + AAA_LORA], axis=-1)
    w_log = -jax.nn.softplus(-(w0 + jnp.tanh(w_low) @ w2).astype(f32)) - 0.5
    decay = jnp.exp(-jnp.exp(w_log))
    a = jax.nn.sigmoid((a0 + a_low @ a2).astype(f32))
    g = jax.nn.sigmoid(g_low) @ g2
    k_mod = k.astype(f32) * (1.0 + (a - 1.0) * k_a)

    def heads(t):
        return t.astype(f32).reshape(b, s, RWKV_HEADS, RWKV_HEAD_DIM)

    kk = heads(k * k_k)
    kk = kk / jnp.maximum(jnp.sqrt(jnp.sum(kk * kk, axis=-1, keepdims=True)), 1e-12)
    r_h, k_h, v_h, w_h, a_h = heads(r), heads(k_mod), heads(v), heads(decay), heads(a)

    def step(state, inp):
        r_t, w_t, k_t, v_t, aa_t, bb_t = inp
        sa = jnp.einsum('bhvk,bhk->bhv', state, aa_t)
        state = state * w_t[:, :, None, :] + sa[..., None] * bb_t[:, :, None, :] + v_t[..., None] * k_t[:, :, None, :]
        return state, jnp.einsum('bhvk,bhk->bhv', state, r_t)

    tm = lambda t: jnp.swapaxes(t, 0, 1)
    state0 = jnp.zeros((b, RWKV_HEADS, RWKV_HEAD_DIM, RWKV_HEAD_DIM), f32)
    _, y = lax.scan(step, state0, (tm(r_h), tm(w_h), tm(k_h), tm(v_h), tm(-kk), tm(kk * a_h)))
    y = tm(y)
    mean = jnp.mean(y, axis=-1, keepdims=True)
    var = jnp.mean(jnp.square(y - mean), axis=-1, keepdims=True)
    y = ((y - mean) * lax.rsqrt(var + GN_EPS)).reshape(b, s, c) * lnx_w + lnx_b
    bonus = (jnp.sum(r_h * k_h * r_k, axis=-1, keepdims=True) * v_h).reshape(b, s, c)
    return ((y + bonus) * g).astype(z.dtype)

def conv_ffn(h, w_up, conv_w, conv_b, w_down):
    s = h.shape[1]
    u = h @ w_up
    up = jnp.pad(u, ((0, 0), (CONV_WIDTH - 1, 0), (0, 0)))
    u = conv_b + sum(conv_w[j] * up[:, j:j + s] for j in range(CONV_WIDTH))
    gate, val = jnp.split(u, 2, axis=-1)
    return (jax.nn.silu(gate) * val) @ w_down

def first_inputs(seed: int = 0) -> dict:
    key = jax.random.key(seed)
    ks = iter(jax.random.split(key, 32))
    f32 = jnp.float32
    L, D, C = DEPTH, D_MODEL, RWKV_WIDTH

    def nrm(shape, scale):
        return jax.random.normal(next(ks), shape, f32) * scale

    ramp = (jnp.arange(C, dtype=f32) / (C - 1)) ** 0.85
    inputs = {}
    inputs['x'] = nrm((BATCH, SEQ, D), 1.0)
    inputs['c'] = nrm((BATCH, D), 1.0)
    inputs['w_ada'] = nrm((L, D, 6 * D), 0.3 * D ** -0.5)
    inputs['b_ada'] = nrm((L, 6 * D), 0.02)
    inputs['norm1_w'] = 1.0 + nrm((L, D), 0.05)
    inputs['w_in'] = nrm((L, D, N_IN), D ** -0.5)
    inputs['b_gate'] = nrm((L, GATE_IN), 0.1)
    inputs['mu_shift'] = jax.random.uniform(next(ks), (L, RWKV_IN), f32)
    inputs['w0'] = -6.5 + 5.0 * ramp + nrm((L, C), 0.1)
    inputs['w2'] = nrm((L, DECAY_LORA, C), 0.1 * DECAY_LORA ** -0.5)
    inputs['a0'] = nrm((L, C), 0.1)
    inputs['a2'] = nrm((L, AAA_LORA, C), AAA_LORA ** -0.5)
    inputs['g2'] = nrm((L, GATE_LORA, C), GATE_LORA ** -0.5)
    inputs['k_k'] = 0.85 + nrm((L, C), 0.05)
    inputs['k_a'] = 1.0 + nrm((L, C), 0.05)
    inputs['r_k'] = nrm((L, RWKV_HEADS, RWKV_HEAD_DIM), 0.1)
    inputs['lnx_w'] = 1.0 + nrm((L, C), 0.05)
    inputs['lnx_b'] = nrm((L, C), 0.02)
    inputs['w_att_out'] = nrm((L, ATT_WIDTH, D), ATT_WIDTH ** -0.5)
    inputs['w_rwkv_out'] = nrm((L, C, D), C ** -0.5)
    inputs['w_o'] = nrm((L, D, D), D ** -0.5)
    inputs['norm2_w'] = 1.0 + nrm((L, D), 0.05)
    inputs['w_up'] = nrm((L, D, 2 * D_FF), D ** -0.5)
    inputs['conv_w'] = nrm((L, CONV_WIDTH, 2 * D_FF), CONV_WIDTH ** -0.5)
    inputs['conv_b'] = nrm((L, 2 * D_FF), 0.02)
    inputs['w_down'] = nrm((L, D_FF, D), D_FF ** -0.5)
    inputs['norm_f_w'] = 1.0 + nrm((D,), 0.05)
    return inputs

def first_block(x, c, w_ada, b_ada, norm1_w, w_in, b_gate, mu_shift, w0, w2, a0, a2, g2, k_k, k_a, r_k,
              lnx_w, lnx_b, w_att_out, w_rwkv_out, w_o, norm2_w, w_up, conv_w, conv_b, w_down, norm_f_w):
    for l in range(DEPTH):
        ada = (c @ w_ada[l] + b_ada[l])[:, None, :]
        sh1, sc1, gt1, sh2, sc2, gt2 = jnp.split(ada, 6, axis=-1)
        h = rms_norm(x, norm1_w[l]) * (1.0 + sc1) + sh1
        proj = h @ w_in[l]
        att_in, rwkv_in, gate_in = jnp.split(proj, [ATT_IN, ATT_IN + RWKV_IN], axis=-1)
        y_att = attention_mixer(att_in) @ w_att_out[l]
        y_rwkv = rwkv7_mixer(rwkv_in, mu_shift[l], w0[l], w2[l], a0[l], a2[l], g2[l], k_k[l], k_a[l],
                             r_k[l], lnx_w[l], lnx_b[l]) @ w_rwkv_out[l]
        g_att, g_rwkv = jnp.split(jax.nn.sigmoid(gate_in + b_gate[l]), N_BRANCHES, axis=-1)
        x = x + gt1 * ((g_att * y_att + g_rwkv * y_rwkv) @ w_o[l])
        h = rms_norm(x, norm2_w[l]) * (1.0 + sc2) + sh2
        x = x + gt2 * conv_ffn(h, w_up[l], conv_w[l], conv_b[l], w_down[l])
    return rms_norm(x, norm_f_w)


DEPTH_2 = 2

EPS = 1e-6
A_HEADS = 8
A_HEAD_DIM = 64
A_WIDTH = A_HEADS * A_HEAD_DIM
POOL_WINDOWS = (2, 4, 8, 16)
B_GROUPS = len(POOL_WINDOWS)
B_GROUP_DIM = 128
B_WIDTH = B_GROUPS * B_GROUP_DIM
EVEN_IN = 3 * A_WIDTH + B_WIDTH
EVEN_MIX = A_WIDTH + B_WIDTH
CHUNK = 128
C_HEADS = 8
C_HEAD_DIM = 128
C_WIDTH = C_HEADS * C_HEAD_DIM

N_EVEN = (DEPTH_2 + 1) // 2
N_ODD = DEPTH_2 // 2


def rms_norm_2(x, g):
    x32 = x.astype(jnp.float32)
    y = x32 * lax.rsqrt(jnp.mean(x32 * x32, axis=-1, keepdims=True) + EPS)
    return y.astype(x.dtype) * g

def causal_dwconv3(x, w):
    s = x.shape[1]
    xp = jnp.pad(x, ((0, 0), (CONV_WIDTH - 1, 0), (0, 0)))
    y = xp[:, 0:s] * w[0]
    for k in range(1, CONV_WIDTH):
        y = y + xp[:, k:k + s] * w[k]
    return y

def short_gated_conv(gate_b, gate_c, val, conv_w):
    return gate_b * causal_dwconv3(gate_c * val, conv_w)

def multiscale_pool(z, w_pool, pool_scale):
    b, s, _ = z.shape
    z32 = z.astype(jnp.float32).reshape(b, s, B_GROUPS, B_GROUP_DIM)
    cs = jnp.cumsum(z32, axis=1)
    pos = jnp.arange(1, s + 1, dtype=jnp.float32)[None, :, None]
    outs = []
    for g, w in enumerate(POOL_WINDOWS):
        csg = cs[:, :, g]
        shifted = jnp.pad(csg, ((0, 0), (w, 0), (0, 0)))[:, :s]
        count = jnp.minimum(pos, jnp.float32(w))
        outs.append((csg - shifted) / count - z32[:, :, g])
    pooled = jnp.stack(outs, axis=2).astype(z.dtype)
    mixed = jnp.einsum('bsgc,gcd->bsgd', pooled, w_pool)
    return mixed.reshape(b, s, B_WIDTH) * pool_scale

def chunked_spatial_gating(u, v, sgu_norm, w_spatial, b_spatial):
    b, s, _ = u.shape
    n = s // CHUNK
    vn = rms_norm_2(v, sgu_norm).reshape(b, n, CHUNK, C_HEADS, C_HEAD_DIM)
    mask = jnp.tril(jnp.ones((CHUNK, CHUNK), dtype=w_spatial.dtype))
    ws = w_spatial * mask
    gate = jnp.einsum('hts,bnshc->bnthc', ws, vn) + b_spatial.T[None, None, :, :, None]
    return u * gate.reshape(b, s, C_WIDTH)

def gated_conv_ffn(x, w_gate, w_up, conv_w, conv_b, w_down):
    g = jnp.einsum('bsd,df->bsf', x, w_gate)
    g = causal_dwconv3(g, conv_w) + conv_b
    up = jnp.einsum('bsd,df->bsf', x, w_up)
    return jnp.einsum('bsf,fd->bsd', jax.nn.silu(g) * up, w_down)

def second_inputs(seed: int = 0) -> dict:
    key = jax.random.key(seed)
    ks = jax.random.split(key, 20)
    f32 = jnp.float32
    nrm = lambda k, shape, s: jax.random.normal(k, shape, f32) * s
    return {
        "x": nrm(ks[0], (BATCH, SEQ, D_MODEL), 1.0),
        "norm_mix": 1.0 + nrm(ks[1], (DEPTH_2, D_MODEL), 0.05),
        "norm_ffn": 1.0 + nrm(ks[2], (DEPTH_2, D_MODEL), 0.05),
        "final_norm": 1.0 + nrm(ks[3], (D_MODEL,), 0.05),
        "w_in_even": nrm(ks[4], (N_EVEN, D_MODEL, EVEN_IN), D_MODEL ** -0.5),
        "conv_a": nrm(ks[5], (N_EVEN, CONV_WIDTH, A_WIDTH), CONV_WIDTH ** -0.5),
        "w_pool": nrm(ks[6], (N_EVEN, B_GROUPS, B_GROUP_DIM, B_GROUP_DIM), B_GROUP_DIM ** -0.5),
        "pool_scale": 1.0 + nrm(ks[7], (N_EVEN, B_WIDTH), 0.1),
        "w_out_even": nrm(ks[8], (N_EVEN, EVEN_MIX, D_MODEL), EVEN_MIX ** -0.5),
        "w_in_odd": nrm(ks[9], (N_ODD, D_MODEL, 2 * C_WIDTH), D_MODEL ** -0.5),
        "sgu_norm": 1.0 + nrm(ks[10], (N_ODD, C_WIDTH), 0.05),
        "w_spatial": nrm(ks[11], (N_ODD, C_HEADS, CHUNK, CHUNK), CHUNK ** -0.5),
        "b_spatial": 1.0 + nrm(ks[12], (N_ODD, C_HEADS, CHUNK), 0.05),
        "w_out_odd": nrm(ks[13], (N_ODD, C_WIDTH, D_MODEL), C_WIDTH ** -0.5),
        "w_ffn_gate": nrm(ks[14], (DEPTH_2, D_MODEL, D_FF), D_MODEL ** -0.5),
        "w_ffn_up": nrm(ks[15], (DEPTH_2, D_MODEL, D_FF), D_MODEL ** -0.5),
        "conv_ffn": nrm(ks[16], (DEPTH_2, CONV_WIDTH, D_FF), CONV_WIDTH ** -0.5),
        "b_conv_ffn": nrm(ks[17], (DEPTH_2, D_FF), 0.02),
        "w_ffn_down": nrm(ks[18], (DEPTH_2, D_FF, D_MODEL), D_FF ** -0.5),
    }

def second_block(x, norm_mix, norm_ffn, final_norm, w_in_even, conv_a, w_pool, pool_scale,
              w_out_even, w_in_odd, sgu_norm, w_spatial, b_spatial, w_out_odd,
              w_ffn_gate, w_ffn_up, conv_ffn, b_conv_ffn, w_ffn_down):
    h = x
    for layer in range(DEPTH_2):
        xn = rms_norm_2(h, norm_mix[layer])
        if layer % 2 == 0:
            i = layer // 2
            proj = jnp.einsum('bsd,de->bse', xn, w_in_even[i])
            a_b = proj[..., 0:A_WIDTH]
            a_c = proj[..., A_WIDTH:2 * A_WIDTH]
            a_v = proj[..., 2 * A_WIDTH:3 * A_WIDTH]
            z_b = proj[..., 3 * A_WIDTH:]
            y_a = short_gated_conv(a_b, a_c, a_v, conv_a[i])
            y_b = multiscale_pool(z_b, w_pool[i], pool_scale[i])
            mix = jnp.concatenate([y_a, y_b], axis=-1)
            h = h + jnp.einsum('bse,ed->bsd', mix, w_out_even[i])
        else:
            i = layer // 2
            proj = jax.nn.gelu(jnp.einsum('bsd,de->bse', xn, w_in_odd[i]), approximate=False)
            u = proj[..., :C_WIDTH]
            v = proj[..., C_WIDTH:]
            mix = chunked_spatial_gating(u, v, sgu_norm[i], w_spatial[i], b_spatial[i])
            h = h + jnp.einsum('bse,ed->bsd', mix, w_out_odd[i])
        hn = rms_norm_2(h, norm_ffn[layer])
        h = h + gated_conv_ffn(hn, w_ffn_gate[layer], w_ffn_up[layer], conv_ffn[layer],
                               b_conv_ffn[layer], w_ffn_down[layer])
    return rms_norm_2(h, final_norm)


def setup_inputs(seed=0):
    out = dict(first_inputs(seed))
    for name, value in second_inputs(seed + 1).items():
        if name != "x":
            out[name + "_2"] = value
    return out


def reference(
    x, c, w_ada, b_ada, norm1_w, w_in, b_gate, mu_shift, w0, w2, a0, a2, g2, k_k, k_a, r_k,
    lnx_w, lnx_b, w_att_out, w_rwkv_out, w_o, norm2_w, w_up, conv_w, conv_b, w_down, norm_f_w,
    norm_mix_2, norm_ffn_2, final_norm_2, w_in_even_2, conv_a_2, w_pool_2, pool_scale_2,
    w_out_even_2, w_in_odd_2, sgu_norm_2, w_spatial_2, b_spatial_2, w_out_odd_2, w_ffn_gate_2,
    w_ffn_up_2, conv_ffn_2, b_conv_ffn_2, w_ffn_down_2,
):
    x = first_block(
        x, c, w_ada, b_ada, norm1_w, w_in, b_gate, mu_shift, w0, w2, a0, a2, g2, k_k, k_a, r_k,
        lnx_w, lnx_b, w_att_out, w_rwkv_out, w_o, norm2_w, w_up, conv_w, conv_b, w_down,
        norm_f_w,
    )
    return second_block(
        x, norm_mix_2, norm_ffn_2, final_norm_2, w_in_even_2, conv_a_2, w_pool_2, pool_scale_2,
        w_out_even_2, w_in_odd_2, sgu_norm_2, w_spatial_2, b_spatial_2, w_out_odd_2,
        w_ffn_gate_2, w_ffn_up_2, conv_ffn_2, b_conv_ffn_2, w_ffn_down_2,
    )


_drawn_inputs = setup_inputs


def setup_inputs(seed=0):
    import zlib

    import numpy as np

    out = dict(_drawn_inputs(seed))
    spreads = {}
    factors = {'norm1_w': 3.974,
     'b_gate': 8.0,
     'w2': 28.463,
     'a0': 8.0,
     'k_k': 43.408,
     'k_a': 5.204,
     'lnx_w': 50.882,
     'lnx_b': 64.0,
     'conv_b': 54.576,
     'sgu_norm_2': 4.022,
     'b_spatial_2': 2.811,
     'b_conv_ffn_2': 5.076,
     'norm2_w': 8.0}
    for name, (base, spread) in spreads.items():
        noise = np.random.default_rng([zlib.crc32(name.encode()), seed]).standard_normal(out[name].shape)
        drawn = base * np.exp(spread * noise) if base else spread * noise
        out[name] = __import__('jax').numpy.asarray(drawn.astype(out[name].dtype))
    for name, factor in factors.items():
        out[name] = (out[name] * factor).astype(out[name].dtype)
    return out
```

```python
from contextlib import ExitStack

import concourse.bass as bass
from concourse import mybir

F32 = mybir.dt.float32
BF16 = mybir.dt.bfloat16
I32 = mybir.dt.int32
ALU = mybir.AluOpType
ACT = mybir.ActivationFunctionType
AX = mybir.AxisListType

P = 128
S = 512
D = 1024
DT = D // P
ATT_GROUPS, ATT_WIDTH, HEAD = 3, 512, 64
DILATIONS = (1, 4, 16)
BLK = 128
PAIRS_ATT = ATT_WIDTH // P
LOW = 64
GATE_LOW = 160
CHUNK = 64
SUB = 16
F = 2816
FT = F // P
ATT_IN = ATT_GROUPS * 3 * ATT_WIDTH
RWKV_IN = 3 * D + 2 * LOW + GATE_LOW
GATE0 = ATT_IN + RWKV_IN
RMS_EPS = 1e-6
GN_EPS = 64e-5
MASKED = -1e30
POOL_WINDOWS = (2, 4, 8, 16)
SLOT = 3584
SLOTS = 4
FIRST_COUNT = 1024


class Count:

    def __init__(self, book, name, step):
        self.book, self.name, self.step = book, name, step
        self.sem = book.ctx.enter_context(book.nc.semaphore(name))
        self.value = 0
        book.counts.append(self)

    def mark(self, instruction):
        instruction.then_inc(self.sem, self.step)
        self.value += self.step
        return self.now()

    def now(self):
        loop = self.book.loop
        if loop is None:
            return (self, None, self.value)
        return (self, loop, self.value - loop.first[self.name])


class Loop:

    def __init__(self, first, gains, names):
        self.first, self.gains, self.names = first, gains, names
        self.new_names = {}
        self.i = None

    def name(self, key, token):
        self.new_names[key] = (token[0].name, token[2])

    def before(self, counts, key):
        name, at = self.names.get(key, (counts[0].name, 0))
        count = [c for c in counts if c.name == name][0]
        return (count, self, at - self.gains.get(name, 0))


class Book:

    def __init__(self, nc, ctx, known):
        self.nc, self.ctx, self.known = nc, ctx, known
        self.counts, self.loop, self.learned = [], None, []

    def value(self, token):
        count, loop, at = token
        if loop is None:
            return at
        first, gain = loop.first[count.name], loop.gains.get(count.name, 0)
        if loop is self.loop:
            return first + at + loop.i * gain if gain else first + at
        return first + at + (loop.n - 1) * gain

    def run(self, n, body):
        k = len(self.learned)
        self.learned.append(None)
        gains, names = self.known[k] if self.known else ({}, {})
        loop = Loop({c.name: c.value for c in self.counts}, gains, names)
        loop.n = n
        with self.nc.Fori(0, n) as i:
            self.loop, loop.i = loop, i
            for c in self.counts:
                c.seen_loop = {}
            body(i, loop)
            self.loop = None
        for c in self.counts:
            c.seen_loop = {}
            gained = c.value - loop.first[c.name]
            if gained:
                self.learned[k] = self.learned[k] or ({}, {})
                self.learned[k][0][c.name] = gained
            c.value = loop.first[c.name] + gained * n
        self.learned[k] = (self.learned[k][0], loop.new_names)


class Queue(Count):

    def __init__(self, book, name, engine, serial):
        super().__init__(book, name, 1)
        self.engine, self.serial = engine, serial
        self.seen, self.seen_loop = {}, {}
        engine.sem_inc(self.sem, FIRST_COUNT)
        self.value = FIRST_COUNT

    def wait(self, *tokens):
        for token in tokens:
            if token is None:
                continue
            count, loop, at = token
            if loop is None or loop is not self.book.loop:
                at = self.book.value(token)
                if self.seen.get(count.name, -1) >= at:
                    continue
                self.seen[count.name] = at
            else:
                if self.seen_loop.get(count.name, -10**9) >= at:
                    continue
                self.seen_loop[count.name] = at
            self.engine.wait_ge(count.sem, self.book.value(token))

    def hold(self, *tokens):
        self.wait(*tokens)
        self.engine.sem_inc(self.book.spare, 1)

    def do(self, make, *after, mark=True, serial=None):
        if self.serial if serial is None else serial:
            self.wait(self.now())
        self.wait(*after)
        instruction = make()
        return self.mark(instruction) if mark else None


class Kernel:
    def __init__(self, nc, ctx, io, known, stop=99):
        self.nc, self.ctx, self.io, self.stop = nc, ctx, io, stop
        self.book = Book(nc, ctx, known)
        self.book.spare = ctx.enter_context(nc.semaphore("spare"))
        book = self.book
        self.pe = Queue(book, "pe", nc.tensor, False)
        self.act = Queue(book, "act", nc.scalar, True)
        self.dve = Queue(book, "dve", nc.vector, True)
        self.pool = Queue(book, "pool", nc.gpsimd, True)
        self.sp = Queue(book, "sp", nc.sync, False)
        self.engines = (self.pe, self.act, self.dve, self.pool)
        self.slot_full = [Count(book, f"slot_full{s}", 16) for s in range(SLOTS)]
        self.slot_read = [None] * SLOTS
        self.load_done = Count(book, "load_done", 16)
        self.store_done = Count(book, "store_done", 16)
        self.bank = [self.psum(f"bank{b}", [P, S]) for b in range(8)]
        self.free = [None] * 8

    def sb(self, name, shape, dtype=F32, ctx=None):
        return (ctx or self.ctx).enter_context(self.nc.sbuf_tensor(name, shape, dtype))

    def psum(self, name, shape, dtype=F32):
        return self.ctx.enter_context(self.nc.psum_tensor(name, shape, dtype))

    def mm(self, out, lhsT, rhs, start, stop, *after, mark=False):
        return self.pe.do(lambda: self.nc.tensor.matmul(out, lhsT, rhs, start=start, stop=stop,
                                                        skip_group_check=True), *after, mark=mark)

    def transpose(self, out, in_, *after, mark=False):
        return self.pe.do(lambda: self.nc.tensor.transpose(out, in_, self.ident[:]), *after, mark=mark)

    def tt(self, q, out, a, b, op, *after, **kw):
        return q.do(lambda: q.engine.tensor_tensor(out, a, b, op), *after, **kw)

    def ts(self, q, out, a, s1, s2, op0, op1=None, *after, **kw):
        if op1 is None:
            return q.do(lambda: q.engine.tensor_scalar(out, a, s1, None, op0), *after, **kw)
        return q.do(lambda: q.engine.tensor_scalar(out, a, s1, s2, op0, op1), *after, **kw)

    def stt(self, out, a, s, b, op0, op1, *after, **kw):
        return self.dve.do(lambda: self.nc.vector.scalar_tensor_tensor(out, a, s, b, op0, op1), *after, **kw)

    def copy(self, q, out, a, *after, **kw):
        if q is self.act:
            return q.do(lambda: self.nc.scalar.copy(out, a), *after, **kw)
        return q.do(lambda: q.engine.tensor_copy(out, a), *after, **kw)

    def fn(self, out, a, func, bias=0.0, scale=1.0, *after, **kw):
        return self.act.do(lambda: self.nc.scalar.activation(out, a, func, bias=bias, scale=scale), *after, **kw)

    def together(self):
        for q in self.engines:
            q.wait(*[o.now() for o in self.engines if o is not q])

    def dense(self, bank, tiles, rhs, *after, start=True, stop=True):
        n = len(tiles)
        for k in range(n):
            t = self.mm(bank, tiles[k], rhs[k], start and k == 0, stop and k == n - 1,
                        *(after if k == 0 else ()), mark=k == n - 1)
        return t

    def fill(self, slot, pieces, *after):
        self.sp.wait(*after)
        for at, dims, source in pieces:
            n = 1
            for d in dims:
                n *= d
            dst = self.ring[0:source.shape[0], slot, at:at + n]
            if len(dims) == 2:
                dst = dst.rearrange("p (k n) -> p k n", k=dims[0])
            t = self.slot_full[slot].mark(self.nc.sync.dma_start(dst, source))
        return t

    def slab(self, slot, at, k, n):
        return self.ring[:, slot, at:at + k * n].rearrange("p (k n) -> p k n", k=k)

    def constants(self):
        nc, pool = self.nc, self.pool
        self.ident = self.sb("ident", [P, P])
        self.ident_bf = self.sb("ident_bf", [P, P], BF16)
        self.ones = self.sb("ones", [P, P])
        self.head_ones = self.sb("head_ones", [P, P])
        g = nc.gpsimd

        def band(t, compare, base, pattern, cm, fill):
            pool.do(lambda: g.affine_select(out=t, in_=t, pattern=pattern, compare_op=compare,
                                            fill=fill, base=base, channel_multiplier=cm))

        def fill(t, v):
            return pool.do(lambda: g.memset(t, v))

        self.band, self.fill_with = band, fill
        fill(self.ident[:], 0.0)
        band(self.ident[:], ALU.not_equal, 0, [[-1, P]], 1, 1.0)
        pool.do(lambda: g.tensor_copy(self.ident_bf[:], self.ident[:]))
        fill(self.ones[:], 1.0)
        self.same_block(self.head_ones[:], HEAD, 1.0)

    def same_block(self, t, size, value, outside=0.0, clear=True):
        if clear:
            self.fill_with(t, value)
        n = P // size
        v = t.rearrange("p (b c) -> p b c", b=n)
        self.band(v, ALU.is_ge, 0, [[-size, n], [0, size]], 1, outside)
        return self.band(v, ALU.is_ge, size - 1, [[size, n], [0, size]], -1, outside)

    def vectors(self):
        io = self.io
        plan = [("norm1_w", 8), ("b_ada", 48), ("norm2_w", 8), ("b_gate", 16), ("norm_f_w", 8), ("c", 8), None,
                ("mu_shift", 24), ("w0", 8), ("a0", 8), ("k_k", 8), ("k_a", 8), ("r_k", 8), ("lnx_w", 8), ("lnx_b", 8), ("mu_low", 3), None,
                ("conv_w0", 44), ("conv_w1", 44), None, ("conv_w2", 44), ("conv_b", 44), ("norm_mix_2", 16), ("norm_ffn_2", 16), None,
                ("conv_ffn_2", 66), ("b_conv_ffn_2", 22), ("final_norm_2", 8), ("sgu_norm_2", 8), ("conv_a_2", 12), ("pool_scale_2", 4), None,
                ("conv_ffn_2b", 66), ("b_conv_ffn_2b", 22)]
        groups = 1 + plan.count(None)
        self.vec = self.sb("vec", [P, groups * P])
        rows = self.big[:, 12:14, :].rearrange("p a n -> p (a n)")[:, 0:groups * P].rearrange("p (g n) -> p g n", n=P)
        zero = self.fill_with(rows, 0.0)
        self.sp.wait(zero)

        def src(name):
            if name.startswith("conv_w"):
                return io["conv_w"][0, int(name[6])].rearrange("(n p) -> n p", p=P)
            if name == "mu_shift":
                return io["mu_shift"][0, 0:3 * D].rearrange("(n p) -> n p", p=P)
            if name.startswith("conv_ffn_2"):
                return io["conv_ffn_2"][1 if name.endswith("b") else 0].rearrange("j (n p) -> (j n) p", p=P)
            if name.startswith("b_conv_ffn_2"):
                return io["b_conv_ffn_2"][1 if name.endswith("b") else 0].rearrange("(n p) -> n p", p=P)
            if name == "conv_a_2":
                return io[name][0].rearrange("j (n p) -> (j n) p", p=P)
            if name == "r_k":
                return io[name].rearrange("a (n h) e -> (a n) (h e)", h=2)
            a = io[name]
            if len(a.shape) == 1:
                return a.rearrange("(n p) -> n p", p=P)
            return a.rearrange("a (n p) -> (a n) p", p=P)

        self.at = {}
        g, row, last = 0, 0, None
        for entry in plan:
            if entry is None:
                g, row = g + 1, 0
                continue
            name, n = entry
            self.at[name] = g * P + row
            if name == "mu_low":
                m = io["mu_shift"]
                parts = [(row, P, m[0:1, 3 * D:3 * D + P]), (row + 1, P, m[0:1, 3 * D + P:3 * D + 2 * P]),
                         (row + 2, GATE_LOW - P, m[0:1, 3 * D + 2 * P:RWKV_IN])]
                for r, w, s in parts:
                    last = self.load_done.mark(self.nc.sync.dma_start(rows[r:r + 1, g, 0:w], s))
            else:
                last = self.load_done.mark(self.nc.sync.dma_start(rows[row:row + n, g, :], src(name)))
            row += n
            assert row <= P
        for g in range(groups):
            b = g // 4
            t = self.transpose(self.bank[b][:, (g % 4) * P:(g % 4 + 1) * P], rows[:, g, :],
                               last, self.pool.now(), self.free[b], mark=True)
        for b in range((groups + 3) // 4):
            w = min(4, groups - 4 * b) * P
            self.free[b] = self.copy(self.dve, self.vec[:, b * 4 * P:b * 4 * P + w], self.bank[b][:, 0:w], t)
        self.vec_ready = self.dve.now()

    def col(self, name, i):
        return self.vec[:, self.at[name] + i:self.at[name] + i + 1]

    def cols(self, name, n, i=0):
        return self.vec[:, self.at[name] + i:self.at[name] + i + n]

    def load_x(self):
        xrow = self.big[:, 0:8, :].rearrange("p (t a) n -> p t (a n)", t=4)
        full = self.load_x_done.mark(self.nc.sync.dma_start(
            xrow, self.io["x"][0].rearrange("(t p) d -> p t d", p=P)))
        for f in range(DT):
            b = f % 4
            for t in range(4):
                done = self.transpose(self.bank[b][:, t * P:(t + 1) * P], xrow[:, t, f * P:(f + 1) * P],
                                      full, self.pool.now(), self.free[b], mark=True)
            self.free[b] = self.copy(self.dve if f % 2 else self.act, self.x[:, f, :], self.bank[b][:], done)

    def ada(self):
        w = self.io["w_ada"][0].rearrange("(k p) n -> p k n", p=P)
        cols = 3 * P
        self.mod = self.sb("mod", [P, 6 * DT])
        b_ada = self.cols("b_ada", 6 * DT)
        self.pe.wait(self.vec_ready)
        self.together()

        def body(i, loop):
            before = lambda key: loop.before(self.book.counts, key)
            for u in range(2):
                self.fill(u, [(0, (DT, cols), w[:, :, bass.ds((2 * i + u) * cols, cols)])],
                          before(f"read{u}"))
            for u in range(2):
                slab = self.slab(u, 0, DT, cols)
                for n in range(3):
                    for k in range(DT):
                        t = self.mm(self.bank[u][:, n:n + 1], slab[:, k, n * P:(n + 1) * P],
                                    self.col("c", k), k == 0, k == DT - 1,
                                    self.slot_full[u].now(), before(f"evac{u}"), mark=n == 2 and k == DT - 1)
                loop.name(f"read{u}", t)
                at = (2 * i + u) * 3
                e = self.tt(self.dve, self.mod[:, bass.ds(at, 3)], self.bank[u][:, 0:3],
                            b_ada[:, bass.ds(at, 3)], ALU.add, t)
                loop.name(f"evac{u}", e)
                self.slot_read[u] = t
                self.free[u] = e

        self.book.run(8, body)
        self.gain1 = self.sb("gain1", [P, DT])
        self.gain2 = self.sb("gain2", [P, DT])
        for gain, part, name in ((self.gain1, 1, "norm1_w"), (self.gain2, 4, "norm2_w")):
            self.stt(gain[:], self.mod[:, part * DT:(part + 1) * DT], 1.0, self.cols(name, DT), ALU.add, ALU.mult)

    def sqrt_inverse(self, t):
        e = self.dve.do(lambda: self.nc.vector.reciprocal(t, t))
        return self.fn(t, t, ACT.Sqrt, 0.0, 1.0, e)

    def inverse_rms(self, src, eps, n, tiles):
        for k in range(tiles):
            sq = self.sq[:, k % 2, :]
            t = self.fn(sq, src[:, k, :], ACT.Square, 0.0, 1.0, self.dve.now(), self.pe.now())
            m = self.mm(self.bank[7][:], self.ones[:], sq, k == 0, k == tiles - 1, t, self.free[7], mark=True)
        e = self.ts(self.dve, self.rinv[:], self.bank[7][:], 1.0 / n, eps, ALU.mult, ALU.add, m)
        self.free[7] = e
        return self.sqrt_inverse(self.rinv[:])

    def norm(self, dst, src, gain, shift=None, tiles=DT):
        r = self.inverse_rms(src, RMS_EPS, tiles * P, tiles)
        for k in range(tiles):
            if shift is None:
                self.stt(dst[:, k, :], src[:, k, :], gain(k), self.rinv[:], ALU.mult, ALU.mult, r)
            else:
                self.stt(dst[:, k, :], src[:, k, :], gain(k), self.rinv[:], ALU.mult, ALU.mult, r)
                self.ts(self.dve, dst[:, k, :], dst[:, k, :], shift(k), None, ALU.add)

    def attention(self):
        nc, pe, act, dve, pool = self.nc, self.pe, self.act, self.dve, self.pool
        w = self.io["w_in"][0].rearrange("(k p) n -> p k n", p=P)
        with ExitStack() as ctx:
            sb = lambda name, shape, dtype=F32: self.sb(name, shape, dtype, ctx)
            masks = sb("att_masks", [P, 4, S], BF16)
            qkv = sb("att_qkv", [P, 3, 3, S])
            v_tok = sb("att_v_tok", [P, 3, 4, 3, HEAD])
            prob = self.big[:, 12:16, :]
            prob_t = self.big[:, 16:20, :]
            top = sb("att_top", [P, 12])
            neg = sb("att_neg", [P, 12])
            diag = sb("att_diag", [P, 2, P])
            join = self.big[:, 20, :]
            factor = self.big[:, 21, :]
            total = self.big[:, 4, :]
            inv = self.big[:, 5, :]
            self.fill_with(masks[:], 0.0)
            self.fill_with(masks[:, 0, 0:P], MASKED)

            def causal(t):
                return self.band(t, ALU.is_ge, 0, [[-1, P]], 1, MASKED)

            for bank, part, kind in ((0, 1, 1), (0, 2, 0), (0, 3, 1), (1, 0, 0), (1, 1, 1), (1, 2, 0), (1, 3, 1),
                                     *((b, part, 1) for b in (2, 3) for part in range(4))):
                t = masks[:, bank, part * P:(part + 1) * P]
                if kind:
                    causal(t)
                else:
                    self.band(t, ALU.is_ge, 0, [[1, P]], -1, MASKED)
                if bank == 3:
                    self.same_block(t, S // DILATIONS[2], 0.0, MASKED, clear=False)
            self.fill_with(v_tok[:, :, :, 1, :], 1.0)
            for s in (2, 3, 0):
                self.sp.wait(self.slot_read[s])
            self.together()

            def in_order(ap, g):
                return ap.rearrange("p (i r) -> p r i", r=DILATIONS[g])

            def body(i, loop):
                before = lambda key: loop.before(self.book.counts, key)
                for g, slot in enumerate((2, 3, 0)):
                    self.fill(slot, [(j * DT * P, (DT, P), w[:, :, bass.ds(i * P + (3 * g + j) * ATT_WIDTH, P)])
                                     for j in range(3)], before(f"read{slot}"))
                for b in range(8):
                    self.free[b] = None
                pe.wait((act, loop, 0), (dve, loop, 0))
                for g, slot in enumerate((2, 3, 0)):
                    for j in range(3):
                        b = (3 * g + j) % 6
                        slab = self.slab(slot, j * DT * P, DT, P)
                        t = self.dense(self.bank[b][:], [slab[:, k, :] for k in range(DT)],
                                       [self.h[:, k, :] for k in range(DT)], self.slot_full[slot].now(), self.free[b])
                        out = qkv[:, g, j, :].rearrange("p (r i) -> p r i", r=DILATIONS[g])
                        self.free[b] = self.copy(act if j == 1 else dve, out, in_order(self.bank[b][:], g), t)
                    loop.name(f"read{slot}", t)
                    self.slot_read[slot] = t
                for g in range(3):
                    b = g
                    for n in range(4):
                        t = self.transpose(self.bank[b][:, n * P:(n + 1) * P], qkv[:, g, 2, n * P:(n + 1) * P],
                                           self.free[b], dve.now(), act.now(), mark=n == 3)
                    self.free[b] = self.copy(dve, v_tok[:, g, :, 0::2, :],
                                             self.bank[b][:].rearrange("p (n h e) -> p n h e", n=4, h=2), t)
                cells = [[None, (0, 0, 0), (0, 1, 0), (0, 1, 1)], [(0, 2, 1), (0, 2, 2), (0, 3, 2), (0, 3, 3)],
                         [(1, n, n) for n in range(4)], [(2, n, n) for n in range(4)]]
                for h in range(2):
                    rows = slice(HEAD * h, HEAD * (h + 1))
                    for c in range(4):
                        self.mm(self.bank[c][:], self.ident_bf[:], masks[:, c, :], True, False, self.free[c])
                        for n, cell in enumerate(cells[c]):
                            if cell is None:
                                continue
                            g, qn, kn = cell
                            t = self.mm(self.bank[c][:, n * P:(n + 1) * P], qkv[rows, g, 0, qn * P:(qn + 1) * P],
                                        qkv[rows, g, 1, kn * P:(kn + 1) * P], False, n == 3, mark=n == 3)
                        width = 2 if c < 2 else 1
                        m = 4 // width
                        at = (0, 2, 4, 8)[c]
                        dve.do(lambda: nc.vector.tensor_reduce(
                            top[:, at:at + m], self.bank[c][:].rearrange("p (m k) -> p m k", m=m), AX.X, ALU.max), t,
                            act.now())
                        e = self.ts(dve, neg[:, at:at + m], top[:, at:at + m], -HEAD ** -0.5, None, ALU.mult)
                        for r in range(m):
                            part = slice(r * width * P, (r + 1) * width * P)
                            e2 = self.fn(prob[:, c, part], self.bank[c][:, part], ACT.Exp,
                                         neg[:, at + r:at + r + 1], HEAD ** -0.5, e, pe.now(), serial=r == 0)
                        self.free[c] = e2
                    for c in range(4):
                        for n in range(4):
                            if cells[c][n] is None:
                                continue
                            t = self.transpose(self.bank[4 + c % 2][:, n * P:(n + 1) * P], prob[:, c, n * P:(n + 1) * P],
                                               act.now(), self.free[4 + c % 2], mark=n == 3)
                        first = P if c == 0 else 0
                        self.free[4 + c % 2] = self.copy(dve, prob_t[:, c, first:], self.bank[4 + c % 2][:, first:], t)
                    ready = dve.now()
                    for g, b in ((0, 6), (1, 7), (2, 0)):
                        out = in_order(self.bank[b][:], g).rearrange("p r i -> p (r i)") if g == 0 else None
                        todo = [(c, n, cell) for c in range(4) for n, cell in enumerate(cells[c])
                                if cell is not None and cell[0] == g]
                        for m, (c, n, (_, qn, kn)) in enumerate(todo):
                            per = P // (S // DILATIONS[g]) if g else 1
                            if g:
                                dst = in_order(self.bank[b][:], g)[:, qn * per:(qn + 1) * per, :]
                                src = prob_t[:, c, n * P:(n + 1) * P].rearrange("p (r i) -> p r i", r=per)
                            else:
                                dst, src = self.bank[b][:, qn * P:(qn + 1) * P], prob_t[:, c, n * P:(n + 1) * P]
                            lhs = v_tok[:, g, kn, h:h + 2, :].rearrange("p a e -> p (a e)")
                            t = self.mm(dst, lhs, src, m == 0, m == len(todo) - 1, ready, self.free[b],
                                        mark=m == len(todo) - 1)
                    nums = t
                    for g, b in ((0, 1), (1, 2), (2, 3)):
                        for n in range(4):
                            d = self.ts(dve, diag[:, n % 2, :], self.ident[:], top[:, 4 * g + n:4 * g + n + 1], None,
                                        ALU.mult, None, pe.now() if n < 2 else spread[n % 2])
                            per = P // (S // DILATIONS[g]) if g else 1
                            if g:
                                dst = in_order(self.bank[b][:], g)[:, n * per:(n + 1) * per, :]
                                src = diag[:, n % 2, :].rearrange("p (r i) -> p r i", r=per)
                            else:
                                dst, src = self.bank[b][:, n * P:(n + 1) * P], diag[:, n % 2, :]
                            t = self.mm(dst, self.ones[:], src, n == 0, n == 3, d, self.free[b], mark=True)
                            if n == 0:
                                spread = [t, t]
                            spread[n % 2] = t
                    self.copy(act, join, self.bank[1][:], t, dve.now())
                    self.tt(dve, join, join, self.bank[2][:], ALU.max, act.now())
                    self.tt(dve, join, join, self.bank[3][:], ALU.max)
                    for g, b, nb in ((0, 1, 6), (1, 2, 7), (2, 3, 0)):
                        e = self.tt(dve, factor, self.bank[b][:], join, ALU.subtract)
                        self.free[b] = e
                        e = self.fn(factor, factor, ACT.Exp, 0.0, HEAD ** -0.5, e)
                        if g == 0:
                            e = self.tt(dve, total, self.bank[nb][:], factor, ALU.mult, e, nums)
                        else:
                            e = self.tt(dve, factor, self.bank[nb][:], factor, ALU.mult, e, nums)
                            self.tt(dve, total, total, factor, ALU.add)
                        self.free[nb] = e
                    other = slice(HEAD * (1 - h), HEAD * (2 - h))
                    dve.do(lambda: nc.vector.reciprocal(inv[rows, :], total[other, :]))
                    self.tt(dve, self.att[rows, bass.ds(i, 1), :].rearrange("p a n -> p (a n)"), total[rows, :], inv[rows, :], ALU.mult)

            self.book.run(PAIRS_ATT, body)
            self.together()

    def shift_mix(self, out, z, mu, tmp):
        self.tt(self.dve, tmp, z[:, 0:S], z[:, 1:S + 1], ALU.subtract)
        return self.stt(out, tmp, mu, z[:, 1:S + 1], ALU.mult, ALU.add)

    def rwkv(self):
        nc, pe, act, dve, pool = self.nc, self.pe, self.act, self.dve, self.pool
        w = self.io["w_in"][0].rearrange("(k p) n -> p k n", p=P)
        ctx = ExitStack()
        with ctx:
            sb = lambda name, shape, dtype=F32: self.sb(name, shape, dtype, ctx)
            mask4 = sb("rw_mask4", [P, 4, P])
            mask2 = sb("rw_mask2", [P, 2, P])
            restart = sb("rw_restart", [P, S])
            low = sb("rw_low", [P, S])
            low_g = sb("rw_low_g", [P, 2, S])
            z = sb("rw_z", [P, 3, S + 1])
            param = sb("rw_param", [P, 10])
            extra = sb("rw_extra", [P, 3])
            names = ["r", "k", "v", "t0", "t1", "lw", "rate", "gate", "kk", "bonus"]
            tile = {n: self.big[:, 12 + j, :] for j, n in enumerate(names)}
            ar = sb("rw_ar", [P, 4, 2, P])
            bt = sb("rw_b", [P, S])
            kt = sb("rw_k", [P, S])
            b_tok = sb("rw_b_tok", [P, 4, P])
            k_tok = sb("rw_k_tok", [P, 4, P])
            v_tok = sb("rw_v_tok", [P, 4, P])
            keep = sb("rw_keep", [P, 8, 4, P])
            de = sb("rw_de", [P, 4, 2, P])
            pw = sb("rw_pw", [P, 4, 2, P])
            pq = sb("rw_pq", [P, 4, 2, P])
            inv = sb("rw_inv", [P, 4, 2, P])
            x_tok = self.rinv[:, 0:P]
            u_tok = self.rinv[:, P:2 * P]
            state = self.sq[:, 0, 0:2 * P].rearrange("p (a n) -> p a n", a=2)
            y = tile["t0"]
            self.fill_with(mask4[:], 1.0)
            strict = lambda t: self.band(t, ALU.is_gt, 0, [[1, P]], -1, 0.0)
            self.same_block(mask4[:, 0, :], SUB, 1.0)
            strict(mask4[:, 0, :])
            for j in (1, 3):
                self.same_block(mask4[:, j, :], CHUNK, 1.0)
                self.band(mask4[:, j, :], ALU.is_ge, 0, [[1, P]], -1, 0.0)
            self.same_block(mask4[:, 2, :], CHUNK, 1.0)
            strict(mask4[:, 2, :])
            self.same_block(mask2[:, 0, :], SUB, 1.0)
            self.band(mask2[:, 0, :], ALU.is_gt, 0, [[-1, P]], 1, 0.0)
            self.same_block(mask2[:, 1, :], CHUNK, 1.0)
            self.band(mask2[:, 1, :], ALU.is_gt, 0, [[-1, P]], 1, 0.0)
            self.tt(pool, mask2[:, 1, :], mask2[:, 1, :], mask2[:, 0, :], ALU.subtract)
            self.fill_with(restart[:], 1.0)
            self.fill_with(restart[:].rearrange("p (c t) -> p c t", t=CHUNK)[:, :, 0:1], 0.0)
            self.fill_with(z[:, :, 0:1], 0.0)
            self.fill_with(state, 0.0)
            self.fill(1, [(0, (DT, RWKV_IN - 3 * D), w[:, :, ATT_IN + 3 * D:GATE0])], self.slot_read[1])
            slab = self.slab(1, 0, DT, RWKV_IN - 3 * D)
            self.together()
            for n, (at, width) in enumerate(((0, P), (P, P), (2 * P, GATE_LOW - P))):
                t = self.dense(self.bank[n][0:width, :], [slab[:, k, at:at + width] for k in range(DT)],
                               [self.h[:, k, :] for k in range(DT)], self.slot_full[1].now(), self.free[n])
                self.free[n] = self.copy(dve, z[0:width, n, 1:S + 1], self.bank[n][0:width, :], t, pool.now())
                self.slot_read[1] = t
                out = low[:] if n == 0 else low_g[0:width, n - 1, :]
                e = self.shift_mix(out, z[0:width, n, :], self.col("mu_low", n)[0:width, :], tile["t0"][0:width, :])
                if n == 0:
                    self.fn(low[0:LOW, :], low[0:LOW, :], ACT.Tanh, 0.0, 1.0, e)
                else:
                    self.fn(out, out, ACT.Sigmoid, 0.0, 1.0, e)
            names10 = self.vec[:, self.at["mu_shift"]:self.at["mu_shift"] + 80].rearrange("p (v n) -> p v n", n=DT)
            for s in (2,):
                self.sp.wait(self.slot_read[s])
            self.together()
            MU, W0, A0, KK, KA, RK, LNW, LNB = 0, 3, 4, 5, 6, 7, 8, 9
            par = lambda j: param[:, j:j + 1]
            w2, a2, g2 = (self.io[n][0] for n in ("w2", "a2", "g2"))
            KEEP_T, KEEP_RB, KEEP_AK, KEEP_RK = range(4)

            def body(i, loop):
                before = lambda key: loop.before(self.book.counts, key)
                SLAB = 2
                self.sp.wait(before("read"))
                lora = 3 * DT * P
                self.fill(SLAB, [(j * DT * P, (DT, P), w[:, :, bass.ds(i * P + ATT_IN + j * D, P)]) for j in range(3)]
                          + [(lora + P, (P,), g2[0:P, bass.ds(i * P, P)])])
                ring = self.ring
                c = self.slot_full[SLAB]
                c.mark(nc.sync.dma_start(ring[0:LOW, SLAB, lora:lora + P], w2[:, bass.ds(i * P, P)]))
                c.mark(nc.sync.dma_start(ring[LOW:2 * LOW, SLAB, lora:lora + P], a2[:, bass.ds(i * P, P)]))
                full = c.mark(nc.sync.dma_start(ring[0:GATE_LOW - P, SLAB, lora + 2 * P:lora + 3 * P],
                                                g2[P:GATE_LOW, bass.ds(i * P, P)]))
                for b in range(8):
                    self.free[b] = None
                pe.wait((act, loop, 0), (dve, loop, 0), (pool, loop, 0))
                dve.wait((act, loop, 0), (pe, loop, 0), (pool, loop, 0))
                act.wait((dve, loop, 0), (pe, loop, 0))
                self.copy(dve, param[:], names10[:, :, bass.ds(i, 1)].rearrange("p v a -> p (v a)"))
                self.ts(dve, extra[:, 0:2], param[:, W0:A0 + 1], -1.0, None, ALU.mult)
                self.ts(dve, extra[:, 2:3], par(KA), -1.0, 1.0, ALU.mult, ALU.add)
                params = dve.now()
                for j, name in enumerate(("r", "k", "v")):
                    slab = self.slab(SLAB, j * DT * P, DT, P)
                    t = self.dense(self.bank[j][:], [slab[:, k, :] for k in range(DT)],
                                   [self.h[:, k, :] for k in range(DT)], full)
                    self.free[j] = self.copy(act, z[:, j, 1:S + 1], self.bank[j][:], t)
                lo = lambda rows, at: ring[rows, SLAB, at:at + P]
                self.mm(self.bank[3][:], lo(slice(0, LOW), lora), low[0:LOW, :], True, True, mark=True)
                td = pe.now()
                ta = self.mm(self.bank[4][:], lo(slice(LOW, 2 * LOW), lora), low[LOW:2 * LOW, :], True, True, mark=True)
                self.mm(self.bank[5][:], lo(slice(0, P), lora + P), low_g[:, 0, :], True, False)
                tg = self.mm(self.bank[5][:], lo(slice(0, GATE_LOW - P), lora + 2 * P), low_g[0:GATE_LOW - P, 1, :],
                             False, True, mark=True)
                loop.name("read", tg)
                self.slot_read[SLAB] = tg

                def sigmoid(out, bank, neg_bias, t):
                    e = self.fn(out, bank, ACT.Exp, neg_bias, -1.0, t, params)
                    self.ts(dve, out, out, 1.0, None, ALU.add, None, e)
                    dve.do(lambda: nc.vector.reciprocal(out, out))
                    return e

                self.free[3] = sigmoid(tile["lw"], self.bank[3][:], extra[:, 0:1], td)
                self.free[4] = sigmoid(tile["rate"], self.bank[4][:], extra[:, 1:2], ta)
                self.free[5] = self.copy(act, tile["gate"], self.bank[5][:], tg)
                t0, t1, lw, rate = tile["t0"], tile["t1"], tile["lw"], tile["rate"]
                dve.wait(act.now())
                for j, name in enumerate(("r", "k", "v")):
                    self.shift_mix(tile[name], z[:, j, :], par(MU + j), t0)
                r, k, v, kk = tile["r"], tile["k"], tile["v"], tile["kk"]
                self.ts(dve, kk, k, par(KK), None, ALU.mult)
                e = self.tt(dve, t0, kk, kk, ALU.mult)
                m = self.mm(self.bank[6][:], self.head_ones[:], t0, True, True, e, mark=True)
                e = self.ts(dve, t0, self.bank[6][:], 1e-24, None, ALU.max, None, m)
                e = self.sqrt_inverse(t0)
                self.ts(dve, lw, lw, -float(2.718281828459045 ** -0.5), None, ALU.mult)
                dve.do(lambda: nc.vector.tensor_tensor_scan(t1, restart[:], lw, 0.0, ALU.mult, ALU.add))
                self.tt(dve, lw, t1, lw, ALU.subtract)
                self.ts(dve, bt[:], rate, par(KA), extra[:, 2:3], ALU.mult, ALU.add)
                self.tt(dve, k, k, bt[:], ALU.mult)
                self.tt(dve, kk, kk, t0, ALU.mult, e)
                sums = dve.now()
                e = self.stt(t0, r, par(RK), k, ALU.mult, ALU.mult)
                m = self.mm(self.bank[7][:], self.head_ones[:], t0, True, True, e, mark=True)
                e0 = self.fn(lw, lw, ACT.Exp, 0.0, 1.0, sums)
                e1 = self.fn(kt[:], t1, ACT.Exp, 0.0, -1.0)
                e2 = self.fn(t1, t1, ACT.Exp, 0.0, 1.0)
                tiles4 = lambda ap: ap.rearrange("p (j t) -> p j t", j=4)
                self.free[7] = self.tt(dve, tile["bonus"], self.bank[7][:], v, ALU.mult, m)
                self.stt(ar[:, :, 0, :], tiles4(kk), -1.0, tiles4(lw), ALU.mult, ALU.mult, e0)
                self.tt(dve, ar[:, :, 1, :], tiles4(r), tiles4(t1), ALU.mult, e2)
                self.tt(dve, kk, kk, rate, ALU.mult)
                self.tt(dve, bt[:], kk, kt[:], ALU.mult, e1)
                e = self.tt(dve, kt[:], k, kt[:], ALU.mult)
                for n, (src, dst) in enumerate(((bt, b_tok), (kt, k_tok), (None, v_tok))):
                    src = v if src is None else src[:]
                    for j in range(4):
                        t = self.transpose(self.bank[n][:, j * P:(j + 1) * P], src[:, j * P:(j + 1) * P],
                                           e, self.free[n], mark=j == 3)
                    self.free[n] = self.copy(act, dst[:].rearrange("p j t -> p (j t)"), self.bank[n][:], t)
                for hd in range(2):
                    rows = slice(HEAD * hd, HEAD * (hd + 1))
                    bank = lambda j: self.bank[j]
                    for j in range(4):
                        b = j
                        rhs = ar[rows, j, :, :].rearrange("p a t -> p (a t)")
                        self.mm(bank(b)[:, 0:2 * P], bt[rows, j * P:(j + 1) * P], rhs, True, False, self.free[b], e)
                        t = self.mm(bank(b)[:, 2 * P:], kt[rows, j * P:(j + 1) * P], rhs, False, True, mark=True)
                        kp = keep[:, 4 * hd + j, :, :]
                        self.free[b] = self.tt(dve, kp, bank(b)[:].rearrange("p (a t) -> p a t", a=4), mask4[:], ALU.mult, t)
                        b = 4 + j % 4
                        t = self.mm(bank(b)[:, 0:P], ar[rows, j, 0, :], bt[rows, j * P:(j + 1) * P], True, True,
                                    self.free[b], mark=True)
                        self.tt(dve, de[:, j, 0, :], bank(b)[:, 0:P], mask2[:, 0, :], ALU.mult, t, pe.now())
                        self.free[b] = self.tt(dve, de[:, j, 1, :], bank(b)[:, 0:P], mask2[:, 1, :], ALU.mult, serial=False)
                        self.tt(dve, inv[:, j, 0, :], self.ident[:], de[:, j, 0, :], ALU.add)
                        self.tt(dve, inv[:, j, 1, :], self.ident[:], kp[:, KEEP_T, :], ALU.add, serial=False)

                    def step(products, evac):
                        ready = (dve.now(), act.now())
                        for j in range(4):
                            b = (j + step.turn) % 8
                            for n, (l, rr) in enumerate(products(j)):
                                t = self.mm(bank(b)[:, n * P:(n + 1) * P], l, rr, n == 0, n == len(products(j)) - 1,
                                            self.free[b], *step.wait[j], mark=n == len(products(j)) - 1)
                            step.wait[j] = evac(j, bank(b), t)
                            self.free[b] = step.wait[j][0]
                            for x in step.wait[j][1:]:
                                if x is not None and x[0] is not step.wait[j][0][0]:
                                    self.mm_free2[b] = x
                        step.turn += 4
                    step.turn = 0
                    step.wait = [[dve.now()] for _ in range(4)]
                    self.mm_free2 = [None] * 8

                    Dn, DTn = lambda j: de[:, j, 0, :], lambda j: keep[:, 4 * hd + j, KEEP_T, :]
                    En = lambda j: de[:, j, 1, :]
                    pair = lambda t, j: t[:, j, :, :].rearrange("p a t -> p (a t)")

                    def copy_to(t):
                        return lambda j, bk, m: [self.copy(act, pair(t, j), bk[:, 0:2 * P], m)]

                    step(lambda j: [(DTn(j), Dn(j)), (Dn(j), DTn(j))], copy_to(pw))

                    def grow(out):
                        def evac(j, bk, m):
                            a = self.copy(act, pair(out, j), bk[:, 0:2 * P], m)
                            d = self.tt(dve, pair(inv, j), bk[:, 2 * P:4 * P], pair(inv, j), ALU.add, m, a)
                            return [d, a]
                        return evac
                    step(lambda j: [(pw[:, j, 1, :], pw[:, j, 0, :]), (pw[:, j, 0, :], pw[:, j, 1, :]),
                                    (pw[:, j, 1, :], inv[:, j, 0, :]), (inv[:, j, 0, :], pw[:, j, 1, :])], grow(pq))
                    step(lambda j: [(pq[:, j, 1, :], pq[:, j, 0, :]), (pq[:, j, 0, :], pq[:, j, 1, :]),
                                    (pq[:, j, 1, :], inv[:, j, 0, :]), (inv[:, j, 0, :], pq[:, j, 1, :])], grow(pw))
                    add_inv = lambda j, bk, m: [self.tt(dve, pair(inv, j), bk[:, 0:2 * P], pair(inv, j), ALU.add, m)]
                    step(lambda j: [(pw[:, j, 1, :], inv[:, j, 0, :]), (inv[:, j, 0, :], pw[:, j, 1, :])], add_inv)
                    step(lambda j: [(inv[:, j, 1, :], En(j)), (En(j), inv[:, j, 1, :])], copy_to(pw))

                    def sum2(j, bk, m):
                        a = self.copy(act, pq[:, j, 1, :], bk[:, 0:P], m)
                        self.tt(dve, pq[:, j, 0, :], bk[:, 0:P], pw[:, j, 1, :], ALU.add, m, a)
                        return [self.tt(dve, pq[:, j, 0, :], pq[:, j, 0, :], self.ident[:], ALU.add), a]
                    step(lambda j: [(pw[:, j, 0, :], pw[:, j, 1, :])], sum2)
                    step(lambda j: [(pw[:, j, 0, :], pq[:, j, 1, :])],
                         lambda j, bk, m: [self.tt(dve, pq[:, j, 0, :], bk[:, 0:P], pq[:, j, 0, :], ALU.add, m)])
                    step(lambda j: [(inv[:, j, 0, :], pq[:, j, 0, :])],
                         lambda j, bk, m: [self.copy(dve, keep[:, 4 * hd + j, KEEP_T, :], bk[:, 0:P], m)])
                Y, X, U, ST = self.bank[6], (self.bank[0], self.bank[1]), (self.bank[2], self.bank[3]), (self.bank[4], self.bank[5])
                pe.wait(dve.now(), act.now())
                dve.do(lambda: nc.vector.memset(state[:, 0, :], 0.0))
                s_ready = dve.now()
                for j in range(4):
                    xb, ub = X[j % 2], U[j % 2]
                    for hd in range(2):
                        cs = slice(HEAD * hd, HEAD * (hd + 1))
                        self.mm(xb[:, cs], keep[:, 4 * hd + j, KEEP_AK, :], v_tok[:, j, cs], hd == 0, False,
                                self.free[j % 2])
                    for ch in range(2):
                        c = 2 * j + ch
                        old, new = state[:, c % 2, :], state[:, (c + 1) % 2, :]
                        half = slice(CHUNK * ch, CHUNK * (ch + 1))
                        t = self.mm(xb[half, 0:P], ar[:, j, 0, half], old, False, ch == 1, s_ready, mark=True)
                        self.mm(Y[:, c * CHUNK:(c + 1) * CHUNK], old, ar[:, j, 1, half], c == 0, False)
                        sb_ = ST[c % 2]
                        self.mm(sb_[:, 0:P], self.ident[:], old, True, False, self.free[4 + c % 2])
                        self.mm(sb_[:, 0:P], k_tok[half, j, :], v_tok[half, j, :], False, False)
                        e = self.copy(dve, x_tok[half, :], xb[half, 0:P], t, pe.now())
                        self.free[j % 2] = e
                        for hd in range(2):
                            cs = slice(HEAD * hd, HEAD * (hd + 1))
                            t = self.mm(ub[:, cs], keep[half, 4 * hd + j, KEEP_T, :], x_tok[half, cs],
                                        ch == 0 and hd == 0, ch == 1 and hd == 1, e, self.free[2 + j % 2], mark=hd == 1)
                        e = self.copy(dve, u_tok[half, :], ub[half, 0:P], t)
                        self.free[2 + j % 2] = e
                        t = self.mm(sb_[:, 0:P], b_tok[half, j, :], u_tok[half, :], False, True, e, mark=True)
                        end = t1[:, (c + 1) * CHUNK - 1:(c + 1) * CHUNK]
                        if c < S // CHUNK - 1:
                            if c == 0:
                                dve.do(lambda: nc.vector.memset(new, 0.0))
                            for hd in range(2):
                                cs = slice(HEAD * hd, HEAD * (hd + 1))
                                self.ts(dve, new[cs, cs], sb_[cs, cs], end[cs, :], None, ALU.mult, None, t)
                            s_ready = dve.now()
                            self.free[4 + c % 2] = s_ready
                    for hd in range(2):
                        cs = slice(HEAD * hd, HEAD * (hd + 1))
                        out = Y[cs, j * P:(j + 1) * P]
                        self.mm(out, u_tok[:, cs], keep[:, 4 * hd + j, KEEP_RB, :], False, False)
                        t = self.mm(out, v_tok[:, j, cs], keep[:, 4 * hd + j, KEEP_RK, :], False, True, mark=True)
                e = self.copy(dve, t0, Y[:], t)
                m = self.mm(self.bank[7][:], self.head_ones[:], t0, True, True, e, self.free[7], mark=True)
                self.stt(t0, self.bank[7][:], -1.0 / HEAD, t0, ALU.mult, ALU.add, m)
                e = self.tt(dve, lw, t0, t0, ALU.mult)
                m = self.mm(self.bank[6][:], self.head_ones[:], lw, True, True, e, mark=True)
                e = self.ts(dve, lw, self.bank[6][:], 1.0 / HEAD, GN_EPS, ALU.mult, ALU.add, m)
                e = self.sqrt_inverse(lw)
                self.tt(dve, t0, t0, lw, ALU.mult, e)
                self.ts(dve, t0, t0, par(LNW), par(LNB), ALU.mult, ALU.add)
                self.tt(dve, t0, t0, tile["bonus"], ALU.add)
                self.tt(dve, self.mixed[:, bass.ds(i, 1), :].rearrange("p a n -> p (a n)"), t0, tile["gate"], ALU.mult)

            self.book.run(DT, body)
            self.together()

    def merge(self):
        act, dve, pe = self.act, self.dve, self.pe
        io = self.io
        w = io["w_in"][0].rearrange("(k p) n -> p k n", p=P)
        wa = io["w_att_out"][0].rearrange("(k p) n -> p k n", p=P)
        wr = io["w_rwkv_out"][0].rearrange("(k p) n -> p k n", p=P)
        bg = self.cols("b_gate", 2 * DT)
        both = self.big[:, 12:20, :]
        with ExitStack() as ctx:
            gate = self.sb("mg_gate", [P, 2, 2, S], F32, ctx)
            bias = self.sb("mg_bias", [P, 2, 2], F32, ctx)
            for s in (0, 1):
                self.sp.wait(self.slot_read[s])
            self.together()

            def body(i, loop):
                before = lambda key: loop.before(self.book.counts, key)
                for u in range(2):
                    n = (2 * i + u) * P
                    self.fill(u, [(0, (DT, P), w[:, :, bass.ds(n + GATE0, P)]),
                                  (DT * P, (DT, P), w[:, :, bass.ds(n + GATE0 + D, P)]),
                                  (2 * DT * P, (4, P), wa[:, :, bass.ds(n, P)]),
                                  ((2 * DT + 4) * P, (DT, P), wr[:, :, bass.ds(n, P)])], before(f"read{u}"))
                for u in range(2):
                    full = self.slot_full[u].now()
                    b = [self.bank[4 * u + j] for j in range(4)]
                    hs = [self.h[:, k, :] for k in range(DT)]
                    parts = ((0, DT, hs), (DT, DT, hs), (2 * DT, 4, [self.att[:, k, :] for k in range(4)]),
                             (2 * DT + 4, DT, [self.mixed[:, k, :] for k in range(DT)]))
                    ts = []
                    for j, (at, n, rhs) in enumerate(parts):
                        slab = self.slab(u, at * P, n, P)
                        ts.append(self.dense(b[j][:], [slab[:, k, :] for k in range(n)], rhs, full, before(f"evac{u}")))
                    loop.name(f"read{u}", ts[3])
                    self.slot_read[u] = ts[3]
                    for j in range(2):
                        e = self.copy(dve, bias[:, u, j:j + 1], bg[:, bass.ds(2 * i + u + j * DT, 1)], act.now())
                        e = self.fn(gate[:, u, j, :], b[j][:], ACT.Sigmoid, bias[:, u, j:j + 1], 1.0, ts[j], e, dve.now())
                        self.tt(dve, gate[:, u, j, :], gate[:, u, j, :], b[2 + j][:], ALU.mult, ts[2 + j], e)
                    e = self.tt(dve, both[:, bass.ds(2 * i + u, 1), :].rearrange("p a n -> p (a n)"), gate[:, u, 0, :], gate[:, u, 1, :], ALU.add)
                    loop.name(f"evac{u}", e)

            self.book.run(DT // 2, body)
            self.together()
        self.project("w_o", io["w_o"][0], both, DT, 2, lambda n: self.mod[:, bass.ds(n + 2 * DT, 1)])

    def project(self, name, weight, src, tiles, first_slot, scale=None):
        w = weight.rearrange("(k p) n -> p k n", p=P)
        with ExitStack() as ctx:
            gt = self.sb(f"{name}_gt", [P, 2], F32, ctx)
            for u in range(2):
                self.sp.wait(self.slot_read[first_slot + u])
            self.together()

            def body(i, loop):
                before = lambda key: loop.before(self.book.counts, key)
                for u in range(2):
                    self.fill(first_slot + u, [(0, (tiles, P), w[:, :, bass.ds((2 * i + u) * P, P)])], before(f"read{u}"))
                for u in range(2):
                    slab = self.slab(first_slot + u, 0, tiles, P)
                    t = self.dense(self.bank[u][:], [slab[:, k, :] for k in range(tiles)],
                                   [src[:, k, :] for k in range(tiles)],
                                   self.slot_full[first_slot + u].now(), before(f"evac{u}"))
                    loop.name(f"read{u}", t)
                    self.slot_read[first_slot + u] = t
                    x = self.x[:, bass.ds(2 * i + u, 1), :].rearrange("p a n -> p (a n)")
                    if scale is None:
                        e = self.tt(self.dve, x, self.bank[u][:], x, ALU.add, t)
                    else:
                        self.copy(self.dve, gt[:, u:u + 1], scale(2 * i + u))
                        e = self.stt(x, self.bank[u][:], gt[:, u:u + 1], x, ALU.mult, ALU.add, t)
                    loop.name(f"evac{u}", e)

            self.book.run(DT // 2, body)
            self.together()

    def conv_rows(self, out, z, taps, bias, *after):
        self.ts(self.dve, out, z[:, 2:S + 2], taps[2], bias, ALU.mult, ALU.add, *after)
        self.stt(out, z[:, 1:S + 1], taps[1], out, ALU.mult, ALU.add)
        return self.stt(out, z[:, 0:S], taps[0], out, ALU.mult, ALU.add)

    def ffn(self, name, w_gate, w_up, taps, biases, both, w_down, scale, slots):
        dve, act, pe = self.dve, self.act, self.pe
        wg = w_gate.rearrange("(k p) n -> p k n", p=P)
        wu = w_up.rearrange("(k p) n -> p k n", p=P)
        hidden = self.big
        with ExitStack() as ctx:
            sb = lambda n, shape: self.sb(f"{name}_{n}", shape, F32, ctx)
            z = sb("z", [P, 2, 2, S + 2])
            c = sb("c", [P, 2, 2, S])
            par = sb("par", [P, 2, 2, 4])
            self.fill_with(z[:, :, :, 0:2], 0.0)
            for u in range(2):
                self.sp.wait(self.slot_read[slots[0] + u])
            self.together()

            def body(i, loop):
                before = lambda key: loop.before(self.book.counts, key)
                for u in range(2):
                    n = (2 * i + u) * P
                    self.fill(slots[0] + u, [(0, (DT, P), wg[:, :, bass.ds(n, P)]), (DT * P, (DT, P), wu[:, :, bass.ds(n, P)])],
                              before(f"read{u}"))
                for u in range(2):
                    full = self.slot_full[slots[0] + u].now()
                    hs = [self.h[:, k, :] for k in range(DT)]
                    n = 2 * i + u
                    ts = []
                    for j in range(2):
                        slab = self.slab(slots[0] + u, j * DT * P, DT, P)
                        ts.append(self.dense(self.bank[2 * u + j][:], [slab[:, k, :] for k in range(DT)], hs, full,
                                             before(f"evac{u}{j}")))
                    loop.name(f"read{u}", ts[1])
                    self.slot_read[slots[0] + u] = ts[1]
                    for j in range(2 if both else 1):
                        for a in range(3):
                            self.copy(dve, par[:, u, j, a:a + 1], taps(a, j)[:, bass.ds(n, 1)])
                        self.copy(dve, par[:, u, j, 3:4], biases(j)[:, bass.ds(n, 1)])
                        e = self.copy(act, z[:, u, j, 2:S + 2], self.bank[2 * u + j][:], ts[j], before(f"conv{u}{j}"))
                        loop.name(f"evac{u}{j}", e)
                        e = self.conv_rows(c[:, u, j, :], z[:, u, j, :], [par[:, u, j, a:a + 1] for a in range(3)],
                                           par[:, u, j, 3:4], e, act.now())
                        loop.name(f"conv{u}{j}", e)
                        if j == 0:
                            s = self.fn(c[:, u, 0, :], c[:, u, 0, :], ACT.Silu, 0.0, 1.0, e)
                    out = hidden[:, bass.ds(n, 1), :].rearrange("p a n -> p (a n)")
                    if both:
                        self.tt(dve, out, c[:, u, 0, :], c[:, u, 1, :], ALU.mult, s)
                    else:
                        e = self.tt(dve, out, c[:, u, 0, :], self.bank[2 * u + 1][:], ALU.mult, s, ts[1])
                        loop.name(f"evac{u}1", e)

            self.book.run(FT // 2, body)
            self.together()
        self.project(name + "_down", w_down, hidden, FT, slots[1], scale)

    def even_layer(self):
        io, dve, act, pe, pool = self.io, self.dve, self.act, self.pe, self.pool
        w = io["w_in_even_2"][0].rearrange("(k p) n -> p k n", p=P)
        W4 = 4 * P
        with ExitStack() as ctx:
            sb = lambda n, shape, dt=F32: self.sb(f"ev_{n}", shape, dt, ctx)
            z = sb("z", [P, 2, S + 2])
            c = sb("c", [P, 2, S])
            par = sb("par", [P, 2, 3])
            zp = sb("zp", [P, 4, S])
            s1 = sb("s1", [P, S])
            s2 = sb("s2", [P, S])
            pos = sb("pos", [P, S], I32)
            posf = sb("posf", [P, S])
            cnt = sb("cnt", [P, S])
            self.fill_with(z[:, :, 0:2], 0.0)
            pool.do(lambda: self.nc.gpsimd.iota(pos[:], pattern=[[1, S]], base=1, channel_multiplier=0))
            self.copy(pool, posf[:], pos[:])
            for u in range(4):
                self.sp.wait(self.slot_read[u])
            self.together()

            def body(i, loop):
                before = lambda key: loop.before(self.book.counts, key)
                for u in range(2):
                    n = (2 * i + u) * P
                    self.fill(u, [(j * DT * P, (DT, P), w[:, :, bass.ds(n + j * W4, P)]) for j in range(3)], before(f"read{u}"))
                for u in range(2):
                    full, n = self.slot_full[u].now(), 2 * i + u
                    ts = []
                    for j in range(3):
                        slab = self.slab(u, j * DT * P, DT, P)
                        ts.append(self.dense(self.bank[3 * u + j][:], [slab[:, k, :] for k in range(DT)],
                                             [self.h[:, k, :] for k in range(DT)], full, before(f"evac{u}")))
                    loop.name(f"read{u}", ts[2])
                    self.slot_read[u] = ts[2]
                    for a in range(3):
                        self.copy(dve, par[:, u, a:a + 1], self.cols("conv_a_2", 4, 4 * a)[:, bass.ds(n, 1)])
                    e = self.copy(act, c[:, u, :], self.bank[3 * u + 1][:], ts[1], dve.now())
                    self.tt(dve, z[:, u, 2:S + 2], self.bank[3 * u + 2][:], c[:, u, :], ALU.mult, ts[2], e)
                    self.conv_rows(c[:, u, :], z[:, u, :], [par[:, u, a:a + 1] for a in range(3)], 0.0)
                    e = self.tt(dve, self.big[:, bass.ds(n, 1), :].rearrange("p a n -> p (a n)"), c[:, u, :], self.bank[3 * u][:], ALU.mult)
                    loop.name(f"evac{u}", e)

            self.book.run(2, body)
            half = W4 // 2
            self.fill(2, [(0, (DT, half), w[:, :, 3 * W4:3 * W4 + half])])
            self.fill(3, [(0, (DT, half), w[:, :, 3 * W4 + half:4 * W4]),
                          (DT * half, (4, P), io["w_pool_2"][0].rearrange("g c d -> c g d"))])
            self.together()
            slabs, wp = [self.slab(u, 0, DT, half) for u in (2, 3)], self.slab(3, DT * half, 4, P)
            for g, window in enumerate(POOL_WINDOWS):
                t = self.dense(self.bank[g][:], [slabs[g // 2][:, k, g % 2 * P:(g % 2 + 1) * P] for k in range(DT)],
                               [self.h[:, k, :] for k in range(DT)], self.slot_full[2 + g // 2].now())
                self.copy(act, zp[:, g, :], self.bank[g][:], t, dve.now())
                self.slot_read[2] = t
                src, spare, width = zp[:, g, :], [s1, s2], 1
                first = act.now()
                while width < window:
                    dst = spare[0][:]
                    self.copy(dve, dst[:, 0:width], src[:, 0:width], first)
                    self.tt(dve, dst[:, width:], src[:, width:], src[:, 0:S - width], ALU.add)
                    src, spare, width = dst, spare[::-1], 2 * width
                self.ts(dve, cnt[:], posf[:], float(window), None, ALU.min)
                dve.do(lambda: self.nc.vector.reciprocal(cnt[:], cnt[:]))
                self.tt(dve, src, src, cnt[:], ALU.mult)
                e = self.tt(dve, zp[:, g, :], src, zp[:, g, :], ALU.subtract)
                t = self.mm(self.bank[4 + g][:], wp[:, g, :], zp[:, g, :], True, True, e, self.slot_full[3].now(), mark=True)
                self.slot_read[3] = t
                self.ts(dve, self.big[:, 4 + g, :], self.bank[4 + g][:], self.col("pool_scale_2", g), None, ALU.mult, None, t)
            self.together()
        self.project("w_out_even", io["w_out_even_2"][0], self.big, DT, 0)

    def odd_layer(self):
        io, dve, act, pe, pool = self.io, self.dve, self.act, self.pe, self.pool
        w = io["w_in_odd_2"][0].rearrange("(k p) n -> p k n", p=P)
        with ExitStack() as ctx:
            sb = lambda n, shape, dt=F32: self.sb(f"od_{n}", shape, dt, ctx)
            for u in (2, 3):
                self.sp.wait(self.slot_read[u])
            self.together()
            uv = self.big

            def body(i, loop):
                before = lambda key: loop.before(self.book.counts, key)
                for u in range(2):
                    self.fill(2 + u, [(0, (DT, 2 * P), w[:, :, bass.ds((2 * i + u) * 2 * P, 2 * P)])], before(f"read{u}"))
                for u in range(2):
                    slab = self.slab(2 + u, 0, DT, 2 * P)
                    for j in range(2):
                        b = 2 * u + j
                        t = self.dense(self.bank[b][:], [slab[:, k, j * P:(j + 1) * P] for k in range(DT)],
                                       [self.h[:, k, :] for k in range(DT)], self.slot_full[2 + u].now(), before(f"evac{b}"))
                        e = self.fn(uv[:, bass.ds(4 * i + b, 1), :].rearrange("p a n -> p (a n)"), self.bank[b][:], ACT.Gelu, 0.0, 1.0, t)
                        loop.name(f"evac{b}", e)
                    loop.name(f"read{u}", t)
                    self.slot_read[2 + u] = t

            self.book.run(4, body)
            self.together()
            r = self.inverse_rms(uv[:, DT:2 * DT, :], RMS_EPS, D, DT)
            vn = sb("vn", [P, 2, S])
            v_tok = sb("v_tok", [P, 2, S])
            ws = sb("ws", [P, 2, P])
            wst = sb("wst", [P, 2, P])
            ws_all = sb("ws_all", [P, DT, P])
            bias = sb("bias", [P, DT, P])
            par = sb("par", [P, 2])
            tril = sb("tril", [P, P])
            self.fill_with(tril[:], 1.0)
            self.band(tril[:], ALU.is_ge, 0, [[-1, P]], 1, 0.0)
            self.together()
            dve.wait(r)
            self.sp.wait(dve.now())
            self.load_done.mark(self.nc.sync.dma_start(ws_all[:], io["w_spatial_2"][0].rearrange("h t s -> t h s")))
            full = self.load_done.mark(self.nc.sync.dma_start(bias[:], io["b_spatial_2"][0].partition_broadcast(P)))

            def head(i, loop):
                before = lambda key: loop.before(self.book.counts, key)
                for u in range(2):
                    n = 2 * i + u
                    e = self.tt(dve, ws[:, u, :], ws_all[:, bass.ds(n, 1), :].rearrange("p a s -> p (a s)"), tril[:],
                                ALU.mult, full, before(f"ws{u}"))
                    t = self.transpose(self.bank[u][:, 0:P], ws[:, u, :], e, before(f"w{u}"), mark=True)
                    loop.name(f"ws{u}", t)
                    e = self.copy(dve, wst[:, u, :], self.bank[u][:, 0:P], t)
                    loop.name(f"w{u}", e)
                    self.copy(dve, par[:, u:u + 1], self.cols("sgu_norm_2", DT)[:, bass.ds(n, 1)])
                    e = self.stt(vn[:, u, :], uv[:, bass.ds(n + DT, 1), :].rearrange("p a n -> p (a n)"), par[:, u:u + 1], self.rinv[:],
                                 ALU.mult, ALU.mult)
                    for q in range(4):
                        t = self.transpose(self.bank[2 + u][:, q * P:(q + 1) * P], vn[:, u, q * P:(q + 1) * P], e,
                                           before(f"v{u}"), mark=q == 3)
                    e = self.copy(act, v_tok[:, u, :], self.bank[2 + u][:], t, before(f"g{u}"))
                    loop.name(f"v{u}", e)
                    for q in range(4):
                        t = self.mm(self.bank[4 + u][:, q * P:(q + 1) * P], v_tok[:, u, q * P:(q + 1) * P], wst[:, u, :],
                                    q == 0, q == 3, e, before(f"o{u}"), mark=q == 3)
                    loop.name(f"g{u}", t)
                    b4 = bias[:, bass.ds(n, 1), :].to_broadcast([P, 4, P])
                    e = self.tt(dve, vn[:, u, :].rearrange("p (q t) -> p q t", q=4),
                                self.bank[4 + u][:].rearrange("p (q t) -> p q t", q=4), b4, ALU.add, t)
                    loop.name(f"o{u}", e)
                    ut = uv[:, bass.ds(n, 1), :].rearrange("p a n -> p (a n)")
                    self.tt(dve, ut, ut, vn[:, u, :], ALU.mult)

            self.book.run(4, head)
            self.together()
        self.project("w_out_odd", io["w_out_odd_2"][0], self.big, DT, 0)

    def store(self):
        out = self.big[:, 0:8, :].rearrange("p (t a) n -> p t (a n)", t=4)
        for t in range(4):
            for half in range(2):
                b = 2 * (t % 2) + half
                for f in range(4):
                    m = self.transpose(self.bank[b][:, f * P:(f + 1) * P], self.h[:, 4 * half + f, t * P:(t + 1) * P],
                                       self.dve.now(), self.free[b], mark=f == 3)
                self.free[b] = self.copy(self.act, out[:, t, half * S:(half + 1) * S], self.bank[b][:], m)
            self.sp.wait(self.free[b])
            done = self.store_done.mark(self.nc.sync.dma_start(
                self.io["out"][0].rearrange("(t p) d -> p t d", p=P)[:, t, :], out[:, t, :]))
        self.sp.wait(done)

    def build(self):
        self.x = self.sb("x_res", [P, DT, S])
        self.h = self.sb("h_norm", [P, DT, S])
        self.big = self.sb("big", [P, FT, S])
        self.att, self.mixed = self.big[:, 0:4, :], self.big[:, 4:12, :]
        self.ring = self.sb("ring", [P, SLOTS, SLOT])
        self.rinv = self.sb("rinv", [P, S])
        self.sq = self.sb("sq", [P, 2, S])
        self.load_x_done = Count(self.book, "load_x_done", 16)
        io, mod = self.io, None
        self.constants()
        self.vectors()
        self.load_x()
        self.ada()
        mod = self.mod
        self.together()
        self.norm(self.h, self.x, lambda k: self.gain1[:, k:k + 1], lambda k: mod[:, k:k + 1])
        self.together()
        stages = [
            self.attention,
            self.rwkv,
            self.merge,
            lambda: (self.together(), self.norm(self.h, self.x, lambda k: self.gain2[:, k:k + 1], lambda k: mod[:, 3 * DT + k:3 * DT + k + 1]),
                     self.ffn("f0", io["w_up"][0][:, 0:F], io["w_up"][0][:, F:2 * F],
                              lambda a, j: self.cols(f"conv_w{a}", FT, FT * j), lambda j: self.cols("conv_b", FT, FT * j),
                              True, io["w_down"][0], lambda n: mod[:, bass.ds(n + 5 * DT, 1)], (0, 2))),
            lambda: (self.together(), self.norm(self.x, self.x, lambda k: self.col("norm_f_w", k)),
                     self.together(), self.norm(self.h, self.x, lambda k: self.col("norm_mix_2", k)), self.even_layer()),
            lambda: (self.together(), self.norm(self.h, self.x, lambda k: self.col("norm_ffn_2", k)), self.gated_ffn(0)),
            lambda: (self.together(), self.norm(self.h, self.x, lambda k: self.col("norm_mix_2", DT + k)), self.odd_layer()),
            lambda: (self.together(), self.norm(self.h, self.x, lambda k: self.col("norm_ffn_2", DT + k)), self.gated_ffn(1)),
        ]
        for stage in stages[:self.stop]:
            stage()
        self.together()
        if self.stop < len(stages):
            return self.book.learned
        self.norm(self.h, self.x, lambda k: self.col("final_norm_2", k))
        self.together()
        self.store()
        return self.book.learned

    def gated_ffn(self, layer):
        io, tail = self.io, "b" if layer else ""
        self.ffn(f"g{layer}", io["w_ffn_gate_2"][layer], io["w_ffn_up_2"][layer],
                 lambda a, j: self.cols("conv_ffn_2" + tail, FT, FT * a), lambda j: self.cols("b_conv_ffn_2" + tail, FT),
                 False, io["w_ffn_down_2"][layer], None, (2, 0))


def build_program(make, io_of, stop=99):
    known = None
    for _ in range(2):
        nc = make()
        with ExitStack() as ctx:
            known = Kernel(nc, ctx, io_of(nc), known, stop).build()
    return nc


_OUT = ((1, S, D), "float32")


def kernel(**inputs):
    import numpy as np
    import concourse.bacc as bacc
    from concourse.bass_utils import run_bass_kernel_spmd

    arrays = {f"in_{n}": np.ascontiguousarray(a) for n, a in inputs.items()}

    def io_of(nc):
        io = {n: nc.dram_tensor(f"in_{n}", a.shape, mybir.dt.from_np(np.asarray(a).dtype), kind="ExternalInput").ap()
              for n, a in inputs.items()}
        io["out"] = nc.dram_tensor("out_0", _OUT[0], F32, kind="ExternalOutput").ap()
        return io

    nc = build_program(lambda: bacc.Bacc("TRN2", target_bir_lowering=False, num_devices=1), io_of)
    r = run_bass_kernel_spmd(nc, [arrays], core_ids=[0])
    return r.results[0]["out_0"]
```

```python
from contextlib import ExitStack

import concourse.bass as bass
from concourse import mybir

F32 = mybir.dt.float32
F32R = mybir.dt.float32r
BF16 = mybir.dt.bfloat16
I32 = mybir.dt.int32
ALU = mybir.AluOpType
ACT = mybir.ActivationFunctionType
AX = mybir.AxisListType

P = 128
S = 512
D = 1024
DT = D // P
ATT_GROUPS, ATT_WIDTH, HEAD = 3, 512, 64
DILATIONS = (1, 4, 16)
BLK = 128
PAIRS_ATT = ATT_WIDTH // P
LOW = 64
GATE_LOW = 160
CHUNK = 64
SUB = 16
F = 2816
FT = F // P
ATT_IN = ATT_GROUPS * 3 * ATT_WIDTH
RWKV_IN = 3 * D + 2 * LOW + GATE_LOW
GATE0 = ATT_IN + RWKV_IN
RMS_EPS = 1e-6
GN_EPS = 64e-5
MASKED = -1e30
POOL_WINDOWS = (2, 4, 8, 16)
UNIT_K = 11
RAW_SLOTS = 4
SPLIT_SLOTS = 2
VEC_GROUPS = 6
FIRST_COUNT = 1024


IN_R, IN_K, IN_V = range(3)
KEEP_T, KEEP_RB, KEEP_AK, KEEP_RK = range(4)
PACE_INVERT, PACE_CHAIN, PACE_REST = (3, 2), (1, 1), (1, 1)
ADA_PER_PRODUCT = 1
ADA_PER_PAIR = 8 * ADA_PER_PRODUCT


def run(steps):
    for _ in steps:
        pass


def woven(a, b, na, nb):
    lines = [(a, na), (b, nb)]
    while lines:
        for line in list(lines):
            for _ in range(line[1]):
                if next(line[0], lines) is lines:
                    lines.remove(line)
                    break
                yield


def interleave(a, b, na, nb):
    run(woven(a, b, na, nb))


def in_order(ap, g):
    return ap.rearrange("p (i r) -> p r i", r=DILATIONS[g])


def tile_at(t, i):
    return t[:, bass.ds(i, 1), :].rearrange("p a n -> p (a n)")


class Scratch:
    pass


class Count:

    def __init__(self, book, name, step, start=0):
        self.book, self.name, self.step = book, name, step
        self.sem = book.ctx.enter_context(book.nc.semaphore(name))
        self.value = start
        if start:
            book.nc.sync.sem_inc(self.sem, start)
        book.counts.append(self)

    def mark(self, instruction):
        instruction.then_inc(self.sem, self.step)
        self.value += self.step
        return self.now()

    def now(self):
        loop = self.book.loop
        if loop is None:
            return (self, None, self.value)
        return (self, loop, self.value - loop.first[self.name])


class Loop:

    def __init__(self, first, gains, names):
        self.first, self.gains, self.names = first, gains, names
        self.new_names = {}
        self.i = None

    def name(self, key, token):
        self.new_names[key] = (token[0].name, token[2])

    def before(self, counts, key):
        name, at = self.names.get(key, (counts[0].name, 0))
        count = [c for c in counts if c.name == name][0]
        return (count, self, at - self.gains.get(name, 0))


class Peeled:

    def __init__(self, loop):
        self.loop = loop

    def name(self, key, token):
        pass

    def before(self, counts, key):
        name, at = self.loop.new_names.get(key, (counts[0].name, 0))
        return ([c for c in counts if c.name == name][0], self.loop, at)


class Book:

    def __init__(self, nc, ctx, known):
        self.nc, self.ctx, self.known = nc, ctx, known
        self.counts, self.loop, self.learned = [], None, []

    def value(self, token):
        count, loop, at = token
        if loop is None:
            return at
        first, gain = loop.first[count.name], loop.gains.get(count.name, 0)
        if loop is self.loop:
            return first + at + loop.i * gain if gain else first + at
        return first + at + (loop.n - 1) * gain

    def run(self, n, body):
        k = len(self.learned)
        self.learned.append(None)
        gains, names = self.known[k] if self.known else ({}, {})
        loop = Loop({c.name: c.value for c in self.counts}, gains, names)
        loop.n = n
        with self.nc.Fori(0, n) as i:
            self.loop, loop.i = loop, i
            for c in self.counts:
                c.seen_loop = {}
            body(i, loop)
            self.loop = None
        for c in self.counts:
            c.seen_loop = {}
            gained = c.value - loop.first[c.name]
            if gained:
                self.learned[k] = self.learned[k] or ({}, {})
                self.learned[k][0][c.name] = gained
            c.value = loop.first[c.name] + gained * n
        self.learned[k] = (self.learned[k][0], loop.new_names)
        return loop


class Queue(Count):

    def __init__(self, book, name, engine, serial):
        super().__init__(book, name, 1)
        self.engine, self.serial = engine, serial
        self.seen, self.seen_loop = {}, {}
        engine.sem_inc(self.sem, FIRST_COUNT)
        self.value = FIRST_COUNT

    def wait(self, *tokens):
        for token in tokens:
            if token is None:
                continue
            count, loop, at = token
            if loop is None or loop is not self.book.loop:
                at = self.book.value(token)
                if self.seen.get(count.name, -1) >= at:
                    continue
                self.seen[count.name] = at
            else:
                if self.seen_loop.get(count.name, -10**9) >= at:
                    continue
                self.seen_loop[count.name] = at
            self.engine.wait_ge(count.sem, self.book.value(token))

    def do(self, make, *after, mark=True, serial=None):
        if self.serial if serial is None else serial:
            self.wait(self.now())
        self.wait(*after)
        instruction = make()
        return self.mark(instruction) if mark else None


class Kernel:
    def __init__(self, nc, ctx, io, known, stop=99):
        self.nc, self.ctx, self.io, self.stop = nc, ctx, io, stop
        self.book = Book(nc, ctx, known)
        book = self.book
        self.pe = Queue(book, "pe", nc.tensor, False)
        self.act = Queue(book, "act", nc.scalar, True)
        self.dve = Queue(book, "dve", nc.vector, True)
        self.pool = Queue(book, "pool", nc.gpsimd, True)
        self.sp = Queue(book, "sp", nc.sync, False)
        self.engines = (self.pe, self.act, self.dve, self.pool)
        self.raw_full = [Count(book, f"raw_full{s}", 16) for s in range(RAW_SLOTS)]
        self.raw_free = [Count(book, f"raw_free{s}", 1, 1) for s in range(RAW_SLOTS)]
        self.split_free = [Count(book, f"split_free{s}", 1, 1) for s in range(SPLIT_SLOTS)]
        self.raw_turn = self.split_turn = 0
        self.carried = None
        self.load_done = Count(book, "load_done", 16)
        self.store_done = Count(book, "store_done", 16)
        self.bank = [self.psum(f"bank{b}", [P, S]) for b in range(8)]
        self.free = [None] * 8

    def sb(self, name, shape, dtype=F32, ctx=None):
        return (ctx or self.ctx).enter_context(self.nc.sbuf_tensor(name, shape, dtype))

    def psum(self, name, shape, dtype=F32):
        return self.ctx.enter_context(self.nc.psum_tensor(name, shape, dtype))

    def mm(self, out, lhsT, rhs, start, stop, *after, mark=False):
        return self.pe.do(lambda: self.nc.tensor.matmul(out, lhsT, rhs, start=start, stop=stop,
                                                        skip_group_check=True), *after, mark=mark)

    def transpose(self, out, in_, *after, mark=False):
        return self.pe.do(lambda: self.nc.tensor.transpose(out, in_, self.ident[:]), *after, mark=mark)

    def tt(self, q, out, a, b, op, *after, **kw):
        return q.do(lambda: q.engine.tensor_tensor(out, a, b, op), *after, **kw)

    def ts(self, q, out, a, s1, s2, op0, op1=None, *after, **kw):
        if op1 is None:
            return q.do(lambda: q.engine.tensor_scalar(out, a, s1, None, op0), *after, **kw)
        return q.do(lambda: q.engine.tensor_scalar(out, a, s1, s2, op0, op1), *after, **kw)

    def stt(self, out, a, s, b, op0, op1, *after, **kw):
        return self.dve.do(lambda: self.nc.vector.scalar_tensor_tensor(out, a, s, b, op0, op1), *after, **kw)

    def copy(self, q, out, a, *after, **kw):
        if q is self.act:
            return q.do(lambda: self.nc.scalar.copy(out, a), *after, **kw)
        return q.do(lambda: q.engine.tensor_copy(out, a), *after, **kw)

    def fn(self, out, a, func, bias=0.0, scale=1.0, *after, **kw):
        return self.act.do(lambda: self.nc.scalar.activation(out, a, func, bias=bias, scale=scale), *after, **kw)

    def together(self):
        for q in self.engines:
            q.wait(*[o.now() for o in self.engines if o is not q])

    def load(self, *pieces):
        s = self.raw_turn
        self.raw_turn = (s + 1) % RAW_SLOTS
        self.sp.wait(self.raw_free[s].now())
        self.nc.sync.sem_inc(self.sp.sem, 1)
        self.sp.value += 1
        for p0, at, k, source in pieces:
            rows = slice(p0, p0 + source.shape[0])
            if k is None:
                dst = self.raw[rows, s, at:at + source.shape[1]]
            else:
                dst = self.raw[rows, s, at:at + k * P].rearrange("p (k n) -> p k n", k=k)
            full = self.raw_full[s].mark(self.nc.sync.dma_start(dst, source))
        return s, full

    def unit(self, source, k):
        s, full = self.load((0, 0, k, source))
        b = self.split_turn
        self.split_turn = (b + 1) % SPLIT_SLOTS
        raw = self.raw[:, s, 0:k * P]
        high, low = self.w_high[:, b, 0:k * P], self.w_low[:, b, 0:k * P]
        rounded = self.act.do(lambda: self.nc.scalar.copy(high, raw), full, self.split_free[b].now(), serial=False)
        self.pool.wait(rounded)
        ready = self.raw_free[s].mark(self.nc.gpsimd.tensor_tensor(low, raw, high.bitcast(F32), ALU.subtract))
        return b, k, ready, s

    def each(self, n, sources, step, then=None):
        unit = self.carried or self.unit(*sources(0)[0])
        b, k, _, s = unit
        assert len(sources(0)) % SPLIT_SLOTS == 0

        def iteration(i, loop, unit, following):
            coming = [*sources(i)[1:], following]
            units = [unit]

            def take():
                source = coming.pop(0)
                if not coming and following is not None:
                    self.raw_turn, self.split_turn = s, b
                units.append(source and self.unit(*source))
                return units[-2]

            step(i, lambda key: loop.before(self.book.counts, key), loop.name, take)
            assert not coming
            self.carried = units[-1]

        loop = self.book.run(n - 1, lambda i, loop: iteration(i, loop, (b, k, (self.raw_free[s], loop, 0), s),
                                                              sources(i + 1)[0]))
        iteration(n - 1, Peeled(loop), (b, k, self.raw_free[s].now(), s), then)

    def product(self, bank, unit, x_high, x_low, start, stop, *after):
        b, n, ready, _ = unit
        for k in range(n):
            high, low = self.w_high[:, b, k * P:(k + 1) * P], self.w_low[:, b, k * P:(k + 1) * P]
            self.mm(bank, high, x_high(k), start and k == 0, False, ready, *after)
            self.mm(bank, high, x_low(k), False, False)
            last = k == n - 1
            ins = self.nc.tensor.matmul(bank, low, x_high(k), start=False, stop=stop and last, skip_group_check=True)
        return self.split_free[b].mark(ins)

    def product_steps(self, bank, unit, x_high, x_low, out, *after):
        b, n, ready, _ = unit
        for k in range(n):
            high, low = self.w_high[:, b, k * P:(k + 1) * P], self.w_low[:, b, k * P:(k + 1) * P]
            self.mm(bank, high, x_high(k), k == 0, False, ready, *after)
            self.mm(bank, high, x_low(k), False, False)
            ins = self.nc.tensor.matmul(bank, low, x_high(k), start=False, stop=k == n - 1, skip_group_check=True)
            if k % 2 and k < n - 1:
                yield
        out.append(self.split_free[b].mark(ins))

    def split(self, high, low, src, *after):
        self.copy(self.dve, high, src, *after)
        return self.tt(self.dve, low, src, high.bitcast(F32), ALU.subtract)

    def h_parts(self):
        return (lambda k: self.h_high[:, k, :]), (lambda k: self.h_low[:, k, :])

    def constants(self):
        nc, pool = self.nc, self.pool
        g = nc.gpsimd

        def band(t, compare, base, pattern, cm, fill):
            pool.do(lambda: g.affine_select(out=t, in_=t, pattern=pattern, compare_op=compare,
                                            fill=fill, base=base, channel_multiplier=cm))

        def fill(t, v):
            return pool.do(lambda: g.memset(t, v))

        self.band, self.fill_with = band, fill
        fill(self.ident[:], 0.0)
        band(self.ident[:], ALU.not_equal, 0, [[-1, P]], 1, 1.0)
        pool.do(lambda: g.tensor_copy(self.ident_bf[:], self.ident[:]))
        fill(self.ones[:], 1.0)
        self.same_block(self.head_ones[:], HEAD, 1.0)

    def same_block(self, t, size, value, outside=0.0, clear=True):
        if clear:
            self.fill_with(t, value)
        n = P // size
        v = t.rearrange("p (b c) -> p b c", b=n)
        self.band(v, ALU.is_ge, 0, [[-size, n], [0, size]], 1, outside)
        return self.band(v, ALU.is_ge, size - 1, [[size, n], [0, size]], -1, outside)

    def vectors(self, scope):
        io = self.io
        plan = [("norm1_w", 8), ("b_ada", 48), ("norm2_w", 8), ("b_gate", 16), ("norm_f_w", 8), ("c", 8), None,
                ("mu_shift", 24), ("w0", 8), ("a0", 8), ("k_k", 8), ("k_a", 8), ("r_k", 8), ("lnx_w", 8), ("lnx_b", 8), ("mu_low", 3), None,
                ("conv_w0", 44), ("conv_w1", 44), None, ("conv_w2", 44), ("conv_b", 44), ("norm_mix_2", 16), ("norm_ffn_2", 16), None,
                ("conv_ffn_2", 66), ("b_conv_ffn_2", 22), ("final_norm_2", 8), ("sgu_norm_2", 8), ("conv_a_2", 12), ("pool_scale_2", 4), None,
                ("conv_ffn_2b", 66), ("b_conv_ffn_2b", 22)]
        groups = 1 + plan.count(None)
        assert groups == VEC_GROUPS
        rows = self.sb("vec_rows", [P, groups, P], F32, scope)
        self.sp.wait(self.fill_with(rows[:], 0.0))

        def src(name):
            if name.startswith("conv_w"):
                return io["conv_w"][0, int(name[6])].rearrange("(n p) -> n p", p=P)
            if name == "mu_shift":
                return io["mu_shift"][0, 0:3 * D].rearrange("(n p) -> n p", p=P)
            if name.startswith("conv_ffn_2"):
                return io["conv_ffn_2"][1 if name.endswith("b") else 0].rearrange("j (n p) -> (j n) p", p=P)
            if name.startswith("b_conv_ffn_2"):
                return io["b_conv_ffn_2"][1 if name.endswith("b") else 0].rearrange("(n p) -> n p", p=P)
            if name == "conv_a_2":
                return io[name][0].rearrange("j (n p) -> (j n) p", p=P)
            if name == "r_k":
                return io[name].rearrange("a (n h) e -> (a n) (h e)", h=2)
            a = io[name]
            if len(a.shape) == 1:
                return a.rearrange("(n p) -> n p", p=P)
            return a.rearrange("a (n p) -> (a n) p", p=P)

        self.at = {}
        g, row, last = 0, 0, None
        for entry in plan:
            if entry is None:
                g, row = g + 1, 0
                continue
            name, n = entry
            self.at[name] = g * P + row
            if name == "mu_low":
                m = io["mu_shift"]
                parts = [(row, P, m[0:1, 3 * D:3 * D + P]), (row + 1, P, m[0:1, 3 * D + P:3 * D + 2 * P]),
                         (row + 2, P, m[0:1, RWKV_IN - P:RWKV_IN])]
                for r, w, s in parts:
                    last = self.load_done.mark(self.nc.sync.dma_start(rows[r:r + 1, g, 0:w], s))
            else:
                last = self.load_done.mark(self.nc.sync.dma_start(rows[row:row + n, g, :], src(name)))
            row += n
            assert row <= P
        for g in range(groups):
            b = g // 4
            t = self.transpose(self.bank[b][:, (g % 4) * P:(g % 4 + 1) * P], rows[:, g, :],
                               last, self.pool.now(), self.free[b], mark=True)
        for b in range((groups + 3) // 4):
            w = min(4, groups - 4 * b) * P
            self.free[b] = self.copy(self.dve, self.vec[:, b * 4 * P:b * 4 * P + w], self.bank[b][:, 0:w], t)
        self.vec_ready = self.dve.now()

    def col(self, name, i):
        return self.vec[:, self.at[name] + i:self.at[name] + i + 1]

    def cols(self, name, n, i=0):
        return self.vec[:, self.at[name] + i:self.at[name] + i + n]

    def load_x(self, scope):
        xrow = self.sb("x_rows", [P, 4, D], F32, scope)
        return xrow, self.load_x_done.mark(self.nc.sync.dma_start(
            xrow[:], self.io["x"][0].rearrange("(t p) d -> p t d", p=P)))

    def turn_x(self, xrow, full):
        for f in range(DT):
            b = 2 + f % 4
            for t in range(4):
                done = self.transpose(self.bank[b][:, t * P:(t + 1) * P], xrow[:, t, f * P:(f + 1) * P],
                                      full, self.pool.now(), self.free[b], mark=t == 3)
            self.free[b] = self.copy(self.dve if f % 2 else self.act, self.x[:, f, :], self.bank[b][:], done)

    def ada_column(self, source, bank, *after):
        s, full = self.load((0, 0, DT, source))
        for k in range(DT):
            self.pe.wait(full, *after)
            ins = self.nc.tensor.matmul(bank, self.raw[:, s, k * P:(k + 1) * P], self.col("c", k),
                                        start=k == 0, stop=k == DT - 1, skip_group_check=True)
        return self.raw_free[s].mark(ins)

    def ada(self):
        w = self.io["w_ada"][0].rearrange("(k p) n -> p k n", p=P)
        b_ada = self.cols("b_ada", 6 * DT)
        self.pe.wait(self.vec_ready)
        self.together()

        def body(i, loop):
            self.pe.wait((self.dve, loop, 0))
            for u in range(4):
                t = self.ada_column(w[:, :, bass.ds((4 * i + u) * P, P)], self.bank[0][:, u:u + 1])
            self.tt(self.dve, self.mod[:, bass.ds(4 * i, 4)], self.bank[0][:, 0:4], b_ada[:, bass.ds(4 * i, 4)], ALU.add, t)

        self.book.run(2 * DT // 4, body)
        self.stt(self.gain1[:], self.mod[:, DT:2 * DT], 1.0, self.cols("norm1_w", DT), ALU.add, ALU.mult)

    def sqrt_inverse(self, t):
        self.fn(t, t, ACT.Ln, 0.0, 1.0, self.dve.now())
        return self.fn(t, t, ACT.Exp, 0.0, -0.5)

    def inverse_rms(self, src, eps, tiles=DT):
        m = [None, None]
        for k in range(tiles):
            t = self.fn(self.sq[:, k % 2, :], src[:, k, :], ACT.Square, 0.0, 1.0, self.dve.now(), m[k % 2])
            m[k % 2] = self.mm(self.bank[7][:], self.ones[:], self.sq[:, k % 2, :], k == 0, k == tiles - 1, t,
                               self.free[7], mark=True)
        e = self.ts(self.dve, self.rinv[:], self.bank[7][:], 1.0 / (tiles * P), eps, ALU.mult, ALU.add, m[1])
        self.free[7] = e
        return self.sqrt_inverse(self.rinv[:])

    def norm(self, src, gain, shift=None, keep=False):
        r = self.inverse_rms(src, RMS_EPS)
        for k in range(DT):
            if keep:
                self.stt(src[:, k, :], src[:, k, :], gain(k), self.rinv[:], ALU.mult, ALU.mult, r)
                continue
            t = self.sq[:, k % 2, :]
            e = self.stt(t, src[:, k, :], gain(k), self.rinv[:], ALU.mult, ALU.mult, r)
            if shift is not None:
                e = self.ts(self.dve, t, t, shift(k), None, ALU.add)
            e = self.copy(self.act, self.h_high[:, k, :], t, e)
            self.tt(self.dve, self.h_low[:, k, :], t, self.h_high[:, k, :].bitcast(F32), ALU.subtract, e)

    def attention(self):
        with ExitStack() as ctx:
            sb = lambda name, shape, dtype=F32: self.sb(name, shape, dtype, ctx)
            self.masks = masks = sb("att_masks", [P, 4, S], BF16)
            self.coming = sb("att_coming", [P, 3, 3, S])
            self.qk = sb("att_qk", [P, 3, 2, S])
            self.v_tok = sb("att_v_tok", [P, 3, 4, 3, HEAD])
            self.prob = sb("att_prob", [P, 4, S])
            self.prob_t = sb("att_prob_t", [P, 4, S])
            self.top = sb("att_top", [P, 12])
            self.neg = sb("att_neg", [P, 12])
            self.diag = sb("att_diag", [P, 2, P])
            self.join = sb("att_join", [P, S])
            self.factor = sb("att_factor", [P, S])
            self.total = sb("att_total", [P, S])
            self.inv_den = sb("att_inv", [P, S])
            self.fill_with(masks[:], 0.0)
            self.fill_with(masks[:, 0, 0:P], MASKED)
            OWN, PREVIOUS = True, False
            for bank, part, kind in ((0, 1, OWN), (0, 2, PREVIOUS), (0, 3, OWN),
                                     (1, 0, PREVIOUS), (1, 1, OWN), (1, 2, PREVIOUS), (1, 3, OWN),
                                     *((b, part, OWN) for b in (2, 3) for part in range(4))):
                t = masks[:, bank, part * P:(part + 1) * P]
                if kind == OWN:
                    self.band(t, ALU.is_ge, 0, [[-1, P]], 1, MASKED)
                else:
                    self.band(t, ALU.is_ge, 0, [[1, P]], -1, MASKED)
                if bank == 3:
                    self.same_block(t, S // DILATIONS[2], 0.0, MASKED, clear=False)
            self.fill_with(self.v_tok[:, :, :, 1, :], 1.0)
            self.together()
            run(self.att_project(0))
            self.att_arrive()

            def body(i, loop):
                self.drain(loop)
                interleave(self.att_mix(i), self.att_project(i + 1, i), 5, 4)
                self.att_arrive()

            self.book.run(PAIRS_ATT - 1, body)
            run(self.att_mix(PAIRS_ATT - 1))
            self.together()
            self.ada_rest(PAIRS_ATT - 1)
            self.stt(self.gain2[:], self.mod[:, 4 * DT:5 * DT], 1.0, self.cols("norm2_w", DT), ALU.add, ALU.mult)
            self.together()

    def drain(self, loop):
        self.pe.wait((self.act, loop, 0), (self.dve, loop, 0))
        self.act.wait((self.dve, loop, 0))
        self.dve.wait((self.act, loop, 0))
        self.free = [None] * 8

    def ada_rest(self, first):
        w = self.io["w_ada"][0].rearrange("(k p) n -> p k n", p=P)
        for n in range(2 * DT + ADA_PER_PAIR * first, 6 * DT):
            b = n % 2
            t = self.ada_column(w[:, :, n * P:(n + 1) * P], self.bank[b][:, 0:1], self.free[b])
            self.free[b] = self.tt(self.dve, self.mod[:, n:n + 1], self.bank[b][:, 0:1], self.cols("b_ada", 1, n), ALU.add, t)

    def att_project(self, pair, step=None):
        io = self.io
        w = io["w_in"][0].rearrange("(k p) n -> p k n", p=P)
        wa = io["w_ada"][0].rearrange("(k p) n -> p k n", p=P)
        source = lambda n: w[:, :, bass.ds(pair * P + n * ATT_WIDTH, P)]
        units, turn = [self.unit(source(0), DT)], 0
        for n in range(9):
            g, j = n // 3, n % 3
            if n < 8:
                units.append(self.unit(source(n + 1), DT))
            b, done = 6 + turn % 2, []
            turn += 1
            yield from self.product_steps(self.bank[b][:], units[n], *self.h_parts(), done, self.free[b])
            out = self.coming[:, g, j, :].rearrange("p (r i) -> p r i", r=DILATIONS[g])
            self.free[b] = self.copy(self.act if n % 3 == 2 else self.dve, out, in_order(self.bank[b][:], g), done[0])
            yield
            for a in range(ADA_PER_PRODUCT if step is not None and n < 8 else 0):
                b = 6 + turn % 2
                turn += 1
                at = step * ADA_PER_PAIR + (2 * DT + n * ADA_PER_PRODUCT + a)
                t = self.ada_column(wa[:, :, bass.ds(at * P, P)], self.bank[b][:, 0:1], self.free[b])
                self.free[b] = self.tt(self.dve, self.mod[:, bass.ds(at, 1)], self.bank[b][:, 0:1],
                                       self.cols("b_ada", 6 * DT)[:, bass.ds(at, 1)], ALU.add, t)
                yield

    def att_arrive(self):
        act, dve = self.act, self.dve
        done = (act.now(), dve.now())
        for g in range(3):
            for n in range(4):
                t = self.transpose(self.bank[g][:, n * P:(n + 1) * P], self.coming[:, g, 2, n * P:(n + 1) * P],
                                   *done, mark=n == 3)
            q = act if g == 1 else dve
            self.copy(q, self.qk[:, g, :, :], self.coming[:, g, 0:2, :], *done)
            self.free[g] = self.copy(q, self.v_tok[:, g, :, 0::2, :],
                                     self.bank[g][:].rearrange("p (n h e) -> p n h e", n=4, h=2), t)
        self.pe.wait(act.now(), dve.now())

    def att_mix(self, i):
        nc, act, dve = self.nc, self.act, self.dve
        qk, prob, prob_t, v_tok, top, neg = self.qk, self.prob, self.prob_t, self.v_tok, self.top, self.neg
        join, factor, total = self.join[:], self.factor[:], self.total[:]
        cells = [[None, (0, 0, 0), (0, 1, 0), (0, 1, 1)], [(0, 2, 1), (0, 2, 2), (0, 3, 2), (0, 3, 3)],
                 [(1, n, n) for n in range(4)], [(2, n, n) for n in range(4)]]
        per = [0, 1, P * DILATIONS[2] // S]

        def block(bank, g, n):
            if g == 0:
                return bank[:, n * P:(n + 1) * P]
            return in_order(bank[:], g)[:, n * per[g]:(n + 1) * per[g], :]

        def like(ap, g):
            return ap if g == 0 else ap.rearrange("p (r i) -> p r i", r=per[g])

        for h in range(2):
            rows = slice(HEAD * h, HEAD * (h + 1))
            exps = []
            for c in range(4):
                self.mm(self.bank[c][:], self.ident_bf[:], self.masks[:, c, :], True, False, self.free[c])
                for n, cell in enumerate(cells[c]):
                    if cell is None:
                        continue
                    g, qn, kn = cell
                    t = self.mm(self.bank[c][:, n * P:(n + 1) * P], qk[rows, g, 0, qn * P:(qn + 1) * P],
                                qk[rows, g, 1, kn * P:(kn + 1) * P], False, n == 3, mark=n == 3)
                width = 2 if c < 2 else 1
                m, at = 4 // width, (0, 2, 4, 8)[c]
                dve.do(lambda: nc.vector.tensor_reduce(
                    top[:, at:at + m], self.bank[c][:].rearrange("p (m k) -> p m k", m=m), AX.X, ALU.max), t)
                e = self.ts(dve, neg[:, at:at + m], top[:, at:at + m], -HEAD ** -0.5, None, ALU.mult)
                yield
                for r in range(m):
                    part = slice(r * width * P, (r + 1) * width * P)
                    e2 = self.fn(prob[:, c, part], self.bank[c][:, part], ACT.Exp,
                                 neg[:, at + r:at + r + 1], HEAD ** -0.5, e, serial=r == 0)
                self.free[c] = e2
                exps.append(e2)
                yield
            for c in range(4):
                b = 4 + c % 2
                for n in range(4):
                    if cells[c][n] is None:
                        continue
                    t = self.transpose(self.bank[b][:, n * P:(n + 1) * P], prob[:, c, n * P:(n + 1) * P],
                                       exps[c], self.free[b], mark=n == 3)
                first = P if c == 0 else 0
                ready = self.free[b] = self.copy(dve, prob_t[:, c, first:], self.bank[b][:, first:], t)
                yield
            spread = [None, None]
            for g in range(3):
                b = 3 + g
                for n in range(4):
                    d = self.ts(dve, self.diag[:, n % 2, :], self.ident[:], top[:, 4 * g + n:4 * g + n + 1], None,
                                ALU.mult, None, spread[n % 2])
                    spread[n % 2] = self.mm(block(self.bank[b], g, n), self.ones[:], like(self.diag[:, n % 2, :], g),
                                            n == 0, n == 3, d, self.free[b], mark=True)
                    if n % 2:
                        yield
            maxima = spread[1]
            nums = []
            for g in range(3):
                todo = [(c, n, cell) for c in range(4) for n, cell in enumerate(cells[c])
                        if cell is not None and cell[0] == g]
                for m, (c, n, (_, qn, kn)) in enumerate(todo):
                    lhs = v_tok[:, g, kn, h:h + 2, :].rearrange("p a e -> p (a e)")
                    t = self.mm(block(self.bank[g], g, qn), lhs, like(prob_t[:, c, n * P:(n + 1) * P], g),
                                m == 0, m == len(todo) - 1, ready, self.free[g], mark=m == len(todo) - 1)
                nums.append(t)
                if g == 0:
                    e = self.copy(act, join, self.bank[3][:], maxima, dve.now())
                    self.tt(dve, join, join, self.bank[4][:], ALU.max, e)
                    self.tt(dve, join, join, self.bank[5][:], ALU.max)
                yield
            for g in range(3):
                e = self.tt(dve, factor, self.bank[3 + g][:], join, ALU.subtract)
                self.free[3 + g] = e
                e = self.fn(factor, factor, ACT.Exp, 0.0, HEAD ** -0.5, e)
                out = total if g == 0 else factor
                self.free[g] = self.tt(dve, out, self.bank[g][:], factor, ALU.mult, e, nums[g])
                if g:
                    self.tt(dve, total, total, factor, ALU.add)
                yield
            other = slice(HEAD * (1 - h), HEAD * (2 - h))
            dve.do(lambda: nc.vector.reciprocal(self.inv_den[rows, :], total[other, :]))
            self.tt(dve, tile_at(self.att[rows], i), total[rows, :], self.inv_den[rows, :], ALU.mult)
            yield

    def rwkv(self):
        dve, pool = self.dve, self.pool
        w = self.io["w_in"][0].rearrange("(k p) n -> p k n", p=P)
        with ExitStack() as ctx:
            sb = lambda name, shape, dtype=F32: self.sb(name, shape, dtype, ctx)
            R = self.rw = Scratch()
            R.mask4 = sb("rw_mask4", [P, 4, P])
            R.mask2 = sb("rw_mask2", [P, 2, P])
            R.restart = sb("rw_restart", [P, S], BF16)
            R.low = sb("rw_low", [P, S])
            R.low_g = sb("rw_low_g", [P, 2, S])
            R.keep_mu = sb("rw_keep_mu", [P, 3 * DT + 3])
            R.keep_a = sb("rw_keep_a", [P, DT])
            R.bias = sb("rw_bias", [P, 2])
            names = ["r", "k", "v", "t0", "sum", "lw", "rate", "kk", "e1", "gate", "gate_next"]
            tiles = sb("rw_tiles", [P, len(names), S])
            R.tile = {n: tiles[:, j, :] for j, n in enumerate(names)}
            R.ar = sb("rw_ar", [P, 4, 2, P])
            R.bt = sb("rw_b", [P, S])
            R.kt = sb("rw_k", [P, S])
            R.b_tok = sb("rw_b_tok", [P, 4, P])
            R.k_tok = sb("rw_k_tok", [P, 4, P])
            R.v_tok = sb("rw_v_tok", [P, 4, P])
            R.keep = sb("rw_keep", [P, 8, 4, P])
            R.de = sb("rw_de", [P, 4, 2, P])
            R.pw = sb("rw_pw", [P, 4, 2, P])
            R.pq = sb("rw_pq", [P, 4, 2, P])
            R.inv = sb("rw_inv", [P, 4, 2, P])
            R.ends = sb("rw_ends", [P, S // CHUNK])
            R.x_tok, R.u_tok = self.rinv[:, 0:P], self.rinv[:, P:2 * P]
            R.state = self.rinv[:, 2 * P:4 * P].rearrange("p (a n) -> p a n", a=2)
            R.y, R.y2 = self.sq[:, 0, :], self.sq[:, 1, :]
            mask4, mask2 = R.mask4, R.mask2
            strict_upper = lambda t: self.band(t, ALU.is_gt, 0, [[1, P]], -1, 0.0)
            self.same_block(mask4[:, 0, :], SUB, 1.0)
            strict_upper(mask4[:, 0, :])
            for j in (1, 3):
                self.same_block(mask4[:, j, :], CHUNK, 1.0)
                self.band(mask4[:, j, :], ALU.is_ge, 0, [[1, P]], -1, 0.0)
            self.same_block(mask4[:, 2, :], CHUNK, 1.0)
            strict_upper(mask4[:, 2, :])
            for j, size in ((0, SUB), (1, CHUNK)):
                self.same_block(mask2[:, j, :], size, 1.0)
                self.band(mask2[:, j, :], ALU.is_gt, 0, [[-1, P]], 1, 0.0)
            self.tt(pool, mask2[:, 1, :], mask2[:, 1, :], mask2[:, 0, :], ALU.subtract)
            self.fill_with(R.restart[:], 1.0)
            self.fill_with(R.restart[:].rearrange("p (c t) -> p c t", t=CHUNK)[:, :, 0:1], 0.0)
            self.fill_with(R.state, 0.0)
            for name, n, at in (("mu_shift", 3 * DT, 0), ("mu_low", 3, 3 * DT)):
                self.ts(dve, R.keep_mu[:, at:at + n], self.cols(name, n), -1.0, 1.0, ALU.mult, ALU.add)
            self.ts(dve, R.keep_a[:], self.cols("k_a", DT), -1.0, 1.0, ALU.mult, ALU.add)
            self.together()
            for n, at in enumerate((ATT_IN + 3 * D, ATT_IN + 3 * D + P, GATE0 - P)):
                t = self.product(self.bank[n][:], self.unit(w[:, :, at:at + P], DT), *self.h_parts(), True, True)
                out = R.low[:] if n == 0 else R.low_g[:, n - 1, :]
                e = self.shift_mix(out, self.bank[n][:], self.col("mu_low", n), R.keep_mu[:, 3 * DT + n:3 * DT + n + 1], t)
                if n == 0:
                    self.fn(R.low[0:LOW, :], R.low[0:LOW, :], ACT.Tanh, 0.0, 1.0, e)
                else:
                    self.fn(out, out, ACT.Sigmoid, 0.0, 1.0, e)
            self.together()
            run(self.rw_front(0))
            run(self.rw_front_rest(0, self.rw_unit(0, IN_R)))
            self.rw_arrive(0)
            self.rw_first_half(iter(()), self.rw_front(1))

            def body(i, loop):
                self.drain(loop)
                self.rw_second_half(i, self.rw_front_rest(i + 1, self.rw_unit(i + 1, IN_R)))
                self.rw_arrive(i + 1)
                self.rw_first_half(self.rw_close(i), self.rw_front(i + 2))

            self.book.run(DT - 2, body)
            self.rw_second_half(DT - 2, self.rw_front_rest(DT - 1, self.rw_unit(DT - 1, IN_R)))
            self.rw_arrive(DT - 1)
            self.rw_first_half(self.rw_close(DT - 2), iter(()))
            self.rw_second_half(DT - 1, iter(()))
            run(self.rw_close(DT - 1))
            self.together()

    def shift_mix(self, out, z, mu, keep, *after):
        self.ts(self.dve, out, z, keep, None, ALU.mult, None, *after)
        return self.stt(out[:, 1:S], z[:, 0:S - 1], mu, out[:, 1:S], ALU.mult, ALU.add)

    def rw_front(self, i):
        nc, act, dve, R = self.nc, self.act, self.dve, self.rw
        w = self.io["w_in"][0].rearrange("(k p) n -> p k n", p=P)
        w2, a2, g2 = (self.io[n][0] for n in ("w2", "a2", "g2"))
        T = R.tile
        col = lambda name, j=0: self.cols(name, DT, j * DT)[:, bass.ds(i, 1)]
        cols, raw = bass.ds(i * P, P), self.raw
        self.copy(dve, R.bias[:, 0:1], col("w0"))
        biases = self.copy(dve, R.bias[:, 1:2], col("a0"))
        slot, full = self.load((0, 0, None, w2[:, cols]), (LOW, 0, None, a2[:, cols]))
        unit = self.rw_unit(i, IN_K)
        td = self.mm(self.bank[5][:], raw[0:LOW, slot, 0:P], R.low[0:LOW, :], True, True, full, self.free[5], mark=True)
        self.pe.wait(self.free[6])
        ins = nc.tensor.matmul(self.bank[6][:], raw[LOW:2 * LOW, slot, 0:P], R.low[LOW:2 * LOW, :],
                               start=True, stop=True, skip_group_check=True)
        ta = self.raw_free[slot].mark(ins)
        self.free[5] = self.fn(T["lw"], self.bank[5][:], ACT.Sigmoid, R.bias[:, 0:1], 1.0, td, biases)
        self.free[6] = self.fn(T["rate"], self.bank[6][:], ACT.Sigmoid, R.bias[:, 1:2], 1.0, ta)
        yield
        yield from self.rw_projected(i, IN_K, unit, 7, T["k"])

    def rw_unit(self, i, j):
        w = self.io["w_in"][0].rearrange("(k p) n -> p k n", p=P)
        return self.unit(w[:, :, bass.ds(i * P + (ATT_IN + j * D), P)], DT)

    def rw_projected(self, i, j, unit, bank, out):
        done = []
        yield from self.product_steps(self.bank[bank][:], unit, *self.h_parts(), done, self.free[bank])
        mu, keep = self.cols("mu_shift", DT, j * DT), self.rw.keep_mu[:, j * DT:(j + 1) * DT]
        self.free[bank] = self.shift_mix(out, self.bank[bank][:], mu[:, bass.ds(i, 1)], keep[:, bass.ds(i, 1)], done[0])
        yield

    def rw_front_rest(self, i, unit):
        nc, act, dve, R = self.nc, self.act, self.dve, self.rw
        g2 = self.io["g2"][0]
        T = R.tile
        col = lambda name: self.cols(name, DT)[:, bass.ds(i, 1)]
        cols, raw = bass.ds(i * P, P), self.raw
        dve.wait(act.now())
        v_unit = self.rw_unit(i, IN_V)
        self.ts(dve, T["kk"], T["k"], col("k_k"), None, ALU.mult)
        e = self.tt(dve, T["t0"], T["kk"], T["kk"], ALU.mult)
        m = self.mm(self.bank[5][:], self.head_ones[:], T["t0"], True, True, e, self.free[5], mark=True)
        yield
        self.ts(dve, T["lw"], T["lw"], -float(2.718281828459045 ** -0.5), None, ALU.mult)
        dve.do(lambda: nc.vector.tensor_tensor_scan(T["sum"], R.restart[:], T["lw"], 0.0, ALU.mult, ALU.add))
        self.tt(dve, T["lw"], T["sum"], T["lw"], ALU.subtract)
        self.free[5] = self.ts(dve, T["t0"], self.bank[5][:], 1e-24, None, ALU.max, None, m)
        yield
        norm = self.sqrt_inverse(T["t0"])
        yield
        yield from self.rw_projected(i, IN_R, unit, 6, T["r"])
        self.ts(dve, T["e1"], T["rate"], col("k_a"), R.keep_a[:, bass.ds(i, 1)], ALU.mult, ALU.add)
        self.tt(dve, T["k"], T["k"], T["e1"], ALU.mult)
        e = self.tt(dve, T["kk"], T["kk"], T["t0"], ALU.mult, norm)
        self.fn(T["lw"], T["lw"], ACT.Exp, 0.0, 1.0, e)
        self.fn(T["e1"], T["sum"], ACT.Exp, 0.0, -1.0)
        self.fn(T["sum"], T["sum"], ACT.Exp, 0.0, 1.0)
        yield
        yield from self.rw_projected(i, IN_V, v_unit, 7, T["v"])
        slot, full = self.load((0, 0, None, g2[0:P, cols]), (P - 32, P, None, g2[P:GATE_LOW, cols]))
        self.mm(self.bank[5][:], raw[0:P, slot, 0:P], R.low_g[:, 0, :], True, False, full, self.free[5])
        ins = nc.tensor.matmul(self.bank[5][:], raw[P - 32:P, slot, P:2 * P], R.low_g[P - 32:P, 1, :],
                               start=False, stop=True, skip_group_check=True)
        self.free[5] = self.copy(act, T["gate_next"], self.bank[5][:], self.raw_free[slot].mark(ins))

    def rw_arrive(self, i):
        act, dve, R = self.act, self.dve, self.rw
        T, ar, bt, kt = R.tile, R.ar, R.bt, R.kt
        col = lambda name: self.cols(name, DT)[:, bass.ds(i, 1)]
        done = (act.now(), dve.now())
        tiles4 = lambda ap: ap.rearrange("p (j t) -> p j t", j=4)

        def turned(src, dst, bank, e, q):
            for j in range(4):
                t = self.transpose(self.bank[bank][:, j * P:(j + 1) * P], src[:, j * P:(j + 1) * P], e,
                                   self.free[bank], mark=j == 3)
            self.free[bank] = self.copy(q, dst[:].rearrange("p j t -> p (j t)"), self.bank[bank][:], t)

        e = self.tt(dve, kt[:], T["k"], T["e1"], ALU.mult, *done)
        turned(kt[:], R.k_tok, 0, e, act)
        self.tt(dve, T["t0"], T["kk"], T["rate"], ALU.mult, act.now())
        e = self.tt(dve, bt[:], T["t0"], T["e1"], ALU.mult)
        turned(bt[:], R.b_tok, 1, e, act)
        self.tt(dve, ar[:, :, 1, :], tiles4(T["r"]), tiles4(T["sum"]), ALU.mult)
        self.stt(ar[:, :, 0, :], tiles4(T["kk"]), -1.0, tiles4(T["lw"]), ALU.mult, ALU.mult)
        self.copy(dve, R.ends[:], T["sum"][:, CHUNK - 1::CHUNK])
        turned(T["v"], R.v_tok, 2, done[1], act)
        e = self.stt(T["t0"], T["r"], col("r_k"), T["k"], ALU.mult, ALU.mult)
        m = self.mm(self.bank[3][:], self.head_ones[:], T["t0"], True, True, e, self.free[3], mark=True)
        self.free[3] = self.tt(dve, tile_at(self.mixed, i), self.bank[3][:], T["v"], ALU.mult, m)

    def rw_first_half(self, close, front):
        self.pe.wait(self.act.now(), self.dve.now())

        def settle():
            yield from close
            self.copy(self.dve, self.rw.tile["gate"], self.rw.tile["gate_next"], self.act.now())

        interleave(self.rw_invert((0, 1), range(4)), woven(front, settle(), 1, 1), *PACE_INVERT)

    def rw_second_half(self, i, front):
        interleave(self.rw_invert((2, 3), range(5, 8)), self.rw_chain((0, 1)), *PACE_CHAIN)
        interleave(self.rw_chain((2, 3)), front, *PACE_REST)
        self.free[4] = self.copy(self.dve, self.rw.y, self.bank[4][:], self.y_done)

    def rw_invert(self, spans, banks):
        act, dve, R = self.act, self.dve, self.rw
        ar, bt, kt, keep, de, pw, pq, inv = R.ar, R.bt, R.kt, R.keep, R.de, R.pw, R.pq, R.inv
        bank, free = self.bank, self.free
        turn = 0

        def next_bank():
            nonlocal turn
            turn += 1
            return banks[turn % len(banks)]

        cells = [(hd, j) for j in spans for hd in range(2)]
        wait = [None] * 4
        for m, (hd, j) in enumerate(cells):
            rows = slice(HEAD * hd, HEAD * (hd + 1))
            b = next_bank()
            rhs = ar[rows, j, :, :].rearrange("p a t -> p (a t)")
            self.mm(bank[b][:, 0:2 * P], bt[rows, j * P:(j + 1) * P], rhs, True, False, free[b])
            t = self.mm(bank[b][:, 2 * P:], kt[rows, j * P:(j + 1) * P], rhs, False, True, mark=True)
            kp = keep[:, 4 * hd + j, :, :]
            free[b] = self.tt(dve, kp, bank[b][:].rearrange("p (a t) -> p a t", a=4), R.mask4[:], ALU.mult, t)
            b = next_bank()
            t = self.mm(bank[b][:, 0:P], ar[rows, j, 0, :], bt[rows, j * P:(j + 1) * P], True, True, free[b], mark=True)
            self.tt(dve, de[:, m, 0, :], bank[b][:, 0:P], R.mask2[:, 0, :], ALU.mult, t)
            free[b] = self.tt(dve, de[:, m, 1, :], bank[b][:, 0:P], R.mask2[:, 1, :], ALU.mult, serial=False)
            self.tt(dve, inv[:, m, 0, :], self.ident[:], de[:, m, 0, :], ALU.add)
            wait[m] = self.tt(dve, inv[:, m, 1, :], self.ident[:], kp[:, KEEP_T, :], ALU.add, serial=False)
            yield

        def step(products, evac):
            for m in range(4):
                b = next_bank()
                todo = products(m)
                for n, (l, rr) in enumerate(todo):
                    t = self.mm(bank[b][:, n * P:(n + 1) * P], l, rr, n == 0, n == len(todo) - 1,
                                free[b], wait[m], mark=n == len(todo) - 1)
                wait[m] = free[b] = evac(m, bank[b], t)
                if m % 2:
                    yield

        T_of = lambda m: keep[:, 4 * cells[m][0] + cells[m][1], KEEP_T, :]
        Dn, DTn, En = (lambda m: de[:, m, 0, :]), T_of, (lambda m: de[:, m, 1, :])
        pair = lambda t, m: t[:, m, :, :].rearrange("p a t -> p (a t)")

        def copy_to(t):
            return lambda m, bk, e: self.copy(act, pair(t, m), bk[:, 0:2 * P], e)

        def grow(out):
            def evac(m, bk, e):
                a = self.copy(act, pair(out, m), bk[:, 0:2 * P], e)
                return self.tt(dve, pair(inv, m), bk[:, 2 * P:4 * P], pair(inv, m), ALU.add, e, a)
            return evac

        def add_inv(m, bk, e):
            return self.tt(dve, pair(inv, m), bk[:, 0:2 * P], pair(inv, m), ALU.add, e)

        def factors(m, bk, e):
            self.tt(dve, pq[:, m, 0, :], bk[:, 0:P], self.ident[:], ALU.add, e)
            return self.tt(dve, pq[:, m, 1, :], bk[:, P:2 * P], inv[:, m, 0, :], ALU.add, serial=False)

        yield from step(lambda m: [(DTn(m), Dn(m)), (Dn(m), DTn(m))], copy_to(pw))
        yield from step(lambda m: [(pw[:, m, 1, :], pw[:, m, 0, :]), (pw[:, m, 0, :], pw[:, m, 1, :]),
                                   (pw[:, m, 1, :], inv[:, m, 0, :]), (inv[:, m, 0, :], pw[:, m, 1, :])], grow(pq))
        yield from step(lambda m: [(pq[:, m, 1, :], pq[:, m, 0, :]), (pq[:, m, 0, :], pq[:, m, 1, :]),
                                   (pq[:, m, 1, :], inv[:, m, 0, :]), (inv[:, m, 0, :], pq[:, m, 1, :])], grow(pw))
        yield from step(lambda m: [(pw[:, m, 1, :], inv[:, m, 0, :]), (inv[:, m, 0, :], pw[:, m, 1, :])], add_inv)
        yield from step(lambda m: [(inv[:, m, 1, :], En(m)), (En(m), inv[:, m, 1, :])], copy_to(pw))
        yield from step(lambda m: [(pw[:, m, 0, :], pw[:, m, 1, :]), (pw[:, m, 1, :], inv[:, m, 0, :])], factors)
        yield from step(lambda m: [(pq[:, m, 1, :], pq[:, m, 0, :])],
                        lambda m, bk, e: self.copy(act, T_of(m), bk[:, 0:P], e))

    def rw_chain(self, spans):
        nc, act, dve, R = self.nc, self.act, self.dve, self.rw
        keep, ar = R.keep, R.ar
        bank, free = self.bank, self.free
        X, U, Y = bank[0], bank[1], bank[4]
        state, x_tok, u_tok = R.state, R.x_tok, R.u_tok
        heads = [slice(HEAD * hd, HEAD * (hd + 1)) for hd in range(2)]
        if spans[0] == 0:
            self.s_ready = dve.do(lambda: nc.vector.memset(state[:, 0, :], 0.0))
            self.pe.wait(free[4])
        self.pe.wait(act.now(), dve.now())
        for j in spans:
            for hd, cs in enumerate(heads):
                self.mm(X[:, cs], keep[:, 4 * hd + j, KEEP_AK, :], R.v_tok[:, j, cs], hd == 0, False, free[0])
            for ch in range(2):
                c = 2 * j + ch
                old, new = state[:, c % 2, :], state[:, (c + 1) % 2, :]
                half = slice(CHUNK * ch, CHUNK * (ch + 1))
                t = self.mm(X[half, 0:P], ar[:, j, 0, half], old, False, ch == 1, self.s_ready, mark=True)
                free[0] = e = self.copy(dve, x_tok[half, :], X[half, 0:P], t)
                self.mm(Y[:, c * CHUNK:(c + 1) * CHUNK], old, ar[:, j, 1, half], c == 0, False)
                sb_ = bank[2 + c % 2]
                self.mm(sb_[:, 0:P], self.ident[:], old, True, False, free[2 + c % 2])
                self.mm(sb_[:, 0:P], R.k_tok[half, j, :], R.v_tok[half, j, :], False, False)
                yield
                for hd, cs in enumerate(heads):
                    t = self.mm(U[:, cs], keep[half, 4 * hd + j, KEEP_T, :], x_tok[half, cs],
                                ch == 0 and hd == 0, ch == 1 and hd == 1, e, free[1], mark=hd == 1)
                free[1] = e = self.copy(act, u_tok[half, :], U[half, 0:P], t)
                yield
                t = self.mm(sb_[:, 0:P], R.b_tok[half, j, :], u_tok[half, :], False, True, e, mark=True)
                if c < S // CHUNK - 1:
                    if c == 0:
                        dve.do(lambda: nc.vector.memset(new, 0.0))
                    self.ts(dve, new[heads[0], heads[0]], sb_[heads[0], heads[0]], R.ends[heads[0], c:c + 1], None, ALU.mult, None, t)
                    self.s_ready = self.ts(dve, new[heads[1], heads[1]], sb_[heads[1], heads[1]],
                                           R.ends[heads[1], c:c + 1], None, ALU.mult, serial=False)
                    free[2 + c % 2] = self.s_ready
                yield
            for hd, cs in enumerate(heads):
                out = Y[cs, j * P:(j + 1) * P]
                self.mm(out, u_tok[:, cs], keep[:, 4 * hd + j, KEEP_RB, :], False, False)
                self.y_done = self.mm(out, R.v_tok[:, j, cs], keep[:, 4 * hd + j, KEEP_RK, :], False, True, mark=True)

    def rw_close(self, i):
        nc, act, dve, R = self.nc, self.act, self.dve, self.rw
        bank, free, T = self.bank, self.free, R.tile
        col = lambda name: self.cols(name, DT)[:, bass.ds(i, 1)]
        y, y2 = R.y, R.y2
        m = self.mm(bank[4][:], self.head_ones[:], y, True, True, dve.now(), free[4], mark=True)
        yield
        free[4] = self.stt(y, bank[4][:], -1.0 / HEAD, y, ALU.mult, ALU.add, m)
        e = self.tt(dve, y2, y, y, ALU.mult)
        m = self.mm(bank[4][:], self.head_ones[:], y2, True, True, e, free[4], mark=True)
        yield
        free[4] = self.ts(dve, y2, bank[4][:], 1.0 / HEAD, GN_EPS, ALU.mult, ALU.add, m)
        e = self.sqrt_inverse(y2)
        yield
        self.tt(dve, y, y, y2, ALU.mult, e)
        self.ts(dve, y, y, col("lnx_w"), col("lnx_b"), ALU.mult, ALU.add)
        self.tt(dve, y, y, tile_at(self.mixed, i), ALU.add)
        self.tt(dve, tile_at(self.mixed, i), y, T["gate"], ALU.mult)

    def merge(self):
        act, dve, io = self.act, self.dve, self.io
        w = io["w_in"][0].rearrange("(k p) n -> p k n", p=P)
        wa = io["w_att_out"][0].rearrange("(k p) n -> p k n", p=P)
        wr = io["w_rwkv_out"][0].rearrange("(k p) n -> p k n", p=P)
        bg = self.cols("b_gate", 2 * DT)
        with ExitStack() as ctx:
            sb = lambda name, shape, dtype=F32: self.sb(name, shape, dtype, ctx)
            a_high, a_low = sb("mg_a_high", [P, 4, S], F32R), sb("mg_a_low", [P, 4, S], F32R)
            r_high, r_low = sb("mg_r_high", [P, DT, S], F32R), sb("mg_r_low", [P, DT, S], F32R)
            both = sb("mg_both", [P, DT, S])
            gate = sb("mg_gate", [P, 2, S])
            bias = sb("mg_bias", [P, 2, 2])
            for k in range(4):
                self.split(a_high[:, k, :], a_low[:, k, :], self.att[:, k, :])
            for k in range(DT):
                self.split(r_high[:, k, :], r_low[:, k, :], self.mixed[:, k, :])
            part = lambda t: lambda k: t[:, k, :]
            self.together()

            def sources(i):
                return [t for u in range(2) for t in (
                    (w[:, :, bass.ds((2 * i + u) * P + GATE0, P)], DT), (w[:, :, bass.ds((2 * i + u) * P + (GATE0 + D), P)], DT),
                    (wa[:, :, bass.ds((2 * i + u) * P, P)], 4), (wr[:, :, bass.ds((2 * i + u) * P, P)], DT))]

            parts = (self.h_parts(), self.h_parts(), (part(a_high), part(a_low)), (part(r_high), part(r_low)))

            def step(i, before, name, take):
                for u in range(2):
                    b = self.bank[4 * u:4 * u + 4]
                    ts = []
                    for j in range(2):
                        self.copy(dve, bias[:, u, j:j + 1], bg[:, bass.ds(2 * i + (u + j * DT), 1)], act.now())
                    biases = dve.now()
                    for j in range(4):
                        ts.append(self.product(b[j][:], take(), *parts[j], True, True, before(f"evac{u}")))
                        if j == 1:
                            for jj in range(2):
                                self.fn(gate[:, jj, :], b[jj][:], ACT.Sigmoid, bias[:, u, jj:jj + 1], 1.0, ts[jj], biases)
                            gates = act.now()
                    for j in range(2):
                        self.tt(dve, gate[:, j, :], gate[:, j, :], b[2 + j][:], ALU.mult, ts[2 + j], gates)
                    e = self.tt(dve, tile_at(both, 2 * i + u), gate[:, 0, :], gate[:, 1, :], ALU.add)
                    name(f"evac{u}", e)
                    self.act.wait(e)

            wo = io["w_o"][0].rearrange("(k p) n -> p k n", p=P)
            self.each(DT // 2, sources, step, (wo[:, :, 0:P], DT))
            self.together()
            for k in range(DT):
                self.split(self.h_high[:, k, :], self.h_low[:, k, :], both[:, k, :])
            self.together()
        self.project(io["w_o"][0], self.h_high, self.h_low, DT, 2)

    def project(self, weight, high, low, tiles, scale=None, then=None):
        w = weight.rearrange("(k p) n -> p k n", p=P)
        parts = [(k0, min(UNIT_K, tiles - k0)) for k0 in range(0, tiles, UNIT_K)]
        outputs = 4 // len(parts)
        todo = [(u, k0, n) for u in range(outputs) for k0, n in parts]

        def step(i, before, name, take):
            for u, k0, n in todo:
                last = k0 + n == tiles
                t = self.product(self.bank[u][:], take(), lambda k: high[:, k0 + k, :], lambda k: low[:, k0 + k, :],
                                 k0 == 0, last, before(f"evac{u}"))
                if last:
                    x = tile_at(self.x, outputs * i + u)
                    if scale is None:
                        e = self.tt(self.dve, x, self.bank[u][:], x, ALU.add, t)
                    else:
                        gt = self.mod[:, scale * DT:(scale + 1) * DT][:, bass.ds(outputs * i + u, 1)]
                        e = self.stt(x, self.bank[u][:], gt, x, ALU.mult, ALU.add, t)
                    name(f"evac{u}", e)

        self.each(DT // outputs, lambda i: [(w[:, k0:k0 + n, bass.ds((outputs * i + u) * P, P)], n) for u, k0, n in todo],
                  step, then)
        self.together()

    def ffn(self, name, w_gate, w_up, taps, biases, both, w_down, scale=None):
        dve, act = self.dve, self.act
        wg = w_gate.rearrange("(k p) n -> p k n", p=P)
        wu = w_up.rearrange("(k p) n -> p k n", p=P)
        with ExitStack() as ctx:
            high = self.sb(f"{name}_high", [P, FT, S], F32R, ctx)
            low = self.sb(f"{name}_low", [P, FT, S], F32R, ctx)
            c = self.sb(f"{name}_c", [P, 2, 2, S], F32, ctx)
            self.together()

            todo = [(u, j) for u in range(2) for j in range(2)]

            def step(i, before, name, take):
                for u, j in todo:
                    n, bank, out = 2 * i + u, self.bank[2 * u + j], c[:, u, j, :]
                    t = self.product(bank[:], take(), *self.h_parts(), True, True, before(f"evac{u}{j}"))
                    if j == 0 or both:
                        tap = [taps(j, a)[:, bass.ds(n, 1)] for a in range(3)]
                        self.ts(dve, out, bank[:], tap[2], biases(j)[:, bass.ds(n, 1)], ALU.mult, ALU.add, t)
                        self.stt(out[:, 1:S], bank[:, 0:S - 1], tap[1], out[:, 1:S], ALU.mult, ALU.add)
                        e = self.stt(out[:, 2:S], bank[:, 0:S - 2], tap[0], out[:, 2:S], ALU.mult, ALU.add)
                        name(f"evac{u}{j}", e)
                    if j == 0:
                        s = self.fn(out, out, ACT.Silu, 0.0, 1.0, e)
                        gate = out
                    else:
                        e = self.tt(dve, gate, gate, out if both else bank[:], ALU.mult, s, t)
                        if not both:
                            name(f"evac{u}1", e)
                        self.split(tile_at(high, n), tile_at(low, n), gate)

            down = w_down.rearrange("(k p) n -> p k n", p=P)
            self.each(FT // 2, lambda i: [((wg, wu)[j][:, :, bass.ds((2 * i + u) * P, P)], DT) for u, j in todo],
                      step, (down[:, 0:UNIT_K, 0:P], UNIT_K))
            self.together()
            self.project(w_down, high, low, FT, scale)

    def even_layer(self):
        io, dve, act, pool = self.io, self.dve, self.act, self.pool
        w = io["w_in_even_2"][0].rearrange("(k p) n -> p k n", p=P)
        W4 = 4 * P
        with ExitStack() as ctx:
            sb = lambda n, shape, dt=F32: self.sb(f"ev_{n}", shape, dt, ctx)
            high, low = sb("high", [P, DT, S], F32R), sb("low", [P, DT, S], F32R)
            z = sb("z", [P, 2, S])
            c = sb("c", [P, 2, S])
            zp = sb("zp", [P, S])
            s1, s2 = sb("s1", [P, S]), sb("s2", [P, S])
            pos, posf = sb("pos", [P, S], I32), sb("posf", [P, S])
            cnt = sb("cnt", [P, 4, S])
            pool.do(lambda: self.nc.gpsimd.iota(pos[:], pattern=[[1, S]], base=1, channel_multiplier=0))
            e = self.copy(pool, posf[:], pos[:])
            for g, window in enumerate(POOL_WINDOWS):
                self.ts(dve, cnt[:, g, :], posf[:], float(window), None, ALU.min, None, e)
                dve.do(lambda: self.nc.vector.reciprocal(cnt[:, g, 0:window], cnt[:, g, 0:window]))
                dve.do(lambda: self.nc.vector.memset(cnt[:, g, window:S], 1.0 / window))
            self.together()

            GATE_B, GATE_C, VALUE = range(3)
            todo = [(u, j) for u in range(2) for j in (GATE_C, VALUE, GATE_B)]

            def step(i, before, name, take):
                for u, j in todo:
                    n, bank = 2 * i + u, self.bank[3 * u + j]
                    t = self.product(bank[:], take(), *self.h_parts(), True, True, before(f"evac{u}"))
                    if j == GATE_C:
                        e = self.copy(act, c[:, u, :], bank[:], t, before(f"evac{u}"))
                    elif j == VALUE:
                        tap = [self.cols("conv_a_2", 4, 4 * a)[:, bass.ds(n, 1)] for a in range(3)]
                        zu, cu = z[:, u, :], c[:, u, :]
                        self.tt(dve, zu, bank[:], cu, ALU.mult, t, e)
                        self.ts(dve, cu, zu, tap[2], None, ALU.mult)
                        self.stt(cu[:, 1:S], zu[:, 0:S - 1], tap[1], cu[:, 1:S], ALU.mult, ALU.add)
                        self.stt(cu[:, 2:S], zu[:, 0:S - 2], tap[0], cu[:, 2:S], ALU.mult, ALU.add)
                    else:
                        e = self.tt(dve, z[:, u, :], c[:, u, :], bank[:], ALU.mult, t)
                        name(f"evac{u}", e)
                        self.split(tile_at(high, n), tile_at(low, n), z[:, u, :])

            self.each(2, lambda i: [(w[:, :, bass.ds((2 * i + u) * P + j * W4, P)], DT) for u, j in todo],
                      step, (w[:, :, 3 * W4:3 * W4 + P], DT))
            units, self.carried = [self.carried], None
            slot_pool = None
            for g, window in enumerate(POOL_WINDOWS):
                if g < 3:
                    units.append(self.unit(w[:, :, 3 * W4 + (g + 1) * P:3 * W4 + (g + 2) * P], DT))
                slot, full = self.load((0, 0, None, io["w_pool_2"][0, g]))
                t = self.product(self.bank[6][:], units[g], *self.h_parts(), True, True, self.free[6])
                self.free[6] = self.copy(dve, zp[:], self.bank[6][:], t)
                src, spare, width = zp[:], [s1[:], s2[:]], 1
                while width < window:
                    dst = spare[0]
                    self.copy(dve, dst[:, 0:width], src[:, 0:width])
                    self.tt(dve, dst[:, width:], src[:, width:], src[:, 0:S - width], ALU.add)
                    src, spare, width = dst, spare[::-1], 2 * width
                self.tt(dve, src, src, cnt[:, g, :], ALU.mult)
                e = self.tt(dve, zp[:], src, zp[:], ALU.subtract)
                self.pe.wait(e, full, self.free[7])
                t = self.raw_free[slot].mark(self.nc.tensor.matmul(self.bank[7][:], self.raw[:, slot, 0:P], zp[:],
                                                                   start=True, stop=True, skip_group_check=True))
                self.free[7] = self.ts(dve, s1[:], self.bank[7][:], self.col("pool_scale_2", g), None, ALU.mult, None, t)
                self.split(high[:, 4 + g, :], low[:, 4 + g, :], s1[:])
            self.together()
            self.project(io["w_out_even_2"][0], high, low, DT)

    def odd_layer(self):
        io, dve, act = self.io, self.dve, self.act
        w = io["w_in_odd_2"][0].rearrange("(k p) n -> p k n", p=P)
        with ExitStack() as ctx:
            sb = lambda n, shape, dt=F32: self.sb(f"od_{n}", shape, dt, ctx)
            high, low = sb("high", [P, DT, S], F32R), sb("low", [P, DT, S], F32R)
            uv = sb("uv", [P, 2 * DT, S])
            vn, v_tok = sb("vn", [P, 2, S]), sb("v_tok", [P, 2, S])
            ws, wst = sb("ws", [P, 2, P]), sb("wst", [P, 2, P])
            ws_all, bias = sb("ws_all", [P, DT, P]), sb("bias", [P, DT, P])
            tril = sb("tril", [P, P])
            self.fill_with(tril[:], 1.0)
            self.band(tril[:], ALU.is_ge, 0, [[-1, P]], 1, 0.0)
            self.together()
            self.sp.wait(dve.now())
            self.load_done.mark(self.nc.sync.dma_start(ws_all[:], io["w_spatial_2"][0].rearrange("h t s -> t h s")))
            full = self.load_done.mark(self.nc.sync.dma_start(bias[:], io["b_spatial_2"][0].partition_broadcast(P)))

            def step(i, before, name, take):
                for n in range(4):
                    t = self.product(self.bank[n][:], take(), *self.h_parts(), True, True, before(f"evac{n}"))
                    e = self.fn(tile_at(uv, 4 * i + n), self.bank[n][:], ACT.Gelu, 0.0, 1.0, t)
                    name(f"evac{n}", e)

            out = io["w_out_odd_2"][0].rearrange("(k p) n -> p k n", p=P)
            self.each(4, lambda i: [(w[:, :, bass.ds((4 * i + n) * P, P)], DT) for n in range(4)],
                      step, (out[:, :, 0:P], DT))
            self.together()
            dve.wait(self.inverse_rms(uv[:, DT:2 * DT, :], RMS_EPS), full)

            def head(i, loop):
                before = lambda key: loop.before(self.book.counts, key)
                for u in range(2):
                    n = 2 * i + u
                    e = self.tt(dve, ws[:, u, :], tile_at(ws_all, n), tril[:], ALU.mult, before(f"ws{u}"))
                    t = self.transpose(self.bank[u][:, 0:P], ws[:, u, :], e, before(f"w{u}"), mark=True)
                    loop.name(f"ws{u}", t)
                    e2 = self.stt(vn[:, u, :], tile_at(uv, n + DT), self.cols("sgu_norm_2", DT)[:, bass.ds(n, 1)],
                                  self.rinv[:], ALU.mult, ALU.mult)
                    e = self.copy(dve, wst[:, u, :], self.bank[u][:, 0:P], t)
                    loop.name(f"w{u}", e)
                    for q in range(4):
                        t = self.transpose(self.bank[2 + u][:, q * P:(q + 1) * P], vn[:, u, q * P:(q + 1) * P], e2,
                                           before(f"v{u}"), mark=q == 3)
                    e = self.copy(act, v_tok[:, u, :], self.bank[2 + u][:], t, before(f"g{u}"))
                    loop.name(f"v{u}", e)
                    for q in range(4):
                        t = self.mm(self.bank[4 + u][:, q * P:(q + 1) * P], v_tok[:, u, q * P:(q + 1) * P], wst[:, u, :],
                                    q == 0, q == 3, e, self.dve.now(), before(f"o{u}"), mark=q == 3)
                    loop.name(f"g{u}", t)
                    b4 = bias[:, bass.ds(n, 1), :].to_broadcast([P, 4, P])
                    e = self.tt(dve, vn[:, u, :].rearrange("p (q t) -> p q t", q=4),
                                self.bank[4 + u][:].rearrange("p (q t) -> p q t", q=4), b4, ALU.add, t)
                    loop.name(f"o{u}", e)
                    self.tt(dve, vn[:, u, :], tile_at(uv, n), vn[:, u, :], ALU.mult)
                    self.split(tile_at(high, n), tile_at(low, n), vn[:, u, :])

            self.book.run(4, head)
            self.together()
            self.project(io["w_out_odd_2"][0], high, low, DT)

    def store(self):
        with ExitStack() as ctx:
            out = self.sb("out_rows", [P, 4, D], F32, ctx)
            rows = self.io["out"][0].rearrange("(t p) d -> p t d", p=P)
            for t in range(4):
                for half in range(2):
                    b = 2 * (t % 2) + half
                    for f in range(4):
                        m = self.transpose(self.bank[b][:, f * P:(f + 1) * P], self.x[:, 4 * half + f, t * P:(t + 1) * P],
                                           self.dve.now(), self.free[b], mark=f == 3)
                    self.free[b] = self.copy(self.act, out[:, t, half * S:(half + 1) * S], self.bank[b][:], m)
                self.sp.wait(self.free[b])
                done = self.store_done.mark(self.nc.sync.dma_start(rows[:, t, :], out[:, t, :]))
            self.sp.wait(done)

    def gated_ffn(self, layer):
        io, tail = self.io, "b" if layer else ""
        self.ffn(f"g{layer}", io["w_ffn_gate_2"][layer], io["w_ffn_up_2"][layer],
                 lambda j, a: self.cols("conv_ffn_2" + tail, FT, FT * a), lambda j: self.cols("b_conv_ffn_2" + tail, FT),
                 False, io["w_ffn_down_2"][layer])

    def build(self):
        io = self.io
        self.x = self.sb("x_res", [P, DT, S])
        self.h_high, self.h_low = self.sb("h_high", [P, DT, S], F32R), self.sb("h_low", [P, DT, S], F32R)
        self.raw = self.sb("w_raw", [P, RAW_SLOTS, UNIT_K * P])
        self.w_high = self.sb("w_high", [P, SPLIT_SLOTS, UNIT_K * P], F32R)
        self.w_low = self.sb("w_low", [P, SPLIT_SLOTS, UNIT_K * P], F32R)
        self.rinv = self.sb("rinv", [P, S])
        self.sq = self.sb("sq", [P, 2, S])
        self.mod = self.sb("mod", [P, 6 * DT])
        self.gain1, self.gain2 = self.sb("gain1", [P, DT]), self.sb("gain2", [P, DT])
        self.ident = self.sb("ident", [P, P])
        self.ident_bf = self.sb("ident_bf", [P, P], BF16)
        self.ones = self.sb("ones", [P, P])
        self.head_ones = self.sb("head_ones", [P, P])
        self.vec = self.sb("vec", [P, VEC_GROUPS * P])
        self.load_x_done = Count(self.book, "load_x_done", 16)
        with ExitStack() as scope:
            xrow, full = self.load_x(scope)
            self.constants()
            self.vectors(scope)
            self.turn_x(xrow, full)
        self.ada()
        mod, col = self.mod, self.col
        self.together()
        self.norm(self.x, lambda k: self.gain1[:, k:k + 1], lambda k: mod[:, k:k + 1])
        self.together()

        def mixers():
            with ExitStack() as ctx:
                self.att = self.sb("att", [P, 4, S], F32, ctx)
                self.mixed = self.sb("mixed", [P, DT, S], F32, ctx)
                for stage in (self.attention, self.rwkv, self.merge)[:self.stop]:
                    stage()

        def first_ffn():
            self.norm(self.x, lambda k: self.gain2[:, k:k + 1], lambda k: mod[:, 3 * DT + k:3 * DT + k + 1])
            self.ffn("f", io["w_up"][0][:, 0:F], io["w_up"][0][:, F:2 * F],
                     lambda j, a: self.cols(f"conv_w{a}", FT, FT * j), lambda j: self.cols("conv_b", FT, FT * j),
                     True, io["w_down"][0], 5)

        def first_layer():
            self.norm(self.x, lambda k: col("norm_f_w", k), keep=True)
            self.together()
            self.norm(self.x, lambda k: col("norm_mix_2", k))
            self.even_layer()

        def layer_ffn(layer):
            self.norm(self.x, lambda k: col("norm_ffn_2", layer * DT + k))
            self.gated_ffn(layer)

        def second_layer():
            self.norm(self.x, lambda k: col("norm_mix_2", DT + k))
            self.odd_layer()

        mixers()
        if self.stop > 3:
            for stage in (first_ffn, first_layer, lambda: layer_ffn(0), second_layer, lambda: layer_ffn(1))[:self.stop - 3]:
                self.together()
                stage()
        self.together()
        if self.stop < 8:
            return self.book.learned
        self.norm(self.x, lambda k: col("final_norm_2", k), keep=True)
        self.together()
        self.store()
        return self.book.learned


def build_program(make, io_of, stop=99):
    known = None
    for _ in range(2):
        nc = make()
        with ExitStack() as ctx:
            known = Kernel(nc, ctx, io_of(nc), known, stop).build()
    return nc


_OUT = ((1, S, D), "float32")


def kernel(**inputs):
    import numpy as np
    import concourse.bacc as bacc
    from concourse.bass_utils import run_bass_kernel_spmd

    arrays = {f"in_{n}": np.ascontiguousarray(a) for n, a in inputs.items()}

    def io_of(nc):
        io = {n: nc.dram_tensor(f"in_{n}", a.shape, mybir.dt.from_np(np.asarray(a).dtype), kind="ExternalInput").ap()
              for n, a in inputs.items()}
        io["out"] = nc.dram_tensor("out_0", _OUT[0], F32, kind="ExternalOutput").ap()
        return io

    nc = build_program(lambda: bacc.Bacc("TRN2", target_bir_lowering=False, num_devices=1), io_of)
    r = run_bass_kernel_spmd(nc, [arrays], core_ids=[0])
    return r.results[0]["out_0"]
```

```python
from contextlib import ExitStack

import concourse.bass as bass
from concourse import mybir

F32 = mybir.dt.float32
F32R = mybir.dt.float32r
BF16 = mybir.dt.bfloat16
I32 = mybir.dt.int32
ALU = mybir.AluOpType
ACT = mybir.ActivationFunctionType
AX = mybir.AxisListType

P = 128
S = 512
D = 1024
DT = D // P
ATT_GROUPS, ATT_WIDTH, HEAD = 3, 512, 64
DILATIONS = (1, 4, 16)
BLK = 128
PAIRS_ATT = ATT_WIDTH // P
LOW = 64
GATE_LOW = 160
CHUNK = 64
SUB = 16
F = 2816
FT = F // P
ATT_IN = ATT_GROUPS * 3 * ATT_WIDTH
RWKV_IN = 3 * D + 2 * LOW + GATE_LOW
GATE0 = ATT_IN + RWKV_IN
RMS_EPS = 1e-6
GN_EPS = 64e-5
MASKED = -1e30
POOL_WINDOWS = (2, 4, 8, 16)
UNIT_K = 11
RAW_SLOTS = 4
SPLIT_SLOTS = 2
LOW_RANK_COLUMNS = (ATT_IN + 3 * D, ATT_IN + 3 * D + P, GATE0 - P)
VEC_GROUPS = 6
FIRST_COUNT = 1024


IN_R, IN_K, IN_V = range(3)
KEEP_T, KEEP_RB, KEEP_AK, KEEP_RK = range(4)
PACE_INVERT, PACE_CHAIN, PACE_REST = (4, 3), (1, 1), (1, 1)
ADA_PER_PRODUCT = 1
ADA_PER_PAIR = 8 * ADA_PER_PRODUCT


def run(steps):
    for _ in steps:
        pass


def woven(a, b, na, nb):
    lines = [(a, na), (b, nb)]
    while lines:
        for line in list(lines):
            for _ in range(line[1]):
                if next(line[0], lines) is lines:
                    lines.remove(line)
                    break
                yield


def interleave(a, b, na, nb):
    run(woven(a, b, na, nb))


def in_order(ap, g):
    return ap.rearrange("p (i r) -> p r i", r=DILATIONS[g])


def tile_at(t, i):
    return t[:, bass.ds(i, 1), :].rearrange("p a n -> p (a n)")


class Scratch:
    pass


class Count:

    def __init__(self, book, name, step, start=0):
        self.book, self.name, self.step = book, name, step
        self.sem = book.ctx.enter_context(book.nc.semaphore(name))
        self.value = start
        if start:
            book.nc.sync.sem_inc(self.sem, start)
        book.counts.append(self)

    def mark(self, instruction):
        instruction.then_inc(self.sem, self.step)
        self.value += self.step
        return self.now()

    def now(self):
        loop = self.book.loop
        if loop is None:
            return (self, None, self.value)
        return (self, loop, self.value - loop.first[self.name])


class Loop:

    def __init__(self, first, gains, names):
        self.first, self.gains, self.names = first, gains, names
        self.new_names = {}
        self.i = None

    def name(self, key, token):
        self.new_names[key] = (token[0].name, token[2])

    def before(self, counts, key):
        name, at = self.names.get(key, (counts[0].name, 0))
        count = [c for c in counts if c.name == name][0]
        return (count, self, at - self.gains.get(name, 0))


class Peeled:

    def __init__(self, loop):
        self.loop = loop

    def name(self, key, token):
        pass

    def before(self, counts, key):
        name, at = self.loop.new_names.get(key, (counts[0].name, 0))
        return ([c for c in counts if c.name == name][0], self.loop, at)


class Book:

    def __init__(self, nc, ctx, known):
        self.nc, self.ctx, self.known = nc, ctx, known
        self.counts, self.loop, self.learned = [], None, []

    def value(self, token):
        count, loop, at = token
        if loop is None:
            return at
        first, gain = loop.first[count.name], loop.gains.get(count.name, 0)
        if loop is self.loop:
            return first + at + loop.i * gain if gain else first + at
        return first + at + (loop.n - 1) * gain

    def run(self, n, body):
        k = len(self.learned)
        self.learned.append(None)
        gains, names = self.known[k] if self.known else ({}, {})
        loop = Loop({c.name: c.value for c in self.counts}, gains, names)
        loop.n = n
        with self.nc.Fori(0, n) as i:
            self.loop, loop.i = loop, i
            for c in self.counts:
                c.seen_loop = {}
            body(i, loop)
            self.loop = None
        for c in self.counts:
            c.seen_loop = {}
            gained = c.value - loop.first[c.name]
            if gained:
                self.learned[k] = self.learned[k] or ({}, {})
                self.learned[k][0][c.name] = gained
            c.value = loop.first[c.name] + gained * n
        self.learned[k] = (self.learned[k][0], loop.new_names)
        return loop


class Queue(Count):

    def __init__(self, book, name, engine, serial):
        super().__init__(book, name, 1)
        self.engine, self.serial = engine, serial
        self.seen, self.seen_loop = {}, {}
        engine.sem_inc(self.sem, FIRST_COUNT)
        self.value = FIRST_COUNT

    def wait(self, *tokens):
        for token in tokens:
            if token is None:
                continue
            count, loop, at = token
            if loop is None or loop is not self.book.loop:
                at = self.book.value(token)
                if self.seen.get(count.name, -1) >= at:
                    continue
                self.seen[count.name] = at
            else:
                if self.seen_loop.get(count.name, -10**9) >= at:
                    continue
                self.seen_loop[count.name] = at
            self.engine.wait_ge(count.sem, self.book.value(token))

    def do(self, make, *after, mark=True, serial=None):
        if self.serial if serial is None else serial:
            self.wait(self.now())
        self.wait(*after)
        instruction = make()
        return self.mark(instruction) if mark else None


class Kernel:
    def __init__(self, nc, ctx, io, known):
        self.nc, self.ctx, self.io = nc, ctx, io
        self.book = Book(nc, ctx, known)
        book = self.book
        self.pe = Queue(book, "pe", nc.tensor, False)
        self.act = Queue(book, "act", nc.scalar, True)
        self.dve = Queue(book, "dve", nc.vector, True)
        self.pool = Queue(book, "pool", nc.gpsimd, True)
        self.sp = Queue(book, "sp", nc.sync, False)
        self.engines = (self.pe, self.act, self.dve, self.pool)
        self.raw_full = [Count(book, f"raw_full{s}", 16) for s in range(RAW_SLOTS)]
        self.raw_free = [Count(book, f"raw_free{s}", 1, 1) for s in range(RAW_SLOTS)]
        self.split_free = [Count(book, f"split_free{s}", 1, 1) for s in range(SPLIT_SLOTS)]
        self.raw_turn = self.split_turn = 0
        self.carried = None
        self.load_done = Count(book, "load_done", 16)
        self.store_done = Count(book, "store_done", 16)
        self.bank = [self.psum(f"bank{b}", [P, S]) for b in range(8)]
        self.free = [None] * 8

    def sb(self, name, shape, dtype=F32, ctx=None):
        return (ctx or self.ctx).enter_context(self.nc.sbuf_tensor(name, shape, dtype))

    def psum(self, name, shape, dtype=F32):
        return self.ctx.enter_context(self.nc.psum_tensor(name, shape, dtype))

    def mm(self, out, lhsT, rhs, start, stop, *after, mark=False):
        return self.pe.do(lambda: self.nc.tensor.matmul(out, lhsT, rhs, start=start, stop=stop,
                                                        skip_group_check=True), *after, mark=mark)

    def transpose(self, out, in_, *after, mark=False):
        return self.pe.do(lambda: self.nc.tensor.transpose(out, in_, self.ident[:]), *after, mark=mark)

    def tt(self, q, out, a, b, op, *after, **kw):
        return q.do(lambda: q.engine.tensor_tensor(out, a, b, op), *after, **kw)

    def ts(self, q, out, a, s1, s2, op0, op1=None, *after, **kw):
        if op1 is None:
            return q.do(lambda: q.engine.tensor_scalar(out, a, s1, None, op0), *after, **kw)
        return q.do(lambda: q.engine.tensor_scalar(out, a, s1, s2, op0, op1), *after, **kw)

    def stt(self, out, a, s, b, op0, op1, *after, **kw):
        return self.dve.do(lambda: self.nc.vector.scalar_tensor_tensor(out, a, s, b, op0, op1), *after, **kw)

    def copy(self, q, out, a, *after, **kw):
        if q is self.act:
            return q.do(lambda: self.nc.scalar.copy(out, a), *after, **kw)
        return q.do(lambda: q.engine.tensor_copy(out, a), *after, **kw)

    def fn(self, out, a, func, bias=0.0, scale=1.0, *after, **kw):
        return self.act.do(lambda: self.nc.scalar.activation(out, a, func, bias=bias, scale=scale), *after, **kw)

    def together(self):
        for q in self.engines:
            q.wait(*[o.now() for o in self.engines if o is not q])

    def load(self, *pieces):
        s = self.raw_turn
        self.raw_turn = (s + 1) % RAW_SLOTS
        self.sp.wait(self.raw_free[s].now())
        self.nc.sync.sem_inc(self.sp.sem, 1)
        self.sp.value += 1
        for p0, at, k, source in pieces:
            rows = slice(p0, p0 + source.shape[0])
            if k is None:
                dst = self.raw[rows, s, at:at + source.shape[1]]
            else:
                dst = self.raw[rows, s, at:at + k * P].rearrange("p (k n) -> p k n", k=k)
            full = self.raw_full[s].mark(self.nc.sync.dma_start(dst, source))
        return s, full

    def load_wide(self, source):
        s = self.raw_turn
        self.raw_turn = (s + 1) % RAW_SLOTS
        self.sp.wait(self.raw_free[s].now())
        self.nc.sync.sem_inc(self.sp.sem, 1)
        self.sp.value += 1
        dst = self.raw[:, s, 0:2 * S].rearrange("p (k n) -> p k n", k=2)
        return s, self.raw_full[s].mark(self.nc.sync.dma_start(dst, source))

    def unit(self, source, k):
        s, full = self.load((0, 0, k, source))
        b = self.split_turn
        self.split_turn = (b + 1) % SPLIT_SLOTS
        raw = self.raw[:, s, 0:k * P]
        high, low = self.w_high[:, b, 0:k * P], self.w_low[:, b, 0:k * P]
        rounded = self.act.do(lambda: self.nc.scalar.copy(high, raw), full, self.split_free[b].now(), serial=False)
        self.pool.wait(rounded)
        ready = self.raw_free[s].mark(self.nc.gpsimd.tensor_tensor(low, raw, high.bitcast(F32), ALU.subtract))
        return b, k, ready, s

    def each(self, n, sources, step, then=None):
        unit = self.carried or self.unit(*sources(0)[0])
        b, k, _, s = unit
        assert len(sources(0)) % SPLIT_SLOTS == 0

        def iteration(i, loop, unit, following):
            coming = [*sources(i)[1:], following]
            units = [unit]

            def take():
                source = coming.pop(0)
                if not coming and following is not None:
                    self.raw_turn, self.split_turn = s, b
                units.append(source and self.unit(*source))
                return units[-2]

            step(i, lambda key: loop.before(self.book.counts, key), loop.name, take)
            assert not coming
            self.carried = units[-1]

        loop = self.book.run(n - 1, lambda i, loop: iteration(i, loop, (b, k, (self.raw_free[s], loop, 0), s),
                                                              sources(i + 1)[0]))
        self.before_last = self.dve.now()
        iteration(n - 1, Peeled(loop), (b, k, self.raw_free[s].now(), s), then)

    def product(self, bank, unit, x_high, x_low, start, stop, *after, needs=lambda k: ()):
        b, n, ready, _ = unit
        for k in range(n):
            self.pe.wait(*needs(k))
            high, low = self.w_high[:, b, k * P:(k + 1) * P], self.w_low[:, b, k * P:(k + 1) * P]
            self.mm(bank, high, x_high(k), start and k == 0, False, ready, *after)
            self.mm(bank, high, x_low(k), False, False)
            last = k == n - 1
            ins = self.nc.tensor.matmul(bank, low, x_high(k), start=False, stop=stop and last, skip_group_check=True)
        return self.split_free[b].mark(ins)

    def product_steps(self, bank, unit, x_high, x_low, out, *after, needs=lambda k: ()):
        b, n, ready, _ = unit
        for k in range(n):
            self.pe.wait(*needs(k))
            high, low = self.w_high[:, b, k * P:(k + 1) * P], self.w_low[:, b, k * P:(k + 1) * P]
            self.mm(bank, high, x_high(k), k == 0, False, ready, *after)
            self.mm(bank, high, x_low(k), False, False)
            ins = self.nc.tensor.matmul(bank, low, x_high(k), start=False, stop=k == n - 1, skip_group_check=True)
            if k % 2 and k < n - 1:
                yield
        out.append(self.split_free[b].mark(ins))

    def split(self, high, low, src, *after):
        self.copy(self.dve, high, src, *after)
        return self.tt(self.dve, low, src, high.bitcast(F32), ALU.subtract)

    def h_need(self, k):
        return self.h_ready[k]

    def h_parts(self):
        return (lambda k: self.h_high[:, k, :]), (lambda k: self.h_low[:, k, :])

    def first(self, weight, at=0):
        return weight.rearrange("(k p) n -> p k n", p=P)[:, :, at:at + P], weight.shape[0] // P

    def constants(self):
        nc, pool = self.nc, self.pool
        g = nc.gpsimd

        def band(t, compare, base, pattern, cm, fill):
            pool.do(lambda: g.affine_select(out=t, in_=t, pattern=pattern, compare_op=compare,
                                            fill=fill, base=base, channel_multiplier=cm))

        def fill(t, v):
            return pool.do(lambda: g.memset(t, v))

        self.band, self.fill_with = band, fill
        fill(self.ident[:], 0.0)
        band(self.ident[:], ALU.not_equal, 0, [[-1, P]], 1, 1.0)
        pool.do(lambda: g.tensor_copy(self.ident_bf[:], self.ident[:]))
        fill(self.ones[:], 1.0)
        self.same_block(self.head_ones[:], HEAD, 1.0)

    def same_block(self, t, size, value, outside=0.0, clear=True):
        if clear:
            self.fill_with(t, value)
        n = P // size
        v = t.rearrange("p (b c) -> p b c", b=n)
        self.band(v, ALU.is_ge, 0, [[-size, n], [0, size]], 1, outside)
        return self.band(v, ALU.is_ge, size - 1, [[size, n], [0, size]], -1, outside)

    def vectors(self, scope):
        io = self.io
        plan = [("norm1_w", 8), ("b_ada", 48), ("norm2_w", 8), ("b_gate", 16), ("norm_f_w", 8), ("c", 8), None,
                ("mu_shift", 24), ("w0", 8), ("a0", 8), ("k_k", 8), ("k_a", 8), ("r_k", 8), ("lnx_w", 8), ("lnx_b", 8), ("mu_low", 3), None,
                ("conv_w0", 44), ("conv_w1", 44), None, ("conv_w2", 44), ("conv_b", 44), ("norm_mix_2", 16), ("norm_ffn_2", 16), None,
                ("conv_ffn_2", 66), ("b_conv_ffn_2", 22), ("final_norm_2", 8), ("sgu_norm_2", 8), ("conv_a_2", 12), ("pool_scale_2", 4), None,
                ("conv_ffn_2b", 66), ("b_conv_ffn_2b", 22)]
        groups = 1 + plan.count(None)
        assert groups == VEC_GROUPS
        rows = self.sb("vec_rows", [P, groups, P], F32, scope)
        self.sp.wait(self.fill_with(rows[:], 0.0))

        def src(name):
            if name.startswith("conv_w"):
                return io["conv_w"][0, int(name[6])].rearrange("(n p) -> n p", p=P)
            if name == "mu_shift":
                return io["mu_shift"][0, 0:3 * D].rearrange("(n p) -> n p", p=P)
            if name.startswith("conv_ffn_2"):
                return io["conv_ffn_2"][1 if name.endswith("b") else 0].rearrange("j (n p) -> (j n) p", p=P)
            if name.startswith("b_conv_ffn_2"):
                return io["b_conv_ffn_2"][1 if name.endswith("b") else 0].rearrange("(n p) -> n p", p=P)
            if name == "conv_a_2":
                return io[name][0].rearrange("j (n p) -> (j n) p", p=P)
            if name == "r_k":
                return io[name].rearrange("a (n h) e -> (a n) (h e)", h=2)
            a = io[name]
            if len(a.shape) == 1:
                return a.rearrange("(n p) -> n p", p=P)
            return a.rearrange("a (n p) -> (a n) p", p=P)

        self.at = {}
        g, row, last = 0, 0, None
        for entry in plan:
            if entry is None:
                g, row = g + 1, 0
                continue
            name, n = entry
            self.at[name] = g * P + row
            if name == "mu_low":
                m = io["mu_shift"]
                parts = [(row, P, m[0:1, 3 * D:3 * D + P]), (row + 1, P, m[0:1, 3 * D + P:3 * D + 2 * P]),
                         (row + 2, P, m[0:1, RWKV_IN - P:RWKV_IN])]
                for r, w, s in parts:
                    last = self.load_done.mark(self.nc.sync.dma_start(rows[r:r + 1, g, 0:w], s))
            else:
                last = self.load_done.mark(self.nc.sync.dma_start(rows[row:row + n, g, :], src(name)))
            row += n
            assert row <= P
        for g in range(groups):
            b = g // 4
            t = self.transpose(self.bank[b][:, (g % 4) * P:(g % 4 + 1) * P], rows[:, g, :],
                               last, self.pool.now(), self.free[b], mark=True)
        for b in range((groups + 3) // 4):
            w = min(4, groups - 4 * b) * P
            self.free[b] = self.copy(self.dve, self.vec[:, b * 4 * P:b * 4 * P + w], self.bank[b][:, 0:w], t)
        self.vec_ready = self.dve.now()

    def col(self, name, i):
        return self.vec[:, self.at[name] + i:self.at[name] + i + 1]

    def cols(self, name, n, i=0):
        return self.vec[:, self.at[name] + i:self.at[name] + i + n]

    def load_x(self, scope):
        xrow = self.sb("x_rows", [P, 4, D], F32, scope)
        return xrow, self.load_x_done.mark(self.nc.sync.dma_start(
            xrow[:], self.io["x"][0].rearrange("(t p) d -> p t d", p=P)))

    def turn_x(self, xrow, full):
        for f in range(DT):
            b = 2 + f % 4
            for t in range(4):
                done = self.transpose(self.bank[b][:, t * P:(t + 1) * P], xrow[:, t, f * P:(f + 1) * P],
                                      full, self.pool.now(), self.free[b], mark=t == 3)
            self.free[b] = self.copy(self.dve if f % 2 else self.act, self.x[:, f, :], self.bank[b][:], done)

    def ada_column(self, source, bank, *after):
        s, full = self.load((0, 0, DT, source))
        for k in range(DT):
            self.pe.wait(full, *after)
            ins = self.nc.tensor.matmul(bank, self.raw[:, s, k * P:(k + 1) * P], self.col("c", k),
                                        start=k == 0, stop=k == DT - 1, skip_group_check=True)
        return self.raw_free[s].mark(ins)

    def ada(self):
        w = self.io["w_ada"][0].rearrange("(k p) n -> p k n", p=P)
        b_ada = self.cols("b_ada", 6 * DT)
        self.pe.wait(self.vec_ready)
        self.together()

        def body(i, loop):
            self.pe.wait((self.dve, loop, 0))
            for half in range(DT // 2):
                slot, full = self.load_wide(w[:, 2 * half:2 * half + 2, bass.ds(i * S, S)])
                for k in range(2):
                    self.pe.wait(full)
                    ins = self.nc.tensor.matmul(self.bank[1][0:1, :], self.col("c", 2 * half + k),
                                                self.raw[:, slot, k * S:(k + 1) * S], start=half == 0 and k == 0,
                                                stop=half == DT // 2 - 1 and k == 1, skip_group_check=True)
                t = self.raw_free[slot].mark(ins)
            e = self.copy(self.dve, self.sq[0:1, 1, :], self.bank[1][0:1, :], t)
            for u in range(4):
                t = self.mm(self.bank[0][:, u:u + 1], self.sq[0:1, 1, u * P:(u + 1) * P], self.ones[0:1, 0:1], u == 0, u == 3,
                            e, mark=u == 3)
            self.tt(self.dve, self.mod[:, bass.ds(4 * i, 4)], self.bank[0][:, 0:4], b_ada[:, bass.ds(4 * i, 4)], ALU.add, t)

        self.book.run(2 * D // S, body)
        self.stt(self.gain1[:], self.mod[:, DT:2 * DT], 1.0, self.cols("norm1_w", DT), ALU.add, ALU.mult)

    def sqrt_inverse(self, t):
        self.fn(t, t, ACT.Ln, 0.0, 1.0, self.dve.now())
        return self.fn(t, t, ACT.Exp, 0.0, -0.5)

    def inverse_rms(self, src, eps, tiles=DT, ready=None):
        m = [None, None]
        for k in range(tiles):
            t = self.fn(self.sq[:, k % 2, :], src[:, k, :], ACT.Square, 0.0, 1.0,
                        ready[k] if ready else self.dve.now(), m[k % 2])
            m[k % 2] = self.mm(self.bank[7][:], self.ones[:], self.sq[:, k % 2, :], k == 0, k == tiles - 1, t,
                               self.free[7], mark=True)
        e = self.ts(self.dve, self.rinv[:], self.bank[7][:], 1.0 / (tiles * P), eps, ALU.mult, ALU.add, m[1])
        self.free[7] = e
        return self.sqrt_inverse(self.rinv[:])

    def norm(self, src, gain, shift=None, keep=False, summed=True, ready=None, factor=None):
        dve, act, pool = self.dve, self.act, self.pool
        if factor is not None:
            r = factor
        elif summed:
            m = self.mm(self.bank[7][:], self.ones[:], self.rinv[:], True, True, dve.now(), self.free[7], mark=True)
            self.free[7] = self.ts(dve, self.rinv[:], self.bank[7][:], 1.0 / D, RMS_EPS, ALU.mult, ALU.add, m)
            self.norm_begun = self.free[7]
            r = self.sqrt_inverse(self.rinv[:])
        else:
            r = self.inverse_rms(src, RMS_EPS, DT, ready)
        if keep:
            return [self.stt(src[:, k, :], src[:, k, :], gain(k), self.rinv[:], ALU.mult, ALU.mult, r) for k in range(DT)]
        self.h_ready, rounded, taken = [], [None] * DT, [None, None]

        def rest(k):
            q = (dve, pool)[k % 2]
            low = self.tt(q, self.h_low[:, k, :], self.sq[:, k % 2, :], self.h_high[:, k, :].bitcast(F32), ALU.subtract,
                          rounded[k])
            taken[k % 2] = low
            self.h_ready.append((rounded[k], low))

        for k in range(DT):
            t = self.sq[:, k % 2, :]
            e = self.stt(t, src[:, k, :], gain(k), self.rinv[:], ALU.mult, ALU.mult, r, taken[k % 2])
            if shift is not None:
                e = self.ts(dve, t, t, shift(k), None, ALU.add)
            rounded[k] = self.copy(act, self.h_high[:, k, :], t, e)
            if k:
                rest(k - 1)
        rest(DT - 1)

    def attention(self):
        with ExitStack() as ctx:
            sb = lambda name, shape, dtype=F32: self.sb(name, shape, dtype, ctx)
            self.masks = masks = sb("att_masks", [P, 4, S], BF16)
            self.coming = sb("att_coming", [P, 3, 3, S])
            self.qk = sb("att_qk", [P, 3, 2, S])
            self.v_tok = sb("att_v_tok", [P, 3, 4, 3, HEAD])
            self.prob = sb("att_prob", [P, 4, S])
            self.prob_t = sb("att_prob_t", [P, 4, S])
            self.top = sb("att_top", [P, 12])
            self.neg = sb("att_neg", [P, 12])
            self.diag = sb("att_diag", [P, 2, P])
            self.join = sb("att_join", [P, S])
            self.factor = sb("att_factor", [P, S])
            self.total = sb("att_total", [P, S])
            self.inv_den = sb("att_inv", [P, S])
            self.fill_with(masks[:], 0.0)
            self.fill_with(masks[:, 0, 0:P], MASKED)
            OWN, PREVIOUS = True, False
            for bank, part, kind in ((0, 1, OWN), (0, 2, PREVIOUS), (0, 3, OWN),
                                     (1, 0, PREVIOUS), (1, 1, OWN), (1, 2, PREVIOUS), (1, 3, OWN),
                                     *((b, part, OWN) for b in (2, 3) for part in range(4))):
                t = masks[:, bank, part * P:(part + 1) * P]
                if kind == OWN:
                    self.band(t, ALU.is_ge, 0, [[-1, P]], 1, MASKED)
                else:
                    self.band(t, ALU.is_ge, 0, [[1, P]], -1, MASKED)
                if bank == 3:
                    self.same_block(t, S // DILATIONS[2], 0.0, MASKED, clear=False)
            self.fill_with(self.v_tok[:, :, :, 1, :], 1.0)
            rms = self.inverse_rms(self.x, RMS_EPS)
            self.ada()
            self.carried = self.unit(*self.first(self.io["w_in"][0]))
            self.together()
            self.norm(self.x, lambda k: self.gain1[:, k:k + 1], lambda k: self.mod[:, k:k + 1], factor=rms)
            run(self.att_project(0))
            self.att_arrive()

            def body(i, loop):
                self.drain(loop)
                interleave(self.att_mix(i), self.att_project(i + 1, i), 5, 4)
                self.att_arrive()

            self.book.run(PAIRS_ATT - 1, body)
            def beside():
                yield from self.rwkv_low_ranks()
                yield from self.ada_rest(PAIRS_ATT - 1)

            interleave(self.att_mix(PAIRS_ATT - 1), beside(), 2, 1)
            self.stt(self.gain2[:], self.mod[:, 4 * DT:5 * DT], 1.0, self.cols("norm2_w", DT), ALU.add, ALU.mult)
            self.together()

    def drain(self, loop):
        self.pe.wait((self.act, loop, 0), (self.dve, loop, 0))
        self.act.wait((self.dve, loop, 0))
        self.dve.wait((self.act, loop, 0))
        self.free = [None] * 8

    def ada_rest(self, first):
        w = self.io["w_ada"][0].rearrange("(k p) n -> p k n", p=P)
        for n in range(2 * DT + ADA_PER_PAIR * first, 6 * DT):
            b = 6 + n % 2
            t = self.ada_column(w[:, :, n * P:(n + 1) * P], self.bank[b][:, 0:1], self.free[b])
            self.free[b] = self.tt(self.dve, self.mod[:, n:n + 1], self.bank[b][:, 0:1], self.cols("b_ada", 1, n), ALU.add, t)
            yield

    def att_project(self, pair, step=None):
        io = self.io
        w = io["w_in"][0].rearrange("(k p) n -> p k n", p=P)
        wa = io["w_ada"][0].rearrange("(k p) n -> p k n", p=P)
        source = lambda n: w[:, :, bass.ds(pair * P + n * ATT_WIDTH, P)]
        units, turn, self.carried = [self.carried or self.unit(source(0), DT)], 0, None
        for n in range(9):
            g, j = n // 3, n % 3
            if n < 8:
                units.append(self.unit(source(n + 1), DT))
            b, done = 6 + turn % 2, []
            turn += 1
            yield from self.product_steps(self.bank[b][:], units[n], *self.h_parts(), done, self.free[b], needs=self.h_need)
            out = self.coming[:, g, j, :].rearrange("p (r i) -> p r i", r=DILATIONS[g])
            self.free[b] = self.copy(self.act if n % 3 == 2 else self.dve, out, in_order(self.bank[b][:], g), done[0])
            yield
            for a in range(ADA_PER_PRODUCT if step is not None and n < 8 else 0):
                b = 6 + turn % 2
                turn += 1
                at = step * ADA_PER_PAIR + (2 * DT + n * ADA_PER_PRODUCT + a)
                t = self.ada_column(wa[:, :, bass.ds(at * P, P)], self.bank[b][:, 0:1], self.free[b])
                self.free[b] = self.tt(self.dve, self.mod[:, bass.ds(at, 1)], self.bank[b][:, 0:1],
                                       self.cols("b_ada", 6 * DT)[:, bass.ds(at, 1)], ALU.add, t)
                yield

    def att_arrive(self):
        act, dve = self.act, self.dve
        done = (act.now(), dve.now())
        for g in range(3):
            for n in range(4):
                t = self.transpose(self.bank[g][:, n * P:(n + 1) * P], self.coming[:, g, 2, n * P:(n + 1) * P],
                                   *done, mark=n == 3)
            q = act if g == 1 else dve
            self.copy(q, self.qk[:, g, :, :], self.coming[:, g, 0:2, :], *done)
            self.free[g] = self.copy(q, self.v_tok[:, g, :, 0::2, :],
                                     self.bank[g][:].rearrange("p (n h e) -> p n h e", n=4, h=2), t)
        self.pe.wait(act.now(), dve.now())

    def att_mix(self, i):
        nc, act, dve = self.nc, self.act, self.dve
        qk, prob, prob_t, v_tok, top, neg = self.qk, self.prob, self.prob_t, self.v_tok, self.top, self.neg
        join, factor, total = self.join[:], self.factor[:], self.total[:]
        cells = [[None, (0, 0, 0), (0, 1, 0), (0, 1, 1)], [(0, 2, 1), (0, 2, 2), (0, 3, 2), (0, 3, 3)],
                 [(1, n, n) for n in range(4)], [(2, n, n) for n in range(4)]]
        per = [0, 1, P * DILATIONS[2] // S]

        def block(bank, g, n):
            if g == 0:
                return bank[:, n * P:(n + 1) * P]
            return in_order(bank[:], g)[:, n * per[g]:(n + 1) * per[g], :]

        def like(ap, g):
            return ap if g == 0 else ap.rearrange("p (r i) -> p r i", r=per[g])

        for h in range(2):
            rows = slice(HEAD * h, HEAD * (h + 1))
            exps = []
            for c in range(4):
                self.mm(self.bank[c][:], self.ident_bf[:], self.masks[:, c, :], True, False, self.free[c])
                for n, cell in enumerate(cells[c]):
                    if cell is None:
                        continue
                    g, qn, kn = cell
                    t = self.mm(self.bank[c][:, n * P:(n + 1) * P], qk[rows, g, 0, qn * P:(qn + 1) * P],
                                qk[rows, g, 1, kn * P:(kn + 1) * P], False, n == 3, mark=n == 3)
                width = 2 if c < 2 else 1
                m, at = 4 // width, (0, 2, 4, 8)[c]
                dve.do(lambda: nc.vector.tensor_reduce(
                    top[:, at:at + m], self.bank[c][:].rearrange("p (m k) -> p m k", m=m), AX.X, ALU.max), t)
                e = self.ts(dve, neg[:, at:at + m], top[:, at:at + m], -HEAD ** -0.5, None, ALU.mult)
                yield
                for r in range(m):
                    part = slice(r * width * P, (r + 1) * width * P)
                    e2 = self.fn(prob[:, c, part], self.bank[c][:, part], ACT.Exp,
                                 neg[:, at + r:at + r + 1], HEAD ** -0.5, e, serial=r == 0)
                self.free[c] = e2
                exps.append(e2)
                yield
            for c in range(4):
                b = 4 + c % 2
                for n in range(4):
                    if cells[c][n] is None:
                        continue
                    t = self.transpose(self.bank[b][:, n * P:(n + 1) * P], prob[:, c, n * P:(n + 1) * P],
                                       exps[c], self.free[b], mark=n == 3)
                first = P if c == 0 else 0
                ready = self.free[b] = self.copy(dve, prob_t[:, c, first:], self.bank[b][:, first:], t)
                yield
            spread = [None, None]
            for g in range(3):
                b = 3 + g
                for n in range(4):
                    d = self.ts(dve, self.diag[:, n % 2, :], self.ident[:], top[:, 4 * g + n:4 * g + n + 1], None,
                                ALU.mult, None, spread[n % 2])
                    spread[n % 2] = self.mm(block(self.bank[b], g, n), self.ones[:], like(self.diag[:, n % 2, :], g),
                                            n == 0, n == 3, d, self.free[b], mark=True)
                    if n % 2:
                        yield
            maxima = spread[1]
            nums = []
            for g in range(3):
                todo = [(c, n, cell) for c in range(4) for n, cell in enumerate(cells[c])
                        if cell is not None and cell[0] == g]
                for m, (c, n, (_, qn, kn)) in enumerate(todo):
                    lhs = v_tok[:, g, kn, h:h + 2, :].rearrange("p a e -> p (a e)")
                    t = self.mm(block(self.bank[g], g, qn), lhs, like(prob_t[:, c, n * P:(n + 1) * P], g),
                                m == 0, m == len(todo) - 1, ready, self.free[g], mark=m == len(todo) - 1)
                nums.append(t)
                if g == 0:
                    e = self.copy(act, join, self.bank[3][:], maxima, dve.now())
                    self.tt(dve, join, join, self.bank[4][:], ALU.max, e)
                    self.tt(dve, join, join, self.bank[5][:], ALU.max)
                yield
            for g in range(3):
                e = self.tt(dve, factor, self.bank[3 + g][:], join, ALU.subtract)
                self.free[3 + g] = e
                e = self.fn(factor, factor, ACT.Exp, 0.0, HEAD ** -0.5, e)
                out = total if g == 0 else factor
                self.free[g] = self.tt(dve, out, self.bank[g][:], factor, ALU.mult, e, nums[g])
                if g:
                    self.tt(dve, total, total, factor, ALU.add)
                yield
            other = slice(HEAD * (1 - h), HEAD * (2 - h))
            dve.do(lambda: nc.vector.reciprocal(self.inv_den[rows, :], total[other, :]))
            self.tt(dve, tile_at(self.att[rows], i), total[rows, :], self.inv_den[rows, :], ALU.mult)
            yield

    def rwkv_constants(self, ctx):
        dve, pool = self.dve, self.pool
        R = self.rw = Scratch()
        sb = lambda name, shape, dtype=F32: self.sb(name, shape, dtype, ctx)
        R.mask4 = sb("rw_mask4", [P, 4, P])
        R.mask2 = sb("rw_mask2", [P, 2, P])
        R.restart = sb("rw_restart", [P, S], BF16)
        R.low = sb("rw_low", [P, S])
        R.low_g = sb("rw_low_g", [P, 2, S])
        R.keep_mu = sb("rw_keep_mu", [P, 3 * DT + 3])
        R.keep_a = sb("rw_keep_a", [P, DT])
        mask4, mask2 = R.mask4, R.mask2
        strict_upper = lambda t: self.band(t, ALU.is_gt, 0, [[1, P]], -1, 0.0)
        self.same_block(mask4[:, 0, :], SUB, 1.0)
        strict_upper(mask4[:, 0, :])
        for j in (1, 3):
            self.same_block(mask4[:, j, :], CHUNK, 1.0)
            self.band(mask4[:, j, :], ALU.is_ge, 0, [[1, P]], -1, 0.0)
        self.same_block(mask4[:, 2, :], CHUNK, 1.0)
        strict_upper(mask4[:, 2, :])
        for j, size in ((0, SUB), (1, CHUNK)):
            self.same_block(mask2[:, j, :], size, 1.0)
            self.band(mask2[:, j, :], ALU.is_gt, 0, [[-1, P]], 1, 0.0)
        self.tt(pool, mask2[:, 1, :], mask2[:, 1, :], mask2[:, 0, :], ALU.subtract)
        self.fill_with(R.restart[:], 1.0)
        self.fill_with(R.restart[:].rearrange("p (c t) -> p c t", t=CHUNK)[:, :, 0:1], 0.0)
        for name, n, at in (("mu_shift", 3 * DT, 0), ("mu_low", 3, 3 * DT)):
            self.ts(dve, R.keep_mu[:, at:at + n], self.cols(name, n), -1.0, 1.0, ALU.mult, ALU.add)
        self.ts(dve, R.keep_a[:], self.cols("k_a", DT), -1.0, 1.0, ALU.mult, ALU.add)

    def rwkv_low_ranks(self):
        R = self.rw
        units = [self.unit(*self.first(self.io["w_in"][0], LOW_RANK_COLUMNS[0]))]
        for n in range(3):
            if n < 2:
                units.append(self.unit(*self.first(self.io["w_in"][0], LOW_RANK_COLUMNS[n + 1])))
            b, done = 6 + n % 2, []
            yield from self.product_steps(self.bank[b][:], units[n], *self.h_parts(), done, self.free[b])
            out = R.low[:] if n == 0 else R.low_g[:, n - 1, :]
            self.free[b] = self.shift_mix(out, self.bank[b][:], self.col("mu_low", n),
                                          R.keep_mu[:, 3 * DT + n:3 * DT + n + 1], done[0])
            yield
        self.fn(R.low_g[:], R.low_g[:], ACT.Sigmoid, 0.0, 1.0, self.dve.now())
        self.fn(R.low[0:LOW, :], R.low[0:LOW, :], ACT.Tanh)

    def rwkv(self):
        dve, pool = self.dve, self.pool
        w = self.io["w_in"][0].rearrange("(k p) n -> p k n", p=P)
        with ExitStack() as ctx:
            sb = lambda name, shape, dtype=F32: self.sb(name, shape, dtype, ctx)
            R = self.rw
            R.bias = sb("rw_bias", [P, 2])
            names = ["r", "k", "v", "t0", "sum", "lw", "rate", "kk", "e1", "gate", "gate_next"]
            tiles = sb("rw_tiles", [P, len(names), S])
            R.tile = {n: tiles[:, j, :] for j, n in enumerate(names)}
            R.ar = sb("rw_ar", [P, 4, 2, P])
            R.bt = sb("rw_b", [P, S])
            R.kt = sb("rw_k", [P, S])
            R.b_tok = sb("rw_b_tok", [P, 4, P])
            R.k_tok = sb("rw_k_tok", [P, 4, P])
            R.v_tok = sb("rw_v_tok", [P, 4, P])
            R.keep = sb("rw_keep", [P, 8, 4, P])
            R.de = sb("rw_de", [P, 4, 2, P])
            R.pw = sb("rw_pw", [P, 4, 2, P])
            R.pq = sb("rw_pq", [P, 4, 2, P])
            R.inv = sb("rw_inv", [P, 4, 2, P])
            R.ends = sb("rw_ends", [P, S // CHUNK])
            R.x_tok, R.u_tok = self.rinv[:, 0:P], self.rinv[:, P:2 * P]
            R.state = self.rinv[:, 2 * P:4 * P].rearrange("p (a n) -> p a n", a=2)
            R.y, R.y2 = self.sq[:, 0, :], self.sq[:, 1, :]
            self.fill_with(R.state, 0.0)
            self.together()
            run(self.rw_front(0))
            run(self.rw_front_rest(0, self.rw_unit(0, IN_R)))
            self.rw_arrive(0)
            self.rw_first_half(iter(()), self.rw_front(1))

            def body(i, loop):
                self.drain(loop)
                self.rw_second_half(i, self.rw_front_rest(i + 1, self.rw_unit(i + 1, IN_R)))
                self.rw_arrive(i + 1)
                self.rw_first_half(self.rw_close(i), self.rw_front(i + 2))

            self.book.run(DT - 2, body)
            self.rw_second_half(DT - 2, self.rw_front_rest(DT - 1, self.rw_unit(DT - 1, IN_R)))
            self.rw_arrive(DT - 1)
            self.rw_first_half(self.rw_close(DT - 2), iter(()))
            self.rw_second_half(DT - 1, iter(()))
            self.carried = self.unit(*self.first(self.io["w_in"][0], GATE0))
            run(self.rw_close(DT - 1))
            self.together()

    def shift_mix(self, out, z, mu, keep, *after):
        self.ts(self.dve, out, z, keep, None, ALU.mult, None, *after)
        return self.stt(out[:, 1:S], z[:, 0:S - 1], mu, out[:, 1:S], ALU.mult, ALU.add)

    def rw_front(self, i):
        nc, act, dve, R = self.nc, self.act, self.dve, self.rw
        w = self.io["w_in"][0].rearrange("(k p) n -> p k n", p=P)
        w2, a2, g2 = (self.io[n][0] for n in ("w2", "a2", "g2"))
        T = R.tile
        col = lambda name, j=0: self.cols(name, DT, j * DT)[:, bass.ds(i, 1)]
        cols, raw = bass.ds(i * P, P), self.raw
        self.copy(dve, R.bias[:, 0:1], col("w0"))
        biases = self.copy(dve, R.bias[:, 1:2], col("a0"))
        slot, full = self.load((0, 0, None, w2[:, cols]), (LOW, 0, None, a2[:, cols]))
        unit = self.rw_unit(i, IN_K)
        td = self.mm(self.bank[5][:], raw[0:LOW, slot, 0:P], R.low[0:LOW, :], True, True, full, self.free[5], mark=True)
        self.pe.wait(self.free[6])
        ins = nc.tensor.matmul(self.bank[6][:], raw[LOW:2 * LOW, slot, 0:P], R.low[LOW:2 * LOW, :],
                               start=True, stop=True, skip_group_check=True)
        ta = self.raw_free[slot].mark(ins)
        self.free[5] = self.fn(T["lw"], self.bank[5][:], ACT.Sigmoid, R.bias[:, 0:1], 1.0, td, biases)
        self.free[6] = self.fn(T["rate"], self.bank[6][:], ACT.Sigmoid, R.bias[:, 1:2], 1.0, ta)
        yield
        yield from self.rw_projected(i, IN_K, unit, 7, T["k"])

    def rw_unit(self, i, j):
        w = self.io["w_in"][0].rearrange("(k p) n -> p k n", p=P)
        return self.unit(w[:, :, bass.ds(i * P + (ATT_IN + j * D), P)], DT)

    def rw_projected(self, i, j, unit, bank, out):
        done = []
        yield from self.product_steps(self.bank[bank][:], unit, *self.h_parts(), done, self.free[bank])
        mu, keep = self.cols("mu_shift", DT, j * DT), self.rw.keep_mu[:, j * DT:(j + 1) * DT]
        self.free[bank] = self.shift_mix(out, self.bank[bank][:], mu[:, bass.ds(i, 1)], keep[:, bass.ds(i, 1)], done[0])
        yield

    def rw_front_rest(self, i, unit):
        nc, act, dve, R = self.nc, self.act, self.dve, self.rw
        g2 = self.io["g2"][0]
        T = R.tile
        col = lambda name: self.cols(name, DT)[:, bass.ds(i, 1)]
        cols, raw = bass.ds(i * P, P), self.raw
        dve.wait(act.now())
        v_unit = self.rw_unit(i, IN_V)
        self.ts(dve, T["kk"], T["k"], col("k_k"), None, ALU.mult)
        e = self.tt(dve, T["t0"], T["kk"], T["kk"], ALU.mult)
        m = self.mm(self.bank[5][:], self.head_ones[:], T["t0"], True, True, e, self.free[5], mark=True)
        yield
        self.ts(dve, T["lw"], T["lw"], -float(2.718281828459045 ** -0.5), None, ALU.mult)
        dve.do(lambda: nc.vector.tensor_tensor_scan(T["sum"], R.restart[:], T["lw"], 0.0, ALU.mult, ALU.add))
        self.tt(dve, T["lw"], T["sum"], T["lw"], ALU.subtract)
        self.free[5] = self.ts(dve, T["t0"], self.bank[5][:], 1e-24, None, ALU.max, None, m)
        yield
        norm = self.sqrt_inverse(T["t0"])
        yield
        yield from self.rw_projected(i, IN_R, unit, 6, T["r"])
        self.ts(dve, T["e1"], T["rate"], col("k_a"), R.keep_a[:, bass.ds(i, 1)], ALU.mult, ALU.add)
        self.tt(dve, T["k"], T["k"], T["e1"], ALU.mult)
        e = self.tt(dve, T["kk"], T["kk"], T["t0"], ALU.mult, norm)
        self.fn(T["lw"], T["lw"], ACT.Exp, 0.0, 1.0, e)
        self.fn(T["e1"], T["sum"], ACT.Exp, 0.0, -1.0)
        self.fn(T["sum"], T["sum"], ACT.Exp, 0.0, 1.0)
        yield
        yield from self.rw_projected(i, IN_V, v_unit, 7, T["v"])
        slot, full = self.load((0, 0, None, g2[0:P, cols]), (P - 32, P, None, g2[P:GATE_LOW, cols]))
        self.mm(self.bank[5][:], raw[0:P, slot, 0:P], R.low_g[:, 0, :], True, False, full, self.free[5])
        ins = nc.tensor.matmul(self.bank[5][:], raw[P - 32:P, slot, P:2 * P], R.low_g[P - 32:P, 1, :],
                               start=False, stop=True, skip_group_check=True)
        self.free[5] = self.copy(act, T["gate_next"], self.bank[5][:], self.raw_free[slot].mark(ins))

    def rw_arrive(self, i):
        act, dve, R = self.act, self.dve, self.rw
        T, ar, bt, kt = R.tile, R.ar, R.bt, R.kt
        col = lambda name: self.cols(name, DT)[:, bass.ds(i, 1)]
        done = (act.now(), dve.now())
        tiles4 = lambda ap: ap.rearrange("p (j t) -> p j t", j=4)

        def turned(src, dst, bank, e, q):
            for j in range(4):
                t = self.transpose(self.bank[bank][:, j * P:(j + 1) * P], src[:, j * P:(j + 1) * P], e,
                                   self.free[bank], mark=j == 3)
            self.free[bank] = self.copy(q, dst[:].rearrange("p j t -> p (j t)"), self.bank[bank][:], t)

        e = self.tt(dve, kt[:], T["k"], T["e1"], ALU.mult, *done)
        turned(kt[:], R.k_tok, 0, e, act)
        self.tt(dve, T["t0"], T["kk"], T["rate"], ALU.mult, act.now())
        e = self.tt(dve, bt[:], T["t0"], T["e1"], ALU.mult)
        turned(bt[:], R.b_tok, 1, e, act)
        self.tt(dve, ar[:, :, 1, :], tiles4(T["r"]), tiles4(T["sum"]), ALU.mult)
        self.stt(ar[:, :, 0, :], tiles4(T["kk"]), -1.0, tiles4(T["lw"]), ALU.mult, ALU.mult)
        self.copy(dve, R.ends[:], T["sum"][:, CHUNK - 1::CHUNK])
        turned(T["v"], R.v_tok, 2, done[1], act)
        e = self.stt(T["t0"], T["r"], col("r_k"), T["k"], ALU.mult, ALU.mult)
        m = self.mm(self.bank[3][:], self.head_ones[:], T["t0"], True, True, e, self.free[3], mark=True)
        self.free[3] = self.tt(dve, tile_at(self.mixed, i), self.bank[3][:], T["v"], ALU.mult, m)

    def rw_first_half(self, close, front):
        self.pe.wait(self.act.now(), self.dve.now())

        def settle():
            yield from close
            self.copy(self.dve, self.rw.tile["gate"], self.rw.tile["gate_next"], self.act.now())

        interleave(self.rw_invert((0, 1), range(4)), woven(front, settle(), 1, 1), *PACE_INVERT)

    def rw_second_half(self, i, front):
        interleave(self.rw_invert((2, 3), range(5, 8)), self.rw_chain((0, 1)), *PACE_CHAIN)
        interleave(self.rw_chain((2, 3)), front, *PACE_REST)
        self.free[4] = self.copy(self.dve, self.rw.y, self.bank[4][:], self.y_done)

    def rw_invert(self, spans, banks):
        act, dve, R = self.act, self.dve, self.rw
        ar, bt, kt, keep, de, pw, pq, inv = R.ar, R.bt, R.kt, R.keep, R.de, R.pw, R.pq, R.inv
        bank, free = self.bank, self.free
        turn = 0

        def next_bank():
            nonlocal turn
            turn += 1
            return banks[turn % len(banks)]

        cells = [(hd, j) for j in spans for hd in range(2)]
        wait = [None] * 4
        for m, (hd, j) in enumerate(cells):
            rows = slice(HEAD * hd, HEAD * (hd + 1))
            b = next_bank()
            rhs = ar[rows, j, :, :].rearrange("p a t -> p (a t)")
            self.mm(bank[b][:, 0:2 * P], bt[rows, j * P:(j + 1) * P], rhs, True, False, free[b])
            t = self.mm(bank[b][:, 2 * P:], kt[rows, j * P:(j + 1) * P], rhs, False, True, mark=True)
            kp = keep[:, 4 * hd + j, :, :]
            free[b] = self.tt(dve, kp, bank[b][:].rearrange("p (a t) -> p a t", a=4), R.mask4[:], ALU.mult, t)
            b = next_bank()
            t = self.mm(bank[b][:, 0:P], ar[rows, j, 0, :], bt[rows, j * P:(j + 1) * P], True, True, free[b], mark=True)
            self.tt(dve, de[:, m, 0, :], bank[b][:, 0:P], R.mask2[:, 0, :], ALU.mult, t)
            free[b] = self.tt(dve, de[:, m, 1, :], bank[b][:, 0:P], R.mask2[:, 1, :], ALU.mult, serial=False)
            self.tt(dve, inv[:, m, 0, :], self.ident[:], de[:, m, 0, :], ALU.add)
            wait[m] = self.tt(dve, inv[:, m, 1, :], self.ident[:], kp[:, KEEP_T, :], ALU.add, serial=False)
            yield

        def step(products, evac):
            for m in range(4):
                b = next_bank()
                todo = products(m)
                for n, (l, rr) in enumerate(todo):
                    t = self.mm(bank[b][:, n * P:(n + 1) * P], l, rr, n == 0, n == len(todo) - 1,
                                free[b], wait[m], mark=n == len(todo) - 1)
                wait[m] = free[b] = evac(m, bank[b], t)
                if m % 2:
                    yield

        T_of = lambda m: keep[:, 4 * cells[m][0] + cells[m][1], KEEP_T, :]
        Dn, DTn, En = (lambda m: de[:, m, 0, :]), T_of, (lambda m: de[:, m, 1, :])
        pair = lambda t, m: t[:, m, :, :].rearrange("p a t -> p (a t)")

        def copy_to(t):
            return lambda m, bk, e: self.copy(act, pair(t, m), bk[:, 0:2 * P], e)

        def grow(out):
            def evac(m, bk, e):
                a = self.copy(act, pair(out, m), bk[:, 0:2 * P], e)
                return self.tt(dve, pair(inv, m), bk[:, 2 * P:4 * P], pair(inv, m), ALU.add, e, a)
            return evac

        def grow_last(m, bk, e):
            a = self.copy(act, pw[:, m, 1, :], bk[:, 0:P], e)
            return self.tt(dve, pair(inv, m), bk[:, P:3 * P], pair(inv, m), ALU.add, e, a)

        def add_inv(m, bk, e):
            return self.tt(dve, pair(inv, m), bk[:, 0:2 * P], pair(inv, m), ALU.add, e)

        def factors(m, bk, e):
            self.tt(dve, pq[:, m, 0, :], bk[:, 0:P], self.ident[:], ALU.add, e)
            return self.tt(dve, pq[:, m, 1, :], bk[:, P:2 * P], inv[:, m, 0, :], ALU.add, serial=False)

        yield from step(lambda m: [(DTn(m), Dn(m)), (Dn(m), DTn(m))], copy_to(pw))
        yield from step(lambda m: [(pw[:, m, 1, :], pw[:, m, 0, :]), (pw[:, m, 0, :], pw[:, m, 1, :]),
                                   (pw[:, m, 1, :], inv[:, m, 0, :]), (inv[:, m, 0, :], pw[:, m, 1, :])], grow(pq))
        yield from step(lambda m: [(pq[:, m, 0, :], pq[:, m, 1, :]),
                                   (pq[:, m, 1, :], inv[:, m, 0, :]), (inv[:, m, 0, :], pq[:, m, 1, :])], grow_last)
        yield from step(lambda m: [(pw[:, m, 1, :], inv[:, m, 0, :]), (inv[:, m, 0, :], pw[:, m, 1, :])], add_inv)
        yield from step(lambda m: [(inv[:, m, 1, :], En(m)), (En(m), inv[:, m, 1, :])], copy_to(pw))
        yield from step(lambda m: [(pw[:, m, 0, :], pw[:, m, 1, :]), (pw[:, m, 1, :], inv[:, m, 0, :])], factors)
        yield from step(lambda m: [(pq[:, m, 1, :], pq[:, m, 0, :])],
                        lambda m, bk, e: self.copy(act, T_of(m), bk[:, 0:P], e))

    def rw_chain(self, spans):
        nc, act, dve, R = self.nc, self.act, self.dve, self.rw
        keep, ar = R.keep, R.ar
        bank, free = self.bank, self.free
        X, U, Y = bank[0], bank[1], bank[4]
        state, x_tok, u_tok = R.state, R.x_tok, R.u_tok
        heads = [slice(HEAD * hd, HEAD * (hd + 1)) for hd in range(2)]
        if spans[0] == 0:
            self.s_ready = dve.do(lambda: nc.vector.memset(state[:, 0, :], 0.0))
            self.pe.wait(free[4])
        self.pe.wait(act.now(), dve.now())
        for j in spans:
            for hd, cs in enumerate(heads):
                self.mm(X[:, cs], keep[:, 4 * hd + j, KEEP_AK, :], R.v_tok[:, j, cs], hd == 0, False, free[0])
            for ch in range(2):
                c = 2 * j + ch
                old, new = state[:, c % 2, :], state[:, (c + 1) % 2, :]
                half = slice(CHUNK * ch, CHUNK * (ch + 1))
                t = self.mm(X[half, 0:P], ar[:, j, 0, half], old, False, ch == 1, self.s_ready, mark=True)
                free[0] = e = self.copy(dve, x_tok[half, :], X[half, 0:P], t)
                self.mm(Y[:, c * CHUNK:(c + 1) * CHUNK], old, ar[:, j, 1, half], c == 0, False)
                sb_ = bank[2 + c % 2]
                self.mm(sb_[:, 0:P], self.ident[:], old, True, False, free[2 + c % 2])
                self.mm(sb_[:, 0:P], R.k_tok[half, j, :], R.v_tok[half, j, :], False, False)
                yield
                for hd, cs in enumerate(heads):
                    t = self.mm(U[:, cs], keep[half, 4 * hd + j, KEEP_T, :], x_tok[half, cs],
                                ch == 0 and hd == 0, ch == 1 and hd == 1, e, free[1], mark=hd == 1)
                free[1] = e = self.copy(act, u_tok[half, :], U[half, 0:P], t)
                yield
                t = self.mm(sb_[:, 0:P], R.b_tok[half, j, :], u_tok[half, :], False, True, e, mark=True)
                if c < S // CHUNK - 1:
                    if c == 0:
                        dve.do(lambda: nc.vector.memset(new, 0.0))
                    self.ts(dve, new[heads[0], heads[0]], sb_[heads[0], heads[0]], R.ends[heads[0], c:c + 1], None, ALU.mult, None, t)
                    self.s_ready = self.ts(dve, new[heads[1], heads[1]], sb_[heads[1], heads[1]],
                                           R.ends[heads[1], c:c + 1], None, ALU.mult, serial=False)
                    free[2 + c % 2] = self.s_ready
                yield
            for hd, cs in enumerate(heads):
                out = Y[cs, j * P:(j + 1) * P]
                self.mm(out, u_tok[:, cs], keep[:, 4 * hd + j, KEEP_RB, :], False, False)
                self.y_done = self.mm(out, R.v_tok[:, j, cs], keep[:, 4 * hd + j, KEEP_RK, :], False, True, mark=True)

    def rw_close(self, i):
        nc, act, dve, R = self.nc, self.act, self.dve, self.rw
        bank, free, T = self.bank, self.free, R.tile
        col = lambda name: self.cols(name, DT)[:, bass.ds(i, 1)]
        y, y2 = R.y, R.y2
        m = self.mm(bank[4][:], self.head_ones[:], y, True, True, dve.now(), free[4], mark=True)
        yield
        free[4] = self.stt(y, bank[4][:], -1.0 / HEAD, y, ALU.mult, ALU.add, m)
        e = self.tt(dve, y2, y, y, ALU.mult)
        m = self.mm(bank[4][:], self.head_ones[:], y2, True, True, e, free[4], mark=True)
        yield
        free[4] = self.ts(dve, y2, bank[4][:], 1.0 / HEAD, GN_EPS, ALU.mult, ALU.add, m)
        e = self.sqrt_inverse(y2)
        yield
        self.tt(dve, y, y, y2, ALU.mult, e)
        self.ts(dve, y, y, col("lnx_w"), col("lnx_b"), ALU.mult, ALU.add)
        self.tt(dve, y, y, tile_at(self.mixed, i), ALU.add)
        self.tt(dve, tile_at(self.mixed, i), y, T["gate"], ALU.mult)

    def merge(self):
        act, dve, io = self.act, self.dve, self.io
        w = io["w_in"][0].rearrange("(k p) n -> p k n", p=P)
        wa = io["w_att_out"][0].rearrange("(k p) n -> p k n", p=P)
        wr = io["w_rwkv_out"][0].rearrange("(k p) n -> p k n", p=P)
        bg = self.cols("b_gate", 2 * DT)
        with ExitStack() as ctx:
            sb = lambda name, shape, dtype=F32: self.sb(name, shape, dtype, ctx)
            a_high, a_low = sb("mg_a_high", [P, 4, S], F32R), sb("mg_a_low", [P, 4, S], F32R)
            r_high, r_low = sb("mg_r_high", [P, DT, S], F32R), sb("mg_r_low", [P, DT, S], F32R)
            both = sb("mg_both", [P, DT, S])
            gate = sb("mg_gate", [P, 2, S])
            bias = sb("mg_bias", [P, 2, 2])
            todo = [(a_high[:, k, :], a_low[:, k, :], self.att[:, k, :]) for k in range(4)]
            todo += [(r_high[:, k, :], r_low[:, k, :], self.mixed[:, k, :]) for k in range(DT)]
            for n, (high, low, src) in enumerate(todo):
                e = self.copy(act, high, src)
                self.tt(self.pool if n % 3 == 2 else dve, low, src, high.bitcast(F32), ALU.subtract, e)
            splits = (dve.now(), self.pool.now())
            part = lambda t: lambda k: t[:, k, :]

            def sources(i):
                return [t for u in range(2) for t in (
                    (w[:, :, bass.ds((2 * i + u) * P + GATE0, P)], DT), (w[:, :, bass.ds((2 * i + u) * P + (GATE0 + D), P)], DT),
                    (wa[:, :, bass.ds((2 * i + u) * P, P)], 4), (wr[:, :, bass.ds((2 * i + u) * P, P)], DT))]

            parts = (self.h_parts(), self.h_parts(), (part(a_high), part(a_low)), (part(r_high), part(r_low)))

            def step(i, before, name, take):
                for u in range(2):
                    b = self.bank[4 * u:4 * u + 4]
                    ts = []
                    for j in range(2):
                        self.copy(dve, bias[:, u, j:j + 1], bg[:, bass.ds(2 * i + (u + j * DT), 1)], act.now())
                    biases = dve.now()
                    for j in range(4):
                        ts.append(self.product(b[j][:], take(), *parts[j], True, True, before(f"evac{u}"),
                                               needs=lambda k: splits if j > 1 else ()))
                        if j == 1:
                            for jj in range(2):
                                self.fn(gate[:, jj, :], b[jj][:], ACT.Sigmoid, bias[:, u, jj:jj + 1], 1.0, ts[jj], biases)
                            gates = act.now()
                    for j in range(2):
                        self.tt(dve, gate[:, j, :], gate[:, j, :], b[2 + j][:], ALU.mult, ts[2 + j], gates)
                    e = self.tt(dve, tile_at(both, 2 * i + u), gate[:, 0, :], gate[:, 1, :], ALU.add)
                    name(f"evac{u}", e)
                    self.act.wait(e)

            wo = io["w_o"][0].rearrange("(k p) n -> p k n", p=P)
            self.each(DT // 2, sources, step, (wo[:, :, 0:P], DT))
            self.together()
            ready = [self.split(self.h_high[:, k, :], self.h_low[:, k, :], both[:, k, :]) for k in range(DT)]
            self.project(io["w_o"][0], self.h_high, self.h_low, DT, 2, self.first(io["w_up"][0]), ready=ready)

    def project(self, weight, high, low, tiles, scale=None, then=None, last_tiles=DT, ready=None):
        early, late = self.before_last, self.dve.now()
        needs = lambda k: (ready[k],) if ready else (late,) if k >= tiles - last_tiles else (early,)
        square = self.sq[:, 0, :]
        self.dve.do(lambda: self.nc.vector.memset(self.rinv[:], 0.0))
        w = weight.rearrange("(k p) n -> p k n", p=P)
        parts = [(k0, min(UNIT_K, tiles - k0)) for k0 in range(0, tiles, UNIT_K)]
        outputs = 4 // len(parts)
        todo = [(u, k0, n) for u in range(outputs) for k0, n in parts]

        def step(i, before, name, take):
            for u, k0, n in todo:
                last = k0 + n == tiles
                t = self.product(self.bank[u][:], take(), lambda k: high[:, k0 + k, :], lambda k: low[:, k0 + k, :],
                                 k0 == 0, last, before(f"evac{u}"), needs=lambda k: needs(k0 + k))
                if last:
                    x = tile_at(self.x, outputs * i + u)
                    if scale is None:
                        e = self.tt(self.dve, x, self.bank[u][:], x, ALU.add, t)
                    else:
                        gt = self.mod[:, scale * DT:(scale + 1) * DT][:, bass.ds(outputs * i + u, 1)]
                        e = self.stt(x, self.bank[u][:], gt, x, ALU.mult, ALU.add, t)
                    name(f"evac{u}", e)
                    self.tt(self.dve, square, x, x, ALU.mult)
                    self.tt(self.dve, self.rinv[:], self.rinv[:], square, ALU.add)

        self.each(DT // outputs, lambda i: [(w[:, k0:k0 + n, bass.ds((outputs * i + u) * P, P)], n) for u, k0, n in todo],
                  step, then)
        self.together()

    def prefer(self, func):
        self.fn(self.spare[:], self.ones[:, 0:1], func)

    def ffn(self, name, w_gate, w_up, taps, biases, both, w_down, scale=None, then=None):
        dve, act = self.dve, self.act
        wg = w_gate.rearrange("(k p) n -> p k n", p=P)
        wu = w_up.rearrange("(k p) n -> p k n", p=P)
        with ExitStack() as ctx:
            high = self.sb(f"{name}_high", [P, FT, S], F32R, ctx)
            low = self.sb(f"{name}_low", [P, FT, S], F32R, ctx)
            c = self.sb(f"{name}_c", [P, 2, 2, S], F32, ctx)
            self.prefer(ACT.Silu)

            todo = [(u, j) for u in range(2) for j in range(2)]

            def step(i, before, name, take):
                for u, j in todo:
                    n, bank, out = 2 * i + u, self.bank[2 * u + j], c[:, u, j, :]
                    unit = take()
                    if j == 1:
                        gate = c[:, u, 0, :]
                        s = self.fn(gate, gate, ACT.Silu, 0.0, 1.0, e)
                    t = self.product(bank[:], unit, *self.h_parts(), True, True, before(f"evac{u}{j}"), needs=self.h_need)
                    if j == 0 or both:
                        tap = [taps(j, a)[:, bass.ds(n, 1)] for a in range(3)]
                        self.ts(dve, out, bank[:], tap[2], biases(j)[:, bass.ds(n, 1)], ALU.mult, ALU.add, t)
                        self.stt(out[:, 1:S], bank[:, 0:S - 1], tap[1], out[:, 1:S], ALU.mult, ALU.add)
                        e = self.stt(out[:, 2:S], bank[:, 0:S - 2], tap[0], out[:, 2:S], ALU.mult, ALU.add)
                        name(f"evac{u}{j}", e)
                    if j == 1:
                        e = self.tt(dve, gate, gate, out if both else bank[:], ALU.mult, s, t)
                        if not both:
                            name(f"evac{u}1", e)
                        self.split(tile_at(high, n), tile_at(low, n), gate)

            down = w_down.rearrange("(k p) n -> p k n", p=P)
            self.each(FT // 2, lambda i: [((wg, wu)[j][:, :, bass.ds((2 * i + u) * P, P)], DT) for u, j in todo],
                      step, (down[:, 0:UNIT_K, 0:P], UNIT_K))
            self.project(w_down, high, low, FT, scale, then, 2)

    def even_layer(self):
        io, dve, act, pool = self.io, self.dve, self.act, self.pool
        w = io["w_in_even_2"][0].rearrange("(k p) n -> p k n", p=P)
        W4 = 4 * P
        with ExitStack() as ctx:
            sb = lambda n, shape, dt=F32: self.sb(f"ev_{n}", shape, dt, ctx)
            high, low = sb("high", [P, DT, S], F32R), sb("low", [P, DT, S], F32R)
            z = sb("z", [P, 2, S])
            c = sb("c", [P, 2, S])
            zp = sb("zp", [P, S])
            s1, s2 = sb("s1", [P, S]), sb("s2", [P, S])
            pos, posf = sb("pos", [P, S], I32), sb("posf", [P, S])
            cnt = sb("cnt", [P, 4, S])
            GATE_B, GATE_C, VALUE = range(3)
            todo = [(u, j) for u in range(2) for j in (GATE_C, VALUE, GATE_B)]

            def step(i, before, name, take):
                for u, j in todo:
                    n, bank = 2 * i + u, self.bank[3 * u + j]
                    t = self.product(bank[:], take(), *self.h_parts(), True, True, before(f"evac{u}"), needs=self.h_need)
                    if j == GATE_C:
                        e = self.copy(act, c[:, u, :], bank[:], t, before(f"evac{u}"))
                    elif j == VALUE:
                        tap = [self.cols("conv_a_2", 4, 4 * a)[:, bass.ds(n, 1)] for a in range(3)]
                        zu, cu = z[:, u, :], c[:, u, :]
                        self.tt(dve, zu, bank[:], cu, ALU.mult, t, e)
                        self.ts(dve, cu, zu, tap[2], None, ALU.mult)
                        self.stt(cu[:, 1:S], zu[:, 0:S - 1], tap[1], cu[:, 1:S], ALU.mult, ALU.add)
                        self.stt(cu[:, 2:S], zu[:, 0:S - 2], tap[0], cu[:, 2:S], ALU.mult, ALU.add)
                    else:
                        e = self.tt(dve, z[:, u, :], c[:, u, :], bank[:], ALU.mult, t)
                        name(f"evac{u}", e)
                        self.split(tile_at(high, n), tile_at(low, n), z[:, u, :])

            self.each(2, lambda i: [(w[:, :, bass.ds((2 * i + u) * P + j * W4, P)], DT) for u, j in todo],
                      step, (w[:, :, 3 * W4:3 * W4 + P], DT))
            pool.do(lambda: self.nc.gpsimd.iota(pos[:], pattern=[[1, S]], base=1, channel_multiplier=0))
            e = self.copy(pool, posf[:], pos[:])
            for g, window in enumerate(POOL_WINDOWS):
                self.ts(dve, cnt[:, g, :], posf[:], float(window), None, ALU.min, None, e)
                dve.do(lambda: self.nc.vector.reciprocal(cnt[:, g, 0:window], cnt[:, g, 0:window]))
                dve.do(lambda: self.nc.vector.memset(cnt[:, g, window:S], 1.0 / window))
            units, self.carried = [self.carried], None
            slot_pool = None
            for g, window in enumerate(POOL_WINDOWS):
                if g < 3:
                    units.append(self.unit(w[:, :, 3 * W4 + (g + 1) * P:3 * W4 + (g + 2) * P], DT))
                else:
                    self.carried = self.unit(*self.first(io["w_out_even_2"][0]))
                slot, full = self.load((0, 0, None, io["w_pool_2"][0, g]))
                t = self.product(self.bank[6][:], units[g], *self.h_parts(), True, True, self.free[6])
                self.free[6] = self.copy(dve, zp[:], self.bank[6][:], t)
                src, spare, width = zp[:], [s1[:], s2[:]], 1
                while width < window:
                    dst = spare[0]
                    self.copy(dve, dst[:, 0:width], src[:, 0:width])
                    self.tt(dve, dst[:, width:], src[:, width:], src[:, 0:S - width], ALU.add)
                    src, spare, width = dst, spare[::-1], 2 * width
                self.tt(dve, src, src, cnt[:, g, :], ALU.mult)
                e = self.tt(dve, zp[:], src, zp[:], ALU.subtract)
                self.pe.wait(e, full, self.free[7])
                t = self.raw_free[slot].mark(self.nc.tensor.matmul(self.bank[7][:], self.raw[:, slot, 0:P], zp[:],
                                                                   start=True, stop=True, skip_group_check=True))
                self.free[7] = self.ts(dve, s1[:], self.bank[7][:], self.col("pool_scale_2", g), None, ALU.mult, None, t)
                self.split(high[:, 4 + g, :], low[:, 4 + g, :], s1[:])
            self.together()
            self.project(io["w_out_even_2"][0], high, low, DT, None, self.first(io["w_ffn_gate_2"][0]))

    def odd_layer(self):
        io, dve, act = self.io, self.dve, self.act
        w = io["w_in_odd_2"][0].rearrange("(k p) n -> p k n", p=P)
        with ExitStack() as ctx:
            sb = lambda n, shape, dt=F32: self.sb(f"od_{n}", shape, dt, ctx)
            high, low = sb("high", [P, DT, S], F32R), sb("low", [P, DT, S], F32R)
            uv = sb("uv", [P, 2 * DT, S])
            vn, v_tok = sb("vn", [P, 2, S]), sb("v_tok", [P, 2, S])
            ws, wst = sb("ws", [P, 2, P]), sb("wst", [P, 2, P])
            ws_all, bias = sb("ws_all", [P, DT, P]), sb("bias", [P, DT, P])
            tril = sb("tril", [P, P])
            self.fill_with(tril[:], 1.0)
            self.band(tril[:], ALU.is_ge, 0, [[-1, P]], 1, 0.0)
            self.sp.wait(self.norm_begun)
            self.load_done.mark(self.nc.sync.dma_start(ws_all[:], io["w_spatial_2"][0].rearrange("h t s -> t h s")))
            full = self.load_done.mark(self.nc.sync.dma_start(bias[:], io["b_spatial_2"][0].partition_broadcast(P)))

            def step(i, before, name, take):
                for n in range(4):
                    t = self.product(self.bank[n][:], take(), *self.h_parts(), True, True, before(f"evac{n}"), needs=self.h_need)
                    e = self.fn(tile_at(uv, 4 * i + n), self.bank[n][:], ACT.Gelu, 0.0, 1.0, t)
                    name(f"evac{n}", e)

            self.prefer(ACT.Gelu)
            out = io["w_out_odd_2"][0].rearrange("(k p) n -> p k n", p=P)
            self.each(4, lambda i: [(w[:, :, bass.ds((4 * i + n) * P, P)], DT) for n in range(4)],
                      step, (out[:, :, 0:P], DT))
            self.together()
            dve.wait(self.inverse_rms(uv[:, DT:2 * DT, :], RMS_EPS), full)

            def head(i, loop):
                before = lambda key: loop.before(self.book.counts, key)
                both = [(u, 2 * i + u) for u in range(2)]
                e, t, normed = [None] * 2, [None] * 2, [None] * 2
                for u, n in both:
                    e[u] = self.tt(dve, ws[:, u, :], tile_at(ws_all, n), tril[:], ALU.mult, before(f"ws{u}"))
                for u, n in both:
                    t[u] = self.transpose(self.bank[u][:, 0:P], ws[:, u, :], e[u], before(f"w{u}"), mark=True)
                    loop.name(f"ws{u}", t[u])
                for u, n in both:
                    normed[u] = self.stt(vn[:, u, :], tile_at(uv, n + DT), self.cols("sgu_norm_2", DT)[:, bass.ds(n, 1)],
                                         self.rinv[:], ALU.mult, ALU.mult)
                for u, n in both:
                    loop.name(f"w{u}", self.copy(dve, wst[:, u, :], self.bank[u][:, 0:P], t[u]))
                for u, n in both:
                    for q in range(4):
                        t[u] = self.transpose(self.bank[2 + u][:, q * P:(q + 1) * P], vn[:, u, q * P:(q + 1) * P], normed[u],
                                              before(f"v{u}"), mark=q == 3)
                for u, n in both:
                    e[u] = self.copy(act, v_tok[:, u, :], self.bank[2 + u][:], t[u], before(f"g{u}"))
                    loop.name(f"v{u}", e[u])
                copied = self.dve.now()
                for u, n in both:
                    for q in range(4):
                        t[u] = self.mm(self.bank[4 + u][:, q * P:(q + 1) * P], v_tok[:, u, q * P:(q + 1) * P], wst[:, u, :],
                                       q == 0, q == 3, e[u], copied, before(f"o{u}"), mark=q == 3)
                    loop.name(f"g{u}", t[u])
                for u, n in both:
                    b4 = bias[:, bass.ds(n, 1), :].to_broadcast([P, 4, P])
                    loop.name(f"o{u}", self.tt(dve, vn[:, u, :].rearrange("p (q t) -> p q t", q=4),
                                               self.bank[4 + u][:].rearrange("p (q t) -> p q t", q=4), b4, ALU.add, t[u]))
                    self.tt(dve, vn[:, u, :], tile_at(uv, n), vn[:, u, :], ALU.mult)
                    self.split(tile_at(high, n), tile_at(low, n), vn[:, u, :])

            self.book.run(4, head)
            self.together()
            self.project(io["w_out_odd_2"][0], high, low, DT, None, self.first(io["w_ffn_gate_2"][1]))

    def store(self):
        with ExitStack() as ctx:
            out = self.sb("out_rows", [P, 4, D], F32, ctx)
            rows = self.io["out"][0].rearrange("(t p) d -> p t d", p=P)
            for t in range(4):
                for half in range(2):
                    b = 2 * (t % 2) + half
                    for f in range(4):
                        m = self.transpose(self.bank[b][:, f * P:(f + 1) * P], self.x[:, 4 * half + f, t * P:(t + 1) * P],
                                           self.dve.now(), self.free[b], mark=f == 3)
                    self.free[b] = self.copy(self.act, out[:, t, half * S:(half + 1) * S], self.bank[b][:], m)
                self.sp.wait(self.free[b])
                done = self.store_done.mark(self.nc.sync.dma_start(rows[:, t, :], out[:, t, :]))
            self.sp.wait(done)

    def gated_ffn(self, layer):
        io, tail = self.io, "b" if layer else ""
        self.ffn(f"g{layer}", io["w_ffn_gate_2"][layer], io["w_ffn_up_2"][layer],
                 lambda j, a: self.cols("conv_ffn_2" + tail, FT, FT * a), lambda j: self.cols("b_conv_ffn_2" + tail, FT),
                 False, io["w_ffn_down_2"][layer], None, None if layer else self.first(io["w_in_odd_2"][0]))

    def build(self):
        io = self.io
        self.x = self.sb("x_res", [P, DT, S])
        self.h_high, self.h_low = self.sb("h_high", [P, DT, S], F32R), self.sb("h_low", [P, DT, S], F32R)
        self.raw = self.sb("w_raw", [P, RAW_SLOTS, UNIT_K * P])
        self.w_high = self.sb("w_high", [P, SPLIT_SLOTS, UNIT_K * P], F32R)
        self.w_low = self.sb("w_low", [P, SPLIT_SLOTS, UNIT_K * P], F32R)
        self.rinv = self.sb("rinv", [P, S])
        self.sq = self.sb("sq", [P, 2, S])
        self.mod = self.sb("mod", [P, 6 * DT])
        self.gain1, self.gain2 = self.sb("gain1", [P, DT]), self.sb("gain2", [P, DT])
        self.ident = self.sb("ident", [P, P])
        self.ident_bf = self.sb("ident_bf", [P, P], BF16)
        self.ones = self.sb("ones", [P, P])
        self.head_ones = self.sb("head_ones", [P, P])
        self.vec = self.sb("vec", [P, VEC_GROUPS * P])
        self.spare = self.sb("spare", [P, 1])
        self.load_x_done = Count(self.book, "load_x_done", 16)
        with ExitStack() as scope:
            xrow, full = self.load_x(scope)
            self.constants()
            self.vectors(scope)
            self.turn_x(xrow, full)
        mod, col = self.mod, self.col
        self.together()

        def mixers():
            with ExitStack() as ctx:
                self.att = self.sb("att", [P, 4, S], F32, ctx)
                self.mixed = self.sb("mixed", [P, DT, S], F32, ctx)
                self.rwkv_constants(ctx)
                self.attention()
                self.rwkv()
                self.merge()

        first = self.first

        def first_ffn():
            self.norm(self.x, lambda k: self.gain2[:, k:k + 1], lambda k: mod[:, 3 * DT + k:3 * DT + k + 1])
            self.ffn("f", io["w_up"][0][:, 0:F], io["w_up"][0][:, F:2 * F],
                     lambda j, a: self.cols(f"conv_w{a}", FT, FT * j), lambda j: self.cols("conv_b", FT, FT * j),
                     True, io["w_down"][0], 5, first(io["w_in_even_2"][0], 4 * P))

        def first_layer():
            ready = self.norm(self.x, lambda k: col("norm_f_w", k), keep=True)
            self.norm(self.x, lambda k: col("norm_mix_2", k), summed=False, ready=ready)
            self.even_layer()

        def layer_ffn(layer):
            self.norm(self.x, lambda k: col("norm_ffn_2", layer * DT + k))
            self.gated_ffn(layer)

        def second_layer():
            self.norm(self.x, lambda k: col("norm_mix_2", DT + k))
            self.odd_layer()

        mixers()
        first_ffn()
        first_layer()
        layer_ffn(0)
        second_layer()
        layer_ffn(1)
        self.together()
        self.norm(self.x, lambda k: col("final_norm_2", k), keep=True)
        self.together()
        self.store()
        return self.book.learned


def build_program(make, io_of):
    known = None
    for _ in range(2):
        nc = make()
        with ExitStack() as ctx:
            known = Kernel(nc, ctx, io_of(nc), known).build()
    return nc


_OUT = ((1, S, D), "float32")


def kernel(**inputs):
    import numpy as np
    import concourse.bacc as bacc
    from concourse.bass_utils import run_bass_kernel_spmd

    arrays = {f"in_{n}": np.ascontiguousarray(a) for n, a in inputs.items()}

    def io_of(nc):
        io = {n: nc.dram_tensor(f"in_{n}", a.shape, mybir.dt.from_np(np.asarray(a).dtype), kind="ExternalInput").ap()
              for n, a in inputs.items()}
        io["out"] = nc.dram_tensor("out_0", _OUT[0], F32, kind="ExternalOutput").ap()
        return io

    nc = build_program(lambda: bacc.Bacc("TRN2", target_bir_lowering=False, num_devices=1), io_of)
    r = run_bass_kernel_spmd(nc, [arrays], core_ids=[0])
    return r.results[0]["out_0"]
```
